# Optimizing a Trainium2 kernel written in Bass

```python
import math
import jax
import jax.numpy as jnp
from jax import lax
import numpy as np

D_MODEL = 1024
BATCH = 1
SEQ = 1024
DEPTH = 2

CTX_LEN = 256
GRID_W = 64
ROPE_BASE = 10000.0
Q_BLOCK = 128
RMS_EPS = 1e-6
LN_EPS = 1e-5

A_WIDTH = 512
A_KERNEL = 31
B_HEADS = 4
B_HEAD_DIM = 64
B_V_DIM = 2 * B_HEAD_DIM
B_QK_COLS = B_HEADS * 2 * B_HEAD_DIM
B_WIDTH = B_HEADS * B_V_DIM
AB_IN = 2 * A_WIDTH + 2 * B_QK_COLS + B_WIDTH
AB_OUT = A_WIDTH + B_WIDTH
C_HEADS = 16
C_NOPE = 64
C_ROPE = 32
C_V = 64
C_Q_RANK = 768
C_KV_RANK = 256
C_IN = C_Q_RANK + C_KV_RANK + C_ROPE
FFN_HIDDEN = 2816
FFN_KERNEL = 3

N_EVEN = (DEPTH + 1) // 2
N_ODD = DEPTH // 2

kernel_name = 'hybrid_conv_diffattn_mla_dit_trunk'

def rms_norm(x, g):
    xf = x.astype(jnp.float32)
    y = xf * lax.rsqrt(jnp.mean(xf * xf, axis=-1, keepdims=True) + RMS_EPS)
    return (y * g.astype(jnp.float32)).astype(x.dtype)

def layer_norm(x, g, b):
    xf = x.astype(jnp.float32)
    mu = jnp.mean(xf, axis=-1, keepdims=True)
    var = jnp.mean(jnp.square(xf - mu), axis=-1, keepdims=True)
    y = (xf - mu) * lax.rsqrt(var + LN_EPS)
    return (y * g.astype(jnp.float32) + b.astype(jnp.float32)).astype(x.dtype)

def modulate(h, shift, scale):
    return h * (1 + scale) + shift

def rope_1d(x, pos):
    half = x.shape[-1] // 2
    inv_freq = ROPE_BASE ** (-jnp.arange(half, dtype=jnp.float32) / half)
    ang = pos.astype(jnp.float32)[:, None] * inv_freq[None, :]
    cos = jnp.cos(ang).astype(x.dtype)
    sin = jnp.sin(ang).astype(x.dtype)
    x1, x2 = x[..., :half], x[..., half:]
    return jnp.concatenate([x1 * cos - x2 * sin, x1 * sin + x2 * cos], axis=-1)

def rope_2d(x):
    n_tokens = x.shape[-2]
    rows_count = n_tokens // GRID_W
    rows = jnp.repeat(jnp.arange(rows_count, dtype=jnp.int32), GRID_W)
    cols = jnp.tile(jnp.arange(GRID_W, dtype=jnp.int32), rows_count)
    r = x.shape[-1] // 2
    return jnp.concatenate([rope_1d(x[..., :r], rows), rope_1d(x[..., r:], cols)], axis=-1)

def depthwise_conv(x, w, b):
    y = lax.conv_general_dilated(x, w[:, None, :].astype(x.dtype), window_strides=(1,), padding='SAME',
                                 dimension_numbers=('NWC', 'WIO', 'NWC'), feature_group_count=x.shape[-1])
    return y + b.astype(x.dtype)

def sweep_query_blocks(fn, *qs):
    bsz, heads, s = qs[0].shape[:3]
    nblk = s // Q_BLOCK
    blocks = tuple(q.reshape(bsz, heads, nblk, Q_BLOCK, q.shape[-1]).transpose(2, 0, 1, 3, 4) for q in qs)
    out = lax.map(lambda blk: fn(*blk), blocks)
    return out.transpose(1, 2, 0, 3, 4).reshape(bsz, heads, s, out.shape[-1])

def diff_attn_block(q1, q2, k1, k2, v, lam):
    scale = B_HEAD_DIM ** -0.5
    s1 = jnp.einsum('bhqd,bhkd->bhqk', q1, k1).astype(jnp.float32) * scale
    s2 = jnp.einsum('bhqd,bhkd->bhqk', q2, k2).astype(jnp.float32) * scale
    p = jax.nn.softmax(s1, axis=-1) - lam * jax.nn.softmax(s2, axis=-1)
    return jnp.einsum('bhqk,bhkd->bhqd', p.astype(v.dtype), v)

def mla_block(q_nope, q_pe, k_nope, k_pe, v):
    scale = (C_NOPE + C_ROPE) ** -0.5
    s = (jnp.einsum('bhqd,bhkd->bhqk', q_nope, k_nope)
         + jnp.einsum('bhqr,bkr->bhqk', q_pe, k_pe)).astype(jnp.float32) * scale
    p = jax.nn.softmax(s, axis=-1)
    return jnp.einsum('bhqk,bhkd->bhqd', p.astype(v.dtype), v)

def conv_ffn(h, w_up, conv_w, conv_b, w_down):
    u = h @ w_up
    val, gate = u[..., :FFN_HIDDEN], u[..., FFN_HIDDEN:]
    gate = depthwise_conv(gate, conv_w, conv_b)
    return (jax.nn.silu(gate) * val) @ w_down

def mixer_conv_diff(hx, hc, w_in, conv_w, conv_b, ln_g, ln_b, lam_vecs, subln_g, w_out, lambda_init, with_ctx):
    lv = lam_vecs.astype(jnp.float32)
    lam = jnp.exp(jnp.sum(lv[0] * lv[1])) - jnp.exp(jnp.sum(lv[2] * lv[3])) + lambda_init

    def split(h):
        bsz, t = h.shape[:2]
        p = h @ w_in
        a = p[..., :2 * A_WIDTH]
        o = 2 * A_WIDTH
        q = p[..., o:o + B_QK_COLS].reshape(bsz, t, B_HEADS, 2, B_HEAD_DIM).transpose(3, 0, 2, 1, 4)
        k = p[..., o + B_QK_COLS:o + 2 * B_QK_COLS].reshape(bsz, t, B_HEADS, 2, B_HEAD_DIM).transpose(3, 0, 2, 1, 4)
        v = p[..., o + 2 * B_QK_COLS:].reshape(bsz, t, B_HEADS, B_V_DIM).transpose(0, 2, 1, 3)
        return a, q, k, v

    def conv_module(a):
        u = a[..., :A_WIDTH] * jax.nn.sigmoid(a[..., A_WIDTH:])
        u = depthwise_conv(u, conv_w, conv_b)
        return jax.nn.silu(layer_norm(u, ln_g, ln_b))

    def merge(ya, ob):
        bsz, _, t, _ = ob.shape
        yb = (rms_norm(ob, subln_g) * (1 - lambda_init)).transpose(0, 2, 1, 3).reshape(bsz, t, B_WIDTH)
        return jnp.concatenate([ya, yb], axis=-1) @ w_out

    ax, qx, kx, vx = split(hx)
    ac, qc, kc, vc = split(hc)
    qx = rope_2d(qx)
    kx = rope_2d(kx)
    k1 = jnp.concatenate([kc[0], kx[0]], axis=2)
    k2 = jnp.concatenate([kc[1], kx[1]], axis=2)
    v_all = jnp.concatenate([vc, vx], axis=2)
    ob_x = sweep_query_blocks(lambda q1, q2: diff_attn_block(q1, q2, k1, k2, v_all, lam), qx[0], qx[1])
    yx = merge(conv_module(ax), ob_x)
    if not with_ctx:
        return yx, None
    ob_c = diff_attn_block(qc[0], qc[1], kc[0], kc[1], vc, lam)
    yc = merge(conv_module(ac), ob_c)
    return yx, yc

def mixer_mla(hx, hc, w_in, q_norm_g, kv_norm_g, w_uq, w_ukv, w_out, with_ctx):
    def project(h, rotate):
        bsz, t = h.shape[:2]
        p = h @ w_in
        cq = rms_norm(p[..., :C_Q_RANK], q_norm_g)
        ckv = rms_norm(p[..., C_Q_RANK:C_Q_RANK + C_KV_RANK], kv_norm_g)
        k_pe = p[..., C_Q_RANK + C_KV_RANK:]
        q = (cq @ w_uq).reshape(bsz, t, C_HEADS, C_NOPE + C_ROPE).transpose(0, 2, 1, 3)
        kv = (ckv @ w_ukv).reshape(bsz, t, C_HEADS, C_NOPE + C_V).transpose(0, 2, 1, 3)
        q_nope, q_pe = q[..., :C_NOPE], q[..., C_NOPE:]
        k_nope, v = kv[..., :C_NOPE], kv[..., C_NOPE:]
        if rotate:
            q_pe = rope_2d(q_pe)
            k_pe = rope_2d(k_pe)
        return q_nope, q_pe, k_nope, k_pe, v

    def out_proj(o):
        bsz, _, t, _ = o.shape
        return o.transpose(0, 2, 1, 3).reshape(bsz, t, C_HEADS * C_V) @ w_out

    qnx, qpx, knx, kpx, vx = project(hx, True)
    qnc, qpc, knc, kpc, vc = project(hc, False)
    kn_all = jnp.concatenate([knc, knx], axis=2)
    kp_all = jnp.concatenate([kpc, kpx], axis=1)
    v_all = jnp.concatenate([vc, vx], axis=2)
    ox = sweep_query_blocks(lambda qn, qp: mla_block(qn, qp, kn_all, kp_all, v_all), qnx, qpx)
    yx = out_proj(ox)
    if not with_ctx:
        return yx, None
    oc = mla_block(qnc, qpc, knc, kpc, vc)
    return yx, out_proj(oc)

def setup_inputs(seed: int = 0) -> dict:
    key = jax.random.key(seed)
    ks = iter(jax.random.split(key, 40))

    def nrm(shape, scale):
        return jax.random.normal(next(ks), shape, jnp.float32) * scale

    def gain(shape):
        return 1.0 + nrm(shape, 0.05)

    D = D_MODEL
    F = FFN_HIDDEN
    return {
        'x': nrm((BATCH, SEQ, D), 1.0),
        'c': nrm((BATCH, D), 1.0),
        'ctx': nrm((BATCH, CTX_LEN, D), 1.0),
        'c_ctx': nrm((D,), 1.0),
        'ada_w': nrm((DEPTH, D, 6 * D), 0.5 * D ** -0.5),
        'ada_b': nrm((DEPTH, 6 * D), 0.02),
        'norm_mix_pre': gain((DEPTH, D)),
        'norm_mix_post': gain((DEPTH, D)),
        'norm_ffn_pre': gain((DEPTH, D)),
        'norm_ffn_post': gain((DEPTH, D)),
        'ffn_w_up': nrm((DEPTH, D, 2 * F), D ** -0.5),
        'ffn_conv_w': nrm((DEPTH, FFN_KERNEL, F), FFN_KERNEL ** -0.5),
        'ffn_conv_b': nrm((DEPTH, F), 0.02),
        'ffn_w_down': nrm((DEPTH, F, D), F ** -0.5),
        'ab_w_in': nrm((N_EVEN, D, AB_IN), D ** -0.5),
        'a_conv_w': nrm((N_EVEN, A_KERNEL, A_WIDTH), A_KERNEL ** -0.5),
        'a_conv_b': nrm((N_EVEN, A_WIDTH), 0.02),
        'a_ln_g': gain((N_EVEN, A_WIDTH)),
        'a_ln_b': nrm((N_EVEN, A_WIDTH), 0.02),
        'b_lambda': nrm((N_EVEN, 4, B_HEAD_DIM), 0.1),
        'b_subln': gain((N_EVEN, B_V_DIM)),
        'ab_w_out': nrm((N_EVEN, AB_OUT, D), AB_OUT ** -0.5),
        'c_w_in': nrm((N_ODD, D, C_IN), D ** -0.5),
        'c_q_norm': gain((N_ODD, C_Q_RANK)),
        'c_kv_norm': gain((N_ODD, C_KV_RANK)),
        'c_w_uq': nrm((N_ODD, C_Q_RANK, C_HEADS * (C_NOPE + C_ROPE)), C_Q_RANK ** -0.5),
        'c_w_ukv': nrm((N_ODD, C_KV_RANK, C_HEADS * (C_NOPE + C_V)), C_KV_RANK ** -0.5),
        'c_w_out': nrm((N_ODD, C_HEADS * C_V, D), (C_HEADS * C_V) ** -0.5),
    }

def reference(x, c, ctx, c_ctx, ada_w, ada_b, norm_mix_pre, norm_mix_post, norm_ffn_pre, norm_ffn_post,
              ffn_w_up, ffn_conv_w, ffn_conv_b, ffn_w_down, ab_w_in, a_conv_w, a_conv_b, a_ln_g, a_ln_b,
              b_lambda, b_subln, ab_w_out, c_w_in, c_q_norm, c_kv_norm, c_w_uq, c_w_ukv, c_w_out):
    silu_c = jax.nn.silu(c)
    silu_cc = jax.nn.silu(c_ctx)
    for i in range(DEPTH):
        with_ctx = i < DEPTH - 1
        mx = jnp.split((silu_c @ ada_w[i] + ada_b[i])[:, None, :], 6, axis=-1)
        mc = jnp.split((silu_cc @ ada_w[i] + ada_b[i])[None, None, :], 6, axis=-1)
        hx = modulate(rms_norm(x, norm_mix_pre[i]), mx[0], mx[1])
        hc = modulate(rms_norm(ctx, norm_mix_pre[i]), mc[0], mc[1])
        j = i // 2
        if i % 2 == 0:
            lambda_init = 0.8 - 0.6 * math.exp(-0.3 * i)
            yx, yc = mixer_conv_diff(hx, hc, ab_w_in[j], a_conv_w[j], a_conv_b[j], a_ln_g[j], a_ln_b[j],
                                     b_lambda[j], b_subln[j], ab_w_out[j], lambda_init, with_ctx)
        else:
            yx, yc = mixer_mla(hx, hc, c_w_in[j], c_q_norm[j], c_kv_norm[j], c_w_uq[j], c_w_ukv[j],
                               c_w_out[j], with_ctx)
        x = x + mx[2] * rms_norm(yx, norm_mix_post[i])
        hx = modulate(rms_norm(x, norm_ffn_pre[i]), mx[3], mx[4])
        x = x + mx[5] * rms_norm(conv_ffn(hx, ffn_w_up[i], ffn_conv_w[i], ffn_conv_b[i], ffn_w_down[i]),
                                 norm_ffn_post[i])
        if with_ctx:
            ctx = ctx + mc[2] * rms_norm(yc, norm_mix_post[i])
            hc = modulate(rms_norm(ctx, norm_ffn_pre[i]), mc[3], mc[4])
            ctx = ctx + mc[5] * rms_norm(conv_ffn(hc, ffn_w_up[i], ffn_conv_w[i], ffn_conv_b[i], ffn_w_down[i]),
                                         norm_ffn_post[i])
    return x


_drawn_inputs = setup_inputs


def setup_inputs(seed=0):
    import zlib

    import numpy as np

    out = dict(_drawn_inputs(seed))
    spreads = {}
    factors = {'norm_mix_pre': 3.671,
     'norm_ffn_post': 2.856,
     'ffn_conv_b': 7.992,
     'a_conv_b': 7.653,
     'a_ln_g': 5.226,
     'a_ln_b': 8.0,
     'b_lambda': 7.274,
     'b_subln': 3.791,
     'c_q_norm': 8.0,
     'c_kv_norm': 3.805}
    for name, (base, spread) in spreads.items():
        noise = np.random.default_rng([zlib.crc32(name.encode()), seed]).standard_normal(out[name].shape)
        drawn = base * np.exp(spread * noise) if base else spread * noise
        out[name] = jnp.asarray(drawn.astype(out[name].dtype))
    for name, factor in factors.items():
        out[name] = (out[name] * factor).astype(out[name].dtype)
    return out
```

```python
import math
from collections import namedtuple
from contextlib import ExitStack, contextmanager

import numpy as np

import concourse.bass as bass
from concourse import mybir

F32 = mybir.dt.float32
F32R = mybir.dt.float32r
ALU = mybir.AluOpType
ACT = mybir.ActivationFunctionType
AX = mybir.AxisListType

P = 128
BANK = 512
D = 1024
KD = D // P
SEQ = 1024
CTX = 256
T = SEQ + CTX
XT = SEQ // P
TT = T // P
GRID_W = 64
ROPE_BASE = 10000.0
RMS_EPS = 1e-6
LN_EPS = 1e-5

A_WIDTH = 512
A_KERNEL = 31
B_HEADS = 4
B_DIM = 64
LAMBDA_INIT = 0.8 - 0.6 * math.exp(-0.3 * 0)
C_HEADS = 16
C_NOPE = 64
C_ROPE = 32
C_V = 64
C_Q_RANK = 768
C_KV_RANK = 256
C_IN = C_Q_RANK + C_KV_RANK + C_ROPE
FFN = 2816
FT = FFN // P

MIX_SHIFT, MIX_SCALE, MIX_GATE, FFN_SHIFT, FFN_SCALE, FFN_GATE = range(6)


def token_chunks(tokens):
    return [(a, min(BANK, tokens - a)) for a in range(0, tokens, BANK)]


class Signal:

    def __init__(self, sem, ahead=0, step=1):
        self.sem, self.ahead, self.step = sem, ahead, step

    def nth(self, n):
        return n * self.step + (1 + self.ahead) * self.step


@contextmanager
def stage(nc, name, signals, ahead=()):
    ahead = dict(ahead)
    handles = [nc.alloc_semaphore(name=f"{name}_{n}") for n in signals]
    yield namedtuple("Signals", signals)(*(
        Signal(h, ahead.get(n, 0), 16 if n.endswith("_in") or n.endswith("_stored") else 1)
        for n, h in zip(signals, handles)))
    nc.clear_and_free_semaphores(handles)
    nc.all_engine_barrier()


def start_ahead(eng, *signals):
    for signal in signals:
        eng.sem_inc(signal.sem, signal.ahead * signal.step)


def exact_product(pe, out, a_hi, a_lo, b_hi, b_lo, first, last):
    pe.matmul(out, a_hi, b_hi, start=first, stop=False)
    pe.matmul(out, a_hi, b_lo, start=False, stop=False)
    return pe.matmul(out, a_lo, b_hi, start=False, stop=last)


def row(ap_1d, n=P):
    return ap_1d.rearrange("(a n) -> a n", a=1).broadcast_to([n, ap_1d.shape[0]])


def column(ap_1d):
    return ap_1d.rearrange("(k p) -> p k", p=P)


def modulation(nc, mod, c, c_ctx, ada_w, ada_b):
    CH = 6 * D // BANK
    with ExitStack() as ctx:
        def sb(label, shape, dt=F32):
            return ctx.enter_context(nc.sbuf_tensor(f"mod_{label}", shape, dt))

        cond = sb("cond", [P, 2, KD])
        silu = sb("silu", [P, KD, 2])
        w = sb("w", [P, 2, KD, BANK])
        bias = sb("bias", [2, 2 * 6 * D])
        rows = sb("rows", [2, 2 * 6 * D])
        ps = ctx.enter_context(nc.psum_tensor("mod_ps", [P, 2, BANK], F32))
        s = ctx.enter_context(stage(nc, "mod", [
            "small_in", "w0_in", "w1_in", "asked", "silu_done", "product", "row_done", "rows_stored"],
            {"product": 2, "row_done": 2}))
        w_in = [s.w0_in, s.w1_in]
        block = ctx.enter_context(nc.Block())

        @block.sync
        def _(sp):
            for r, vec in enumerate((c, c_ctx)):
                sp.dma_start(cond[:, r, :], column(vec), allow_slow_non_contiguous=True)\
                  .then_inc(s.small_in.sem, 16)
            sp.dma_start(bias[:, :], row(ada_b.rearrange("l n -> (l n)"), 2)).then_inc(s.small_in.sem, 16)
            for layer in range(2):
                tiles = ada_w[layer].rearrange("(k p) n -> p k n", p=P)
                with sp.Fori(0, CH // 2) as i:
                    for j in range(2):
                        n = i * 2 + (CH * layer + j)
                        sp.wait_ge(s.product.sem, s.product.nth(n - 2))
                        sp.sem_inc(s.asked.sem, 1)
                        sp.dma_start(w[:, j, :, :], tiles[:, :, bass.ds(i * (2 * BANK) + j * BANK, BANK)])\
                          .then_inc(w_in[j].sem, 16)
            sp.wait_ge(s.row_done.sem, s.row_done.nth(2 * CH - 1))
            sp.dma_start(mod, rows[:, :]).then_inc(s.rows_stored.sem, 16)
            sp.wait_ge(s.rows_stored.sem, 16)

        @block.scalar
        def _(act):
            act.wait_ge(s.small_in.sem, s.small_in.nth(2))
            act.activation(silu[:, :, :], cond[:, :, :].rearrange("p r k -> p k r"), ACT.Silu)\
               .then_inc(s.silu_done.sem, 1)

        @block.tensor
        def _(pe):
            start_ahead(pe, s.product)
            pe.wait_ge(s.silu_done.sem, s.silu_done.nth(0))
            for layer in range(2):
                with pe.Fori(0, CH // 2) as i:
                    for j in range(2):
                        n = i * 2 + (CH * layer + j)
                        pe.wait_ge(w_in[j].sem, w_in[j].nth(i + CH // 2 * layer))
                        pe.wait_ge(s.row_done.sem, s.row_done.nth(n - 2))
                        for k in range(KD):
                            mm = pe.matmul(ps[0:2, j, :], silu[:, k, :], w[:, j, k, :],
                                           start=k == 0, stop=k == KD - 1)
                        mm.then_inc(s.product.sem, 1)

        @block.vector
        def _(dve):
            start_ahead(dve, s.row_done)
            dve.wait_ge(s.small_in.sem, s.small_in.nth(2))
            for layer in range(2):
                with dve.Fori(0, CH // 2) as i:
                    for j in range(2):
                        n = i * 2 + (CH * layer + j)
                        dve.wait_ge(s.product.sem, s.product.nth(n))
                        part = bass.ds(i * (2 * BANK) + (6 * D * layer + BANK * j), BANK)
                        dve.tensor_tensor(rows[:, part], ps[0:2, j, :], bias[:, part], ALU.add)\
                           .then_inc(s.row_done.sem, 1)


def load_constants(nc, consts, ident, turn_a, turn_c):
    with ExitStack() as ctx:
        s = ctx.enter_context(stage(nc, "const", ["const_in"]))
        block = ctx.enter_context(nc.Block())

        @block.sync
        def _(sp):
            for j, m in enumerate((ident, turn_a, turn_c)):
                sp.dma_start(m[:, :], consts[:, j * P:(j + 1) * P]).then_inc(s.const_in.sem, 16)
            sp.wait_ge(s.const_in.sem, 48)


class TokenTail:

    SIGNALS = ["half_set", "rows_in", "gs_done", "x0_in", "x1_in", "x2_in", "square", "rstd_step", "rstd", "post_step", "x_new",
               "x0_stored", "x1_stored", "x2_stored", "pre_step", "h_done", "h_turned", "h_hi", "h_lo"]

    def __init__(self, nc, ctx, name, s, post, pre, kinds, turns, ident):
        def sb(label, shape, dt=F32):
            return ctx.enter_context(nc.sbuf_tensor(f"{name}_{label}", shape, dt))

        self.s, self.post, self.pre, self.kinds, self.ident = s, post, pre, kinds, ident
        self.turns = turns
        self.x_in = [s.x0_in, s.x1_in, s.x2_in]
        self.x_stored = [s.x0_stored, s.x1_stored, s.x2_stored]
        self.x = sb("x", [P, 3, D])
        self.junk = sb("junk", [P, D])
        self.small = sb("small", [P, 8, TT])
        self.minus_half = sb("minus_half", [P, 1])
        self.rows = sb("rows", [P, kinds * (3 if post and pre else 1 if post else 2), D])
        if pre:
            self.h = sb("h", [P, 2, D])
            self.turned = ctx.enter_context(nc.psum_tensor(f"{name}_turned", [P, 2, BANK], F32))
        n = 0
        self.gate_row = self.scale_row = self.shift_row = None
        if post:
            self.gate_row, n = n, kinds
        if pre:
            self.scale_row, self.shift_row = n, n + kinds
        self.squares_per_tile = (1 if post else 0) + (1 if pre else 0)
        self.row_loads = kinds * ((1 if post else 0) + (2 if pre else 0)) + (1 if post else 0) + (1 if pre else 0)

    def kind(self, tile):
        return 0 if tile < XT else 1

    def load_rows(self, sp):
        s = self.s
        if self.post:
            gates, gain = self.post
            for r in range(self.kinds):
                sp.dma_start(self.rows[:, self.gate_row + r, :], row(gates[r])).then_inc(s.rows_in.sem, 16)
            sp.dma_start(self.x[:, 0, :], row(gain)).then_inc(s.rows_in.sem, 16)
        if self.pre:
            scales, shifts, gain = self.pre
            for r in range(self.kinds):
                sp.dma_start(self.rows[:, self.scale_row + r, :], row(scales[r])).then_inc(s.rows_in.sem, 16)
                sp.dma_start(self.rows[:, self.shift_row + r, :], row(shifts[r])).then_inc(s.rows_in.sem, 16)
            sp.dma_start(self.x[:, 1, :], row(gain)).then_inc(s.rows_in.sem, 16)
        sp.wait_ge(s.gs_done.sem, s.gs_done.nth((1 if self.post else 0) * self.kinds
                                                + (1 if self.pre else 0) * self.kinds - 1))

    def load_x(self, sp, turn, src):
        s = self.s
        if turn >= 3:
            if self.post:
                sp.wait_ge(self.x_stored[turn % 3].sem, 16 * (turn // 3))
            if self.pre:
                sp.wait_ge(s.h_done.sem, turn - 2)
        sp.dma_start(self.x[:, turn % 3, :], src).then_inc(self.x_in[turn % 3].sem, 16)

    def store_x(self, sp, turn, dst):
        s = self.s
        sp.wait_ge(s.x_new.sem, turn + 1)
        sp.dma_start(dst, self.x[:, turn % 3, :]).then_inc(self.x_stored[turn % 3].sem, 16)

    def stores_over(self, sp):
        for j, stored in enumerate(self.x_stored):
            sp.wait_ge(stored.sem, 16 * len(range(j, self.turns, 3)))

    def prepare_rows(self, dve):
        s = self.s
        dve.wait_ge(s.rows_in.sem, 16 * self.row_loads)
        if self.post:
            for r in range(self.kinds):
                g = self.rows[:, self.gate_row + r, :]
                dve.tensor_tensor(g, g, self.x[:, 0, :], ALU.mult).then_inc(s.gs_done.sem, 1)
        if self.pre:
            for r in range(self.kinds):
                g = self.rows[:, self.scale_row + r, :]
                dve.scalar_tensor_tensor(out=g, in0=g, scalar=1.0, in1=self.x[:, 1, :],
                                         op0=ALU.add, op1=ALU.mult).then_inc(s.gs_done.sem, 1)
        dve.wait_ge(s.gs_done.sem, self.kinds * self.squares_per_tile)

    def post_vector(self, dve, turn, tile, y):
        s = self.s
        x = self.x[:, turn % 3, :]
        dve.wait_ge(s.rstd.sem, self.square_of_post(turn) + 1)
        dve.scalar_tensor_tensor(out=y, in0=y, scalar=self.small[:, 2, turn:turn + 1],
                                 in1=self.rows[:, self.gate_row + self.kind(tile), :],
                                 op0=ALU.mult, op1=ALU.mult).then_inc(s.post_step.sem, 1)
        dve.wait_ge(s.post_step.sem, turn + 1)
        dve.wait_ge(self.x_in[turn % 3].sem, 16 * (turn // 3 + 1))
        dve.tensor_tensor(x, x, y, ALU.add).then_inc(s.x_new.sem, 1)

    def pre_vector(self, dve, turn, tile):
        s = self.s
        x, h = self.x[:, turn % 3, :], self.h[:, turn % 2, :]
        dve.wait_ge(s.rstd.sem, self.square_of_pre(turn) + 1)
        if turn >= 2:
            dve.wait_ge(s.h_turned.sem, 2 * (turn - 1))
        dve.scalar_tensor_tensor(out=h, in0=x, scalar=self.small[:, 5, turn:turn + 1],
                                 in1=self.rows[:, self.scale_row + self.kind(tile), :],
                                 op0=ALU.mult, op1=ALU.mult).then_inc(s.pre_step.sem, 1)
        dve.wait_ge(s.pre_step.sem, turn + 1)
        dve.tensor_tensor(h, h, self.rows[:, self.shift_row + self.kind(tile), :], ALU.add)\
           .then_inc(s.h_done.sem, 1)

    def split_vector(self, dve, turn, hi, lo):
        s = self.s
        for b in range(2):
            dve.wait_ge(s.h_hi.sem, 2 * turn + b + 1)
            dve.tensor_tensor(lo[:, 4 * b:4 * b + 4, :],
                              self.turned[:, b, :].rearrange("p (k n) -> p k n", n=P),
                              hi[:, 4 * b:4 * b + 4, :].bitcast(F32), ALU.subtract).then_inc(s.h_lo.sem, 1)

    def square_of_post(self, turn):
        return turn if not self.pre else (0 if turn == 0 else 2 * turn - 1)

    def square_of_pre(self, turn):
        if not self.post:
            return turn
        return 2 * turn + 2 if turn < self.turns - 1 else 2 * turn + 1

    def square(self, act, n, src, out):
        s = self.s
        if n:
            act.wait_ge(s.square.sem, n)
        act.activation(self.junk[:, :], src, ACT.Square, accum_out=out).then_inc(s.square.sem, 1)

    def post_scalar(self, act, turn, y):
        self.square(act, self.square_of_post(turn), y, self.small[:, 0, turn:turn + 1])

    def pre_scalar(self, act, turn):
        s = self.s
        if self.post:
            act.wait_ge(s.x_new.sem, turn + 1)
        else:
            act.wait_ge(self.x_in[turn % 3].sem, 16 * (turn // 3 + 1))
        self.square(act, self.square_of_pre(turn), self.x[:, turn % 3, :], self.small[:, 3, turn:turn + 1])

    def split_scalar(self, act, turn, hi):
        s = self.s
        for b in range(2):
            act.wait_ge(s.h_turned.sem, 2 * turn + b + 1)
            act.activation(hi[:, 4 * b:4 * b + 4, :], self.turned[:, b, :].rearrange("p (k n) -> p k n", n=P),
                           ACT.Copy).then_inc(s.h_hi.sem, 1)

    def prepare_gpsimd(self, pool):
        pool.memset(self.minus_half[:, :], -0.5).then_inc(self.s.half_set.sem, 1)
        pool.wait_ge(self.s.half_set.sem, 1)

    def rstd_gpsimd(self, pool, n, turn, at):
        s = self.s
        ss, ms, rstd = (self.small[:, at + j, turn:turn + 1] for j in range(3))
        pool.wait_ge(s.square.sem, n + 1)
        pool.tensor_scalar(ms, ss, 1.0 / D, RMS_EPS, ALU.mult, ALU.add).then_inc(s.rstd_step.sem, 1)
        pool.wait_ge(s.rstd_step.sem, n + 1)
        pool.tensor_tensor(rstd, ms, self.minus_half[:, :], ALU.pow).then_inc(s.rstd.sem, 1)

    def post_gpsimd(self, pool, turn):
        self.rstd_gpsimd(pool, self.square_of_post(turn), turn, 0)

    def pre_gpsimd(self, pool, turn):
        self.rstd_gpsimd(pool, self.square_of_pre(turn), turn, 3)

    def turn_tensor(self, pe, turn):
        s = self.s
        pe.wait_ge(s.h_done.sem, turn + 1)
        for b in range(2):
            if turn:
                pe.wait_ge(s.h_lo.sem, 2 * (turn - 1) + b + 1)
            for k in range(4):
                mm = pe.transpose(self.turned[:, b, k * P:(k + 1) * P],
                                  self.h[:, turn % 2, (4 * b + k) * P:(4 * b + k + 1) * P], self.ident[:, :])
            mm.then_inc(s.h_turned.sem, 1)


def first_norm(nc, h_hi, h_lo, x, ctx_rows, pre, ident):
    with ExitStack() as ctx:
        s = ctx.enter_context(stage(nc, "norm", TokenTail.SIGNALS))
        tail = TokenTail(nc, ctx, "norm", s, None, pre, 2, TT, ident)
        block = ctx.enter_context(nc.Block())

        @block.sync
        def _(sp):
            tail.load_rows(sp)
            for t in range(TT):
                tail.load_x(sp, t, x[t * P:(t + 1) * P, :] if t < XT else ctx_rows[(t - XT) * P:(t - XT + 1) * P, :])

        @block.scalar
        def _(act):
            act.wait_ge(s.gs_done.sem, 2)
            for t in range(TT + 1):
                if t < TT:
                    tail.pre_scalar(act, t)
                if t >= 1:
                    tail.split_scalar(act, t - 1, h_hi[:, :, (t - 1) * P:t * P])

        @block.vector
        def _(dve):
            tail.prepare_rows(dve)
            for t in range(TT + 1):
                if t < TT:
                    tail.pre_vector(dve, t, t)
                if t >= 1:
                    tail.split_vector(dve, t - 1, h_hi[:, :, (t - 1) * P:t * P], h_lo[:, :, (t - 1) * P:t * P])

        @block.gpsimd
        def _(pool):
            tail.prepare_gpsimd(pool)
            for t in range(TT):
                tail.pre_gpsimd(pool, t)

        @block.tensor
        def _(pe):
            for t in range(TT):
                tail.turn_tensor(pe, t)


def project_conv_diff(nc, h_hi, h_lo, conv_out, qk, v_rows, w_in, conv_w, conv_b, cos, sin, turn):
    chunks = token_chunks(T)
    NC = len(chunks)
    HALO = A_KERNEL // 2
    PAD = T + 3 * HALO
    SPAN = T + HALO
    AT = A_WIDTH // P
    QT = 2 * B_HEADS
    PIECES = 2 * AT + QT + A_WIDTH // P

    def padded(a):
        return a + HALO + (HALO if a >= SEQ else 0)

    with ExitStack() as ctx:
        def sb(label, shape, dt=F32):
            return ctx.enter_context(nc.sbuf_tensor(f"ab_{label}", shape, dt))

        raw = sb("raw", [P, 2, KD, P])
        w_hi = sb("w_hi", [P, 2, KD, P], F32R)
        w_lo = sb("w_lo", [P, 2, KD, P], F32R)
        v_hi = sb("v_hi", [P, KD, A_WIDTH], F32R)
        v_lo = sb("v_lo", [P, KD, A_WIDTH], F32R)
        u = sb("u", [P, PAD])
        conv = sb("conv", [P, SPAN])
        sig = sb("sig", [P, T])
        taps = sb("taps", [P, AT, A_KERNEL + 1])
        cos_t = sb("cos", [P, SEQ])
        sin_t = sb("sin", [P, SEQ])
        qk_t = sb("qk", [P, 2, T])
        part = sb("part", [P, 2, SEQ])
        v_t = sig
        main_ps = ctx.enter_context(nc.psum_tensor("ab_main", [P, 2, NC, BANK], F32))
        turn_ps = ctx.enter_context(nc.psum_tensor("ab_turn", [P, 2, BANK], F32))
        s = ctx.enter_context(stage(nc, "ab", [
            "small_in", "raw0_in", "raw1_in", "asked", "hi_done", "w_ready", "zeroed", "full0", "full1",
            "sig_done", "u_done", "conv_step", "conv_done", "conv_stored", "storing", "conv_free", "qk_free", "copied", "turned", "cos_part",
            "sin_part", "sum_done", "qk0_stored", "qk1_stored", "v_full", "v_copied", "v0_stored",
            "v1_stored"],
            {"sig_done": 3, "u_done": 3, "conv_done": 1, "conv_free": 1, "copied": 2, "cos_part": 2,
             "sin_part": 4, "sum_done": 2, "qk_free": 2, "w_ready": 2, "full0": 1, "full1": 1}))
        s.conv_stored.step = 32
        qk_stored, v_stored = [s.qk0_stored, s.qk1_stored], [s.v0_stored, s.v1_stored]
        raw_in, full = [s.raw0_in, s.raw1_in], [s.full0, s.full1]
        block = ctx.enter_context(nc.Block())
        w_tiles = w_in.rearrange("(k p) n -> p k n", p=P)

        def loops(eng, pair_ab, pair_qk, piece_v):
            with eng.Fori(0, AT) as i:
                pair_ab(i)
            with eng.Fori(0, QT // 2) as i:
                pair_qk(i)
            for j in range(AT):
                piece_v(j)

        @block.sync
        def _(sp):
            for j in range(AT):
                sp.dma_start(taps[:, j, 0:A_KERNEL], conv_w[:, j * P:(j + 1) * P].rearrange("t p -> p t"),
                             allow_slow_non_contiguous=True).then_inc(s.small_in.sem, 16)
                sp.dma_start(taps[:, j, A_KERNEL:], conv_b[j * P:(j + 1) * P].rearrange("(p a) -> p a", a=1))\
                  .then_inc(s.small_in.sem, 16)
            sp.dma_start(cos_t[:, :], cos).then_inc(s.small_in.sem, 16)
            sp.dma_start(sin_t[:, :], sin).then_inc(s.small_in.sem, 16)

            def load(piece, slot, cols):
                sp.wait_ge(s.w_ready.sem, s.w_ready.nth(piece - 2))
                sp.sem_inc(s.asked.sem, 1)
                sp.dma_start(raw[:, slot, :, :], w_tiles[:, :, cols]).then_inc(raw_in[slot].sem, 16)

            def pair_ab(i):
                load(i * 2, 0, bass.ds(i * P + A_WIDTH, P))
                load(i * 2 + 1, 1, bass.ds(i * P, P))

            def pair_qk(i):
                for j in range(2):
                    load(i * 2 + (2 * AT + j), j, bass.ds(i * (2 * P) + (2 * A_WIDTH + j * P), P))

            def piece_v(j):
                first = 2 * A_WIDTH + QT * P + j * P
                load(2 * AT + QT + j, j % 2, slice(first, first + P))

            loops(sp, pair_ab, pair_qk, piece_v)

        @block.scalar
        def _(act):
            start_ahead(act, s.sig_done, s.copied)

            def hi(piece, slot, n, dst):
                act.wait_ge(raw_in[slot].sem, raw_in[slot].nth(n))
                act.activation(dst, raw[:, slot, :, :], ACT.Copy).then_inc(s.hi_done.sem, 1)

            def pair_ab(i):
                for j in range(2):
                    act.wait_ge(full[j].sem, full[j].nth(i * NC - 1))
                    hi(i * 2 + j, j, i, w_hi[:, j, :, :])
                act.wait_ge(s.u_done.sem, s.u_done.nth(i * NC - 1))
                for c, (a, n) in enumerate(chunks):
                    act.wait_ge(s.full0.sem, s.full0.nth(i * NC + c))
                    act.activation(sig[:, a:a + n], main_ps[:, 0, c, 0:n], ACT.Sigmoid).then_inc(s.sig_done.sem, 1)

            def pair_qk(i):
                for j in range(2):
                    act.wait_ge(full[j].sem, full[j].nth(i * NC + (AT * NC - 1)))
                    hi(i * 2 + (2 * AT + j), j, i + AT, w_hi[:, j, :, :])
                for j in range(2):
                    act.wait_ge(s.qk_free.sem, s.qk_free.nth(i * 2 + (j - 2)))
                    for c, (a, n) in enumerate(chunks):
                        act.wait_ge(full[j].sem, full[j].nth(i * NC + (AT * NC + c)))
                        ins = act.activation(qk_t[:, j, a:a + n], main_ps[:, j, c, 0:n], ACT.Copy)
                    ins.then_inc(s.copied.sem, 1)

            def piece_v(j):
                hi(2 * AT + QT + j, j % 2, AT + QT // 2 + j // 2, v_hi[:, :, j * P:(j + 1) * P])

            loops(act, pair_ab, pair_qk, piece_v)
            act.wait_ge(s.u_done.sem, s.u_done.nth(AT * NC - 1))
            for t in range(TT):
                act.wait_ge(s.v_full.sem, t + 1)
                if t >= 2:
                    act.wait_ge(v_stored[t % 2].sem, 16 * (t // 2))
                act.activation(v_t[:, (t % 2) * BANK:(t % 2 + 1) * BANK], turn_ps[:, t % 2, :], ACT.Copy)\
                   .then_inc(s.v_copied.sem, 1)

        @block.vector
        def _(dve):
            start_ahead(dve, s.w_ready, s.u_done, s.conv_done, s.sin_part, s.sum_done)
            dve.memset(u[:, :], 0.0).then_inc(s.zeroed.sem, 1)
            dve.wait_ge(s.zeroed.sem, 1)
            dve.wait_ge(s.small_in.sem, s.small_in.nth(2 * AT + 1))

            def lo(piece, slot, hi_part, dst):
                dve.wait_ge(s.hi_done.sem, s.hi_done.nth(piece))
                dve.tensor_tensor(dst, raw[:, slot, :, :], hi_part.bitcast(F32), ALU.subtract)\
                   .then_inc(s.w_ready.sem, 1)

            def pair_ab(i):
                for j in range(2):
                    lo(i * 2 + j, j, w_hi[:, j, :, :], w_lo[:, j, :, :])
                dve.wait_ge(s.conv_done.sem, s.conv_done.nth(i - 1))
                for c, (a, n) in enumerate(chunks):
                    dve.wait_ge(s.sig_done.sem, s.sig_done.nth(i * NC + c))
                    dve.wait_ge(s.full1.sem, s.full1.nth(i * NC + c))
                    dve.tensor_tensor(u[:, padded(a):padded(a) + n], main_ps[:, 1, c, 0:n], sig[:, a:a + n],
                                      ALU.mult).then_inc(s.u_done.sem, 1)
                dve.wait_ge(s.u_done.sem, s.u_done.nth(i * NC + (NC - 1)))
                dve.wait_ge(s.conv_free.sem, s.conv_free.nth(i - 1))
                w = taps[:, bass.ds(i, 1), :]
                steps = A_KERNEL - 1
                dve.tensor_scalar(conv[:, :], u[:, 0:SPAN], w[:, 0, 0:1], w[:, 0, A_KERNEL:], ALU.mult, ALU.add)\
                   .then_inc(s.conv_step.sem, 1)
                for j in range(1, A_KERNEL):
                    dve.wait_ge(s.conv_step.sem, s.conv_step.nth(i * steps + (j - 1)))
                    dve.scalar_tensor_tensor(out=conv[:, :], in0=u[:, j:j + SPAN], scalar=w[:, 0, j:j + 1],
                                             in1=conv[:, :], op0=ALU.mult, op1=ALU.add)\
                       .then_inc((s.conv_step if j < A_KERNEL - 1 else s.conv_done).sem, 1)

            def pair_qk(i):
                for j in range(2):
                    lo(i * 2 + (2 * AT + j), j, w_hi[:, j, :, :], w_lo[:, j, :, :])
                for j in range(2):
                    n = i * 2 + j
                    for c in range(2):
                        dve.wait_ge(s.turned.sem, s.turned.nth(n * 2 + c))
                        dve.tensor_tensor(part[:, j, c * BANK:(c + 1) * BANK], turn_ps[:, c, :],
                                          sin_t[:, c * BANK:(c + 1) * BANK], ALU.mult).then_inc(s.sin_part.sem, 1)
                    dve.wait_ge(s.sin_part.sem, s.sin_part.nth(n * 2 + 1))
                    dve.wait_ge(s.cos_part.sem, s.cos_part.nth(n))
                    dve.tensor_tensor(qk_t[:, j, 0:SEQ], qk_t[:, j, 0:SEQ], part[:, j, :], ALU.add)\
                       .then_inc(s.sum_done.sem, 1)

            def piece_v(j):
                lo(2 * AT + QT + j, j % 2, v_hi[:, :, j * P:(j + 1) * P], v_lo[:, :, j * P:(j + 1) * P])

            loops(dve, pair_ab, pair_qk, piece_v)

        @block.gpsimd
        def _(pool):
            start_ahead(pool, s.conv_free, s.cos_part, s.qk_free)
            pool.wait_ge(s.small_in.sem, s.small_in.nth(2 * AT + 1))

            def pair_ab(i):
                pool.wait_ge(s.conv_done.sem, s.conv_done.nth(i))
                pool.sem_inc(s.storing.sem, 1)
                rows = conv_out[bass.ds(i * P, P), :]
                pool.dma_start(rows[:, 0:SEQ], conv[:, 0:SEQ]).then_inc(s.conv_stored.sem, 16)
                pool.dma_start(rows[:, SEQ:T], conv[:, SEQ + HALO:T + HALO]).then_inc(s.conv_stored.sem, 16)
                pool.wait_ge(s.conv_stored.sem, s.conv_stored.nth(i))
                pool.sem_inc(s.conv_free.sem, 1)

            def pair_qk(i):
                for j in range(2):
                    n = i * 2 + j
                    pool.wait_ge(s.turned.sem, s.turned.nth(n * 2 + 1))
                    pool.tensor_tensor(qk_t[:, j, 0:SEQ], qk_t[:, j, 0:SEQ], cos_t[:, :], ALU.mult)\
                        .then_inc(s.cos_part.sem, 1)
                for j in range(2):
                    n = i * 2 + j
                    pool.wait_ge(s.sum_done.sem, s.sum_done.nth(n))
                    pool.sem_inc(s.storing.sem, 1)
                    pool.dma_start(qk[bass.ds(i * (2 * P) + j * P, P), :], qk_t[:, j, :])\
                        .then_inc(qk_stored[j].sem, 16)
                for j in range(2):
                    pool.wait_ge(qk_stored[j].sem, qk_stored[j].nth(i))
                    pool.sem_inc(s.qk_free.sem, 1)

            loops(pool, pair_ab, pair_qk, lambda j: None)
            for t in range(TT):
                pool.wait_ge(s.v_copied.sem, t + 1)
                pool.dma_start(v_rows[t * P:(t + 1) * P, :], v_t[:, (t % 2) * BANK:(t % 2 + 1) * BANK])\
                    .then_inc(v_stored[t % 2].sem, 16)
            for j in range(2):
                pool.wait_ge(v_stored[j].sem, 16 * TT // 2)

        @block.tensor
        def _(pe):
            start_ahead(pe, s.full0, s.full1)

            def product(piece, j, bank_read):
                pe.wait_ge(s.w_ready.sem, s.w_ready.nth(piece))
                for c, (a, n) in enumerate(chunks):
                    bank_read(c)
                    for k in range(KD):
                        mm = exact_product(pe, main_ps[:, j, c, 0:n], w_hi[:, j, k, :], w_lo[:, j, k, :],
                                           h_hi[:, k, a:a + n], h_lo[:, k, a:a + n], k == 0, k == KD - 1)
                    mm.then_inc(full[j].sem, 1)

            def pair_ab(i):
                product(i * 2, 0, lambda c: pe.wait_ge(s.sig_done.sem, s.sig_done.nth(i * NC + (c - NC))))
                product(i * 2 + 1, 1, lambda c: pe.wait_ge(s.u_done.sem, s.u_done.nth(i * NC + (c - NC))))

            def pair_qk(i):
                for j in range(2):
                    pe.wait_ge(s.copied.sem, s.copied.nth(i * 2 + (j - 2)))
                    if j == 0:
                        pe.wait_ge(s.sig_done.sem, s.sig_done.nth(AT * NC - 1))
                    else:
                        pe.wait_ge(s.u_done.sem, s.u_done.nth(AT * NC - 1))
                    product(i * 2 + (2 * AT + j), j, lambda c: None)
                for j in range(2):
                    n = i * 2 + j
                    pe.wait_ge(s.copied.sem, s.copied.nth(n))
                    for c in range(2):
                        pe.wait_ge(s.sin_part.sem, s.sin_part.nth(n * 2 + (c - 2)))
                        pe.matmul(turn_ps[:, c, :], turn[:, :], qk_t[:, j, c * BANK:(c + 1) * BANK],
                                  start=True, stop=True).then_inc(s.turned.sem, 1)

            loops(pe, pair_ab, pair_qk, lambda j: None)
            pe.wait_ge(s.w_ready.sem, s.w_ready.nth(PIECES - 1))
            for t in range(TT):
                if t < 2:
                    pe.wait_ge(s.sin_part.sem, s.sin_part.nth((QT - 1) * 2 + t))
                else:
                    pe.wait_ge(s.v_copied.sem, t - 1)
                for k in range(KD):
                    mm = exact_product(pe, turn_ps[:, t % 2, :], h_hi[:, k, t * P:(t + 1) * P],
                                       h_lo[:, k, t * P:(t + 1) * P], v_hi[:, k, :], v_lo[:, k, :],
                                       k == 0, k == KD - 1)
                mm.then_inc(s.v_full.sem, 1)


@contextmanager
def bare_stage(nc, name, signals):
    handles = {n: nc.alloc_semaphore(name=f"{name}_{n}") for n in signals}
    yield namedtuple("Semaphores", signals)(*handles.values())
    nc.clear_and_free_semaphores(list(handles.values()))
    nc.all_engine_barrier()


def ffn(nc, name, tokens, h_hi, h_lo, y_sum, w_up, conv_w, conv_b, w_down):
    chunks = token_chunks(tokens)
    NC = len(chunks)
    TT = tokens // P
    SUMS = 2 * TT
    segments = [(0, SEQ)] + ([(SEQ, CTX)] if tokens > SEQ else [])
    NS = len(segments)
    PAD = tokens + 1 + NS
    GROUPS = FT // 2

    def padded(a):
        return a + 1 + (a >= SEQ)

    with ExitStack() as ctx:
        def sb(label, shape, dt=F32):
            return ctx.enter_context(nc.sbuf_tensor(f"{name}_{label}", shape, dt))

        def ps(label, shape):
            return ctx.enter_context(nc.psum_tensor(f"{name}_{label}", shape, F32))

        raw = sb("raw", [P, 2, D])
        w_hi = sb("w_hi", [P, 4, D], F32R)
        w_lo = sb("w_lo", [P, 4, D], F32R)
        act_hi = sb("act_hi", [P, 2, tokens], F32R)
        act_lo = sb("act_lo", [P, 2, tokens], F32R)
        gate = sb("gate", [P, PAD])
        conv = sb("conv", [P, PAD])
        taps = sb("taps", [P, 4, FT])
        gate_ps = ps("gate_ps", [P, NC, BANK])
        val_ps = ps("val_ps", [P, NC, BANK])
        down_ps = ps("down_ps", [P, 2, BANK])

        s = ctx.enter_context(bare_stage(nc, name, [
            "taps_in", "raw_in0", "raw_in1", "raw_free", "w_hi_done", "w_ready", "gate_full", "gate_in",
            "zeroed", "val_full", "val_used", "conv_step", "conv_done", "silu_done",
            "act_hi_done", "act_ready", "sum_full", "sum_done"]))
        raw_in = [s.raw_in0, s.raw_in1]
        block = ctx.enter_context(nc.Block())

        VALUE, GATE, DOWN0, DOWN1 = range(4)
        RAW = (1, 0, 0, 1)
        w_up_tiles = w_up.rearrange("(k p) (two f) -> p k two f", p=P, two=2)

        def schedule(eng, split, gate_product, gate_work, value_product, value_work, down):
            split(GATE, 0, 0)
            split(VALUE, 0, 1)
            for tile in range(2):
                gate_product(tile, 2 * tile)
                gate_work(tile)
                split(GATE, tile + 1, 2 * tile + 2)
                value_product(tile, 2 * tile + 1)
                split(VALUE, tile + 1, 2 * tile + 3)
                value_work(tile, tile)

            def group(g, more):
                gate_product(2 * g, 6 * g - 2)
                gate_work(2 * g)
                split(DOWN0, 2 * g - 2, 6 * g)
                split(DOWN1, 2 * g - 1, 6 * g + 1)
                split(GATE, 2 * g + 1, 6 * g + 2)
                value_product(2 * g, 6 * g - 1)
                split(VALUE, 2 * g + 1, 6 * g + 3)
                down(g - 1, 6 * g + 1)
                value_work(2 * g, 0)
                gate_product(2 * g + 1, 6 * g + 2)
                gate_work(2 * g + 1)
                split(GATE if more else DOWN0, 2 * g + 2 if more else 2 * g, 6 * g + 4)
                value_product(2 * g + 1, 6 * g + 3)
                split(VALUE if more else DOWN1, 2 * g + 2 if more else 2 * g + 1, 6 * g + 5)
                value_work(2 * g + 1, 1)

            with eng.Fori(1, GROUPS - 1) as g:
                group(g, True)
            group(GROUPS - 1, False)
            down(GROUPS - 1, 6 * GROUPS - 1)

        def idle(*_):
            pass

        @block.sync
        def _(sp):
            for j in range(3):
                sp.dma_start(taps[:, j, :], conv_w[j].rearrange("(t p) -> p t", p=P),
                             allow_slow_non_contiguous=True).then_inc(s.taps_in, 16)
            sp.dma_start(taps[:, 3, :], conv_b.rearrange("(t p) -> p t", p=P),
                         allow_slow_non_contiguous=True).then_inc(s.taps_in, 16)

            def split(kind, tile, piece):
                if kind in (GATE, VALUE):
                    src = w_up_tiles[:, :, kind, :][:, :, bass.ds(tile * P, P)]
                else:
                    src = w_down[bass.ds(tile * P, P), :].rearrange("(k p) n -> p k n", k=1)
                if not (isinstance(piece, int) and piece < 2):
                    sp.wait_ge(s.w_ready, piece - 1)
                    sp.sem_inc(s.raw_free, 1)
                slot = RAW[kind]
                sp.dma_start(raw[:, slot, :].rearrange("p (k n) -> p k n", n=src.shape[-1]), src)\
                  .then_inc(raw_in[slot], 16)

            schedule(sp, split, idle, idle, idle, idle, idle)

        @block.scalar
        def _(act):
            def split(kind, tile, piece):
                slot = RAW[kind]
                act.wait_ge(raw_in[slot], (piece - slot) * 8 + 16)
                if kind in (GATE, VALUE):
                    if not (isinstance(tile, int) and tile == 0):
                        act.wait_ge(s.gate_full if kind == GATE else s.val_full, tile * NC)
                else:
                    act.wait_ge(s.sum_full, (tile - slot) * TT + 1)
                act.activation(w_hi[:, kind, :], raw[:, slot, :], ACT.Copy).then_inc(s.w_hi_done, 1)

            def gate_work(tile):
                if isinstance(tile, int) and tile == 0:
                    act.wait_ge(s.zeroed, 2)
                else:
                    act.wait_ge(s.conv_done, tile)
                for c, (a, n) in enumerate(chunks):
                    act.wait_ge(s.gate_full, tile * NC + (c + 1))
                    act.activation(gate[:, padded(a):padded(a) + n], gate_ps[:, c, 0:n], ACT.Copy)\
                       .then_inc(s.gate_in, 1)
                act.wait_ge(s.conv_done, tile + 1)
                act.activation(conv[:, 1:PAD - 1], conv[:, 1:PAD - 1], ACT.Silu).then_inc(s.silu_done, 1)

            def value_work(tile, slot):
                act.wait_ge(s.val_used, tile * NC + NC)
                if not (isinstance(tile, int) and tile < 2):
                    act.wait_ge(s.sum_full, (tile - slot) * TT + 1)
                for b, m in segments:
                    act.activation(act_hi[:, slot, b:b + m], conv[:, padded(b):padded(b) + m], ACT.Copy)\
                       .then_inc(s.act_hi_done, 1)

            schedule(act, split, idle, gate_work, idle, value_work, idle)

        @block.vector
        def _(dve):
            dve.memset(gate[:, :], 0.0).then_inc(s.zeroed, 1)
            dve.memset(y_sum[:, 0:TT, :], 0.0).then_inc(s.zeroed, 1)
            dve.wait_ge(s.zeroed, 2)
            dve.sem_inc(s.sum_done, SUMS)
            dve.wait_ge(s.taps_in, 64)

            def split(kind, tile, piece):
                dve.wait_ge(s.w_hi_done, piece + 1)
                dve.tensor_tensor(w_lo[:, kind, :], raw[:, RAW[kind], :], w_hi[:, kind, :].bitcast(F32),
                                  ALU.subtract).then_inc(s.w_ready, 1)

            def gate_work(tile):
                dve.wait_ge(s.gate_in, tile * NC + NC)
                if not (isinstance(tile, int) and tile == 0):
                    dve.wait_ge(s.act_ready, tile * NS)
                before, here, after, bias = (taps[:, j, bass.ds(tile, 1)] for j in range(4))
                inner = conv[:, 1:PAD - 1]
                dve.tensor_scalar(inner, gate[:, 1:PAD - 1], here, bias, ALU.mult, ALU.add)\
                   .then_inc(s.conv_step, 1)
                dve.wait_ge(s.conv_step, tile * 2 + 1)
                dve.scalar_tensor_tensor(out=inner, in0=gate[:, 0:PAD - 2], scalar=before, in1=inner,
                                         op0=ALU.mult, op1=ALU.add).then_inc(s.conv_step, 1)
                dve.wait_ge(s.conv_step, tile * 2 + 2)
                dve.scalar_tensor_tensor(out=inner, in0=gate[:, 2:PAD], scalar=after, in1=inner,
                                         op0=ALU.mult, op1=ALU.add).then_inc(s.conv_done, 1)

            def value_work(tile, slot):
                dve.wait_ge(s.silu_done, tile + 1)
                for c, (a, n) in enumerate(chunks):
                    dve.wait_ge(s.val_full, tile * NC + (c + 1))
                    part = conv[:, padded(a):padded(a) + n]
                    dve.tensor_tensor(part, val_ps[:, c, 0:n], part, ALU.mult).then_inc(s.val_used, 1)
                for i, (b, m) in enumerate(segments):
                    dve.wait_ge(s.act_hi_done, tile * NS + (i + 1))
                    dve.tensor_tensor(act_lo[:, slot, b:b + m], conv[:, padded(b):padded(b) + m],
                                      act_hi[:, slot, b:b + m].bitcast(F32), ALU.subtract)\
                       .then_inc(s.act_ready, 1)

            def down(group, piece):
                for t in range(TT):
                    for half in range(2):
                        n = t * 2 + half
                        dve.wait_ge(s.sum_full, group * SUMS + (n + 2))
                        dve.wait_ge(s.sum_done, group * SUMS + (n + 1))
                        part = y_sum[:, t, half * BANK:(half + 1) * BANK]
                        dve.tensor_tensor(part, down_ps[:, half, :], part, ALU.add).then_inc(s.sum_done, 1)

            schedule(dve, split, idle, gate_work, idle, value_work, down)

        @block.tensor
        def _(pe):
            pe.sem_inc(s.sum_full, 1)

            def product(kind, bank, full, used, tile, piece):
                pe.wait_ge(s.w_ready, piece + 1)
                for c, (a, n) in enumerate(chunks):
                    if not (isinstance(tile, int) and tile == 0):
                        pe.wait_ge(used, (tile - 1) * NC + (c + 1))
                    for k in range(KD):
                        w = slice(k * P, (k + 1) * P)
                        mm = exact_product(pe, bank[:, c, 0:n], w_hi[:, kind, w], w_lo[:, kind, w],
                                           h_hi[:, k, a:a + n], h_lo[:, k, a:a + n],
                                           k == 0, k == KD - 1)
                    mm.then_inc(full, 1)

            def gate_product(tile, piece):
                product(GATE, gate_ps, s.gate_full, s.gate_in, tile, piece)

            def value_product(tile, piece):
                product(VALUE, val_ps, s.val_full, s.val_used, tile, piece)

            def down(group, piece):
                pe.wait_ge(s.w_ready, piece + 1)
                pe.wait_ge(s.act_ready, (group * 2 + 2) * NS)
                for t in range(TT):
                    for half in range(2):
                        n = t * 2 + half
                        pe.wait_ge(s.sum_done, (group + 1) * SUMS + (n - 1))
                        for j in range(2):
                            mm = exact_product(pe, down_ps[:, half, :],
                                               act_hi[:, j, t * P:(t + 1) * P],
                                               act_lo[:, j, t * P:(t + 1) * P],
                                               w_hi[:, DOWN0 + j, half * BANK:(half + 1) * BANK],
                                               w_lo[:, DOWN0 + j, half * BANK:(half + 1) * BANK],
                                               j == 0, j == 1)
                        mm.then_inc(s.sum_full, 1)

            schedule(pe, idle, gate_product, idle, value_product, idle, down)


QP = 2


def diff_attention(nc, o_heads, qk, v_rows, lam_vecs, ident):
    KT = T // P
    chunks = token_chunks(T)
    units = [(u, 0) for u in range(XT)] + [(u, XT) for u in range(XT, TT)]
    NU = len(units)
    groups = [[list(range(a, min(a + 4, KT))) for a in range(k0, KT, 4)] for _, k0 in units]
    PAIRS = NU // QP
    fills_before = [sum(len(g) for g in groups[:u]) + u // QP for u in range(NU + 1)]
    FILLS = fills_before[NU]
    TURNS = FILLS - PAIRS

    def product_fill(h, pair):
        return h * FILLS + (pair // PAIRS * FILLS + fills_before[(pair % PAIRS + 1) * QP] - 1)

    with ExitStack() as ctx:
        def sb(label, shape, dt=F32):
            return ctx.enter_context(nc.sbuf_tensor(f"da_{label}", shape, dt))

        raw = sb("raw", [P, 2, T])
        q_top = sb("q_top", [P, T], F32R)
        q_st = sb("q_stacked", [P, 2, 2, T], F32R)
        k_hi = sb("k_hi", [P, 2, 2, T], F32R)
        k_lo = sb("k_lo", [P, 2, 2, T], F32R)
        v_hi = sb("v_hi", [P, 2, KT, P], F32R)
        v_lo = sb("v_lo", [P, 2, KT, P], F32R)
        e1 = sb("e1", [P, 2, T])
        e2 = sb("e2", [P, 2, T])
        pt_hi = sb("pt_hi", [P, 2, KT, QP * P], F32R)
        pt_lo = sb("pt_lo", [P, 2, KT, QP * P], F32R)
        o_t = sb("o", [P, 2, QP * P])
        lam_t = sb("lam", [P, 4, B_DIM])
        lam_prod = sb("lam_prod", [P, 2, B_DIM])
        lam_small = sb("lam_small", [P, 8])
        stats = sb("stats", [P, 2, 8])
        s_ps = ctx.enter_context(nc.psum_tensor("da_scores", [P, 2, 3 * BANK], F32))
        t_ps = ctx.enter_context(nc.psum_tensor("da_turned", [P, 2, BANK], F32))
        s = ctx.enter_context(stage(nc, "da", [
            "lam_in", "raw0_in", "raw1_in", "asked", "lam_step", "lam_exp", "lam_done", "raw_hi", "raw_split",
            "s1_full", "s2_full", "max1", "max2", "exp1", "exp2", "scale_step", "scale_done", "p_step", "p_done",
            "t_full", "t_hi", "t_lo", "o0_stored", "o1_stored", "o_free"],
            {"raw_split": 2, "exp1": 1, "exp2": 1, "max1": 2, "max2": 2, "p_done": 2, "t_full": FILLS + 1,
             "t_hi": 2, "t_lo": 2, "o_free": 2, "scale_done": 2, "p_step": 2,
             "s1_full": 1, "s2_full": 1}))
        raw_in = [s.raw0_in, s.raw1_in]
        o_stored = [s.o0_stored, s.o1_stored]
        block = ctx.enter_context(nc.Block())
        PIECES = 5

        def heads(eng, one_head):
            with eng.Fori(0, B_HEADS // 2) as i:
                for j in range(2):
                    one_head(i, j, i * 2 + j)

        @block.sync
        def _(sp):
            sp.dma_start(lam_t[:, :, :].rearrange("p a d -> p (a d)"), row(lam_vecs.rearrange("a d -> (a d)")))\
              .then_inc(s.lam_in.sem, 16)

            def one_head(i, j, h):
                for n in range(PIECES):
                    piece = h * PIECES + n
                    slot = (j * PIECES + n) % 2
                    sp.wait_ge(s.raw_split.sem, s.raw_split.nth(piece - 2))
                    sp.sem_inc(s.asked.sem, 1)
                    if n < 4:
                        first = i * (4 * B_DIM) + (j * 2 * B_DIM + (n // 2) * B_HEADS * 2 * B_DIM + n % 2 * B_DIM)
                        for half in range(2):
                            sp.dma_start(raw[half * B_DIM:(half + 1) * B_DIM, slot, :],
                                         qk[bass.ds(first, B_DIM), :]).then_inc(raw_in[slot].sem, 16)
                    else:
                        first = i * (2 * P) + j * P
                        sp.dma_start(raw[:, slot, :].rearrange("p (t n) -> p t n", n=P),
                                     v_rows.rearrange("(t p) n -> p t n", p=P)[:, :, bass.ds(first, P)])\
                          .then_inc(raw_in[slot].sem, 16)

            heads(sp, one_head)

        def loads_done(i, j, n):
            def dmas(k):
                slot = (j * PIECES + n) % 2
                return sum((1 if m % PIECES == 4 else 2) for m in range(k) if m % 2 == slot)
            return i * (16 * dmas(2 * PIECES)) + 16 * dmas(j * PIECES + n + 1)

        @block.scalar
        def _(act):
            start_ahead(act, s.exp1, s.exp2, s.t_hi)
            act.wait_ge(s.lam_step.sem, 2)
            act.activation(lam_small[:, 2:4], lam_small[:, 0:2], ACT.Exp).then_inc(s.lam_exp.sem, 1)

            def one_head(i, j, h):
                for n in range(PIECES):
                    slot = (j * PIECES + n) % 2
                    act.wait_ge(raw_in[slot].sem, loads_done(i, j, n))
                    act.wait_ge(s.t_full.sem, s.t_full.nth(product_fill(h, -PAIRS - 1)))
                    half = n % 2
                    if n < 2:
                        act.activation(q_st[0:B_DIM, j, half, :], raw[0:B_DIM, slot, :], ACT.Copy)
                        act.wait_ge(s.raw_split.sem, s.raw_split.nth(h * PIECES + n - 1))
                        act.activation(q_top[B_DIM:P, :], raw[B_DIM:P, slot, :], ACT.Copy).then_inc(s.raw_hi.sem, 1)
                    else:
                        dst = k_hi[:, j, half, :] if n < 4 else v_hi[:, j, :, :].rearrange("p t n -> p (t n)")
                        act.activation(dst, raw[:, slot, :], ACT.Copy).then_inc(s.raw_hi.sem, 1)
                for u in range(NU + 1):
                    if u < NU:
                        n = h * NU + u
                        first = units[u][1] * P
                        act.wait_ge(s.p_done.sem, s.p_done.nth(n - 2))
                        for e, sums, full, mx, done, half in ((e1, 2, s.s1_full, s.max1, s.exp1, 0),
                                                              (e2, 3, s.s2_full, s.max2, s.exp2, 1)):
                            act.wait_ge(mx.sem, mx.nth(n))
                            act.activation(e[:, u % 2, first:T], s_ps[:, half, first:T], ACT.Exp, scale=B_DIM ** -0.5,
                                           bias=stats[:, u % 2, half:half + 1],
                                           accum_out=stats[:, u % 2, sums:sums + 1]).then_inc(done.sem, 1)
                    if u >= 1:
                        turn_copies(i, j, h, u - 1)

            def turn_copies(i, j, h, u):
                pair = u // QP
                slot = (j * PAIRS + pair) % 2
                for f, group in enumerate(groups[u]):
                    n = fills_before[u] + f
                    act.wait_ge(s.t_full.sem, s.t_full.nth(h * FILLS + n))
                    if f == 0 and u % QP == 0:
                        act.wait_ge(s.t_full.sem, s.t_full.nth(product_fill(h, pair - 2)))
                    act.activation(pt_hi[:, slot, group[0]:group[-1] + 1, u % QP * P:(u % QP + 1) * P],
                                   t_ps[:, (j * FILLS + n) % 2, 0:len(group) * P]
                                   .rearrange("p (k n) -> p k n", n=P), ACT.Copy).then_inc(s.t_hi.sem, 1)

            heads(act, one_head)

        @block.vector
        def _(dve):
            start_ahead(dve, s.raw_split, s.max1, s.max2, s.scale_done, s.p_step, s.p_done, s.t_lo)
            dve.wait_ge(s.lam_in.sem, 16)
            for a in range(2):
                dve.tensor_tensor_reduce(lam_prod[:, a, :], lam_t[:, 2 * a, :], lam_t[:, 2 * a + 1, :], 1.0, 0.0,
                                         ALU.mult, ALU.add, lam_small[:, a:a + 1]).then_inc(s.lam_step.sem, 1)
            dve.wait_ge(s.lam_exp.sem, 1)
            dve.tensor_tensor(lam_small[:, 4:5], lam_small[:, 3:4], lam_small[:, 2:3], ALU.subtract)\
               .then_inc(s.lam_step.sem, 1)
            dve.wait_ge(s.lam_step.sem, 3)
            dve.tensor_scalar(lam_small[:, 5:6], lam_small[:, 4:5], -LAMBDA_INIT, None, ALU.add)\
               .then_inc(s.lam_done.sem, 1)
            dve.wait_ge(s.lam_done.sem, 1)

            def one_head(i, j, h):
                for n in range(PIECES):
                    slot = (j * PIECES + n) % 2
                    half = n % 2
                    dve.wait_ge(s.raw_hi.sem, s.raw_hi.nth(h * PIECES + n))
                    if n < 2:
                        ins = dve.tensor_tensor(q_st[B_DIM:P, j, half, :], raw[B_DIM:P, slot, :],
                                                q_top[B_DIM:P, :].bitcast(F32), ALU.subtract)
                    elif n < 4:
                        ins = dve.tensor_tensor(k_lo[:, j, half, :], raw[:, slot, :],
                                                k_hi[:, j, half, :].bitcast(F32), ALU.subtract)
                    else:
                        ins = dve.tensor_tensor(v_lo[:, j, :, :].rearrange("p t n -> p (t n)"), raw[:, slot, :],
                                                v_hi[:, j, :, :].rearrange("p t n -> p (t n)").bitcast(F32),
                                                ALU.subtract)
                    ins.then_inc(s.raw_split.sem, 1)
                for u in range(NU + 1):
                    if u < NU:
                        combine(h, u)
                    if u >= 1:
                        turn_halves(j, h, u - 1)

            def turn_halves(j, h, u):
                pair = u // QP
                slot = (j * PAIRS + pair) % 2
                cols = slice(u % QP * P, (u % QP + 1) * P)
                for f, group in enumerate(groups[u]):
                    n = fills_before[u] + f
                    dve.wait_ge(s.t_hi.sem, s.t_hi.nth(h * TURNS + (n - pair)))
                    dve.tensor_tensor(pt_lo[:, slot, group[0]:group[-1] + 1, cols],
                                      t_ps[:, (j * FILLS + n) % 2, 0:len(group) * P]
                                      .rearrange("p (k n) -> p k n", n=P),
                                      pt_hi[:, slot, group[0]:group[-1] + 1, cols].bitcast(F32),
                                      ALU.subtract).then_inc(s.t_lo.sem, 1)
                if u % QP == QP - 1:
                    n = fills_before[u + 1] - 1
                    dve.wait_ge(s.t_full.sem, s.t_full.nth(h * FILLS + n))
                    dve.wait_ge(s.o_free.sem, s.o_free.nth(h * PAIRS + (pair - 2)))
                    dve.tensor_copy(o_t[:, slot, :], t_ps[:, (j * FILLS + n) % 2, 0:QP * P])\
                       .then_inc(s.t_lo.sem, 1)

            def combine(h, u):
                n = h * NU + u
                first = units[u][1] * P
                st = stats[:, u % 2, :]
                for half, full, mx in ((0, s.s1_full, s.max1), (1, s.s2_full, s.max2)):
                    dve.wait_ge(full.sem, full.nth(n))
                    dve.wait_ge(s.p_done.sem, s.p_done.nth(n - 2))
                    dve.tensor_reduce(st[:, 4 + half:5 + half], s_ps[:, half, first:T], AX.X, ALU.max)\
                       .then_inc(s.scale_step.sem, 1)
                    dve.wait_ge(s.scale_step.sem, s.scale_step.nth(n * 4 + half))
                    dve.tensor_scalar(st[:, half:half + 1], st[:, 4 + half:5 + half], -(B_DIM ** -0.5), None,
                                      ALU.mult).then_inc(mx.sem, 1)
                dve.wait_ge(s.exp1.sem, s.exp1.nth(n))
                dve.wait_ge(s.exp2.sem, s.exp2.nth(n))
                dve.reciprocal(st[:, 6:8], st[:, 2:4]).then_inc(s.scale_step.sem, 1)
                dve.wait_ge(s.scale_step.sem, s.scale_step.nth(n * 4 + 2))
                dve.tensor_scalar(st[:, 7:8], st[:, 7:8], lam_small[:, 5:6], None, ALU.mult)\
                   .then_inc(s.scale_step.sem, 1)
                dve.wait_ge(s.scale_step.sem, s.scale_step.nth(n * 4 + 3))
                a, b = e1[:, u % 2, first:T], e2[:, u % 2, first:T]
                dve.tensor_scalar(b, b, st[:, 7:8], None, ALU.mult).then_inc(s.p_step.sem, 1)
                dve.wait_ge(s.p_step.sem, s.p_step.nth(n))
                dve.scalar_tensor_tensor(out=a, in0=a, scalar=st[:, 6:7], in1=b, op0=ALU.mult, op1=ALU.add)\
                   .then_inc(s.p_done.sem, 1)

            heads(dve, one_head)

        @block.gpsimd
        def _(pool):
            start_ahead(pool, s.o_free)

            def one_head(i, j, h):
                for pair in range(PAIRS):
                    slot = (j * PAIRS + pair) % 2
                    pool.wait_ge(s.t_lo.sem, s.t_lo.nth(product_fill(h, pair)))
                    pool.sem_inc(s.asked.sem, 1)
                    pool.dma_start(o_heads[bass.ds(i * (2 * P) + j * P, P), pair * QP * P:(pair + 1) * QP * P],
                                   o_t[:, slot, :]).then_inc(o_stored[slot].sem, 16)
                    if pair >= 1:
                        stored(i, j, pair - 1)
                stored(i, j, PAIRS - 1)

            def stored(i, j, pair):
                n = j * PAIRS + pair
                pool.wait_ge(o_stored[n % 2].sem, o_stored[n % 2].nth(i * PAIRS + n // 2))
                pool.sem_inc(s.o_free.sem, 1)

            heads(pool, one_head)

        @block.tensor
        def _(pe):
            start_ahead(pe, s.s1_full, s.s2_full, s.t_full)

            def one_head(i, j, h):
                pe.wait_ge(s.raw_split.sem, s.raw_split.nth(h * PIECES + PIECES - 1))
                for u in range(NU + 1):
                    if u < NU:
                        n = h * NU + u
                        for half, full, exp in ((0, s.s1_full, s.exp1), (1, s.s2_full, s.exp2)):
                            pe.wait_ge(exp.sem, exp.nth(n - 1))
                            q = q_st[:, j, half, u * P:(u + 1) * P]
                            for a, m in chunks:
                                if a + m <= units[u][1] * P:
                                    continue
                                pe.matmul(s_ps[:, half, a:a + m], q, k_hi[:, j, half, a:a + m], start=True, stop=False)
                                mm = pe.matmul(s_ps[:, half, a:a + m], q, k_lo[:, j, half, a:a + m],
                                               start=False, stop=True)
                            mm.then_inc(full.sem, 1)
                    if u >= 1:
                        turned(i, j, h, u - 1)

            def turned(i, j, h, u):
                pe.wait_ge(s.p_done.sem, s.p_done.nth(h * NU + u))
                for f, group in enumerate(groups[u]):
                    n = h * FILLS + fills_before[u] + f
                    bank = (j * FILLS + fills_before[u] + f) % 2
                    pe.wait_ge(s.t_lo.sem, s.t_lo.nth(n - 2))
                    for g, kt in enumerate(group):
                        mm = pe.transpose(t_ps[:, bank, g * P:(g + 1) * P], e1[:, u % 2, kt * P:(kt + 1) * P],
                                          ident[:, :])
                    mm.then_inc(s.t_full.sem, 1)
                if u % QP == QP - 1:
                    n = fills_before[u + 1] - 1
                    pe.wait_ge(s.t_lo.sem, s.t_lo.nth(h * FILLS + (n - 1)))
                    slot = (j * PAIRS + u // QP) % 2
                    keys = list(range(units[u][1], KT))
                    for kt in keys:
                        mm = exact_product(pe, t_ps[:, (j * FILLS + n) % 2, 0:QP * P], v_hi[:, j, kt, :],
                                           v_lo[:, j, kt, :], pt_hi[:, slot, kt, :], pt_lo[:, slot, kt, :],
                                           kt == keys[0], kt == keys[-1])
                    mm.then_inc(s.t_full.sem, 1)

            heads(pe, one_head)


def join_conv_diff(nc, y_hi, y_lo, conv_out, o_heads, ln_g, ln_b, subln):
    chunks = token_chunks(T)
    AT = A_WIDTH // P
    with ExitStack() as ctx:
        def sb(label, shape, dt=F32):
            return ctx.enter_context(nc.sbuf_tensor(f"join_{label}", shape, dt))

        u = sb("u", [P, 2, AT, BANK])
        o = sb("o", [P, 2, B_HEADS, BANK])
        u_sq = sb("u_sq", [P, 2, AT, BANK])
        o_sq = sb("o_sq", [P, 2, B_HEADS, BANK])
        std = sb("std", [P, 1 + B_HEADS, BANK])
        ones = sb("ones", [P, P])
        eps = sb("eps", [P, 2])
        gains = sb("gains", [P, 2 * AT + 1])
        ps = ctx.enter_context(nc.psum_tensor("join_ps", [P, 2 + B_HEADS, BANK], F32))
        s = ctx.enter_context(stage(nc, "join", [
            "small_in", "set", "subln_scaled", "u0_in", "u1_in", "o0_in", "o1_in", "sum_full", "centred", "u_squared",
            "o_squared", "var_full", "ms_full", "u_std", "o_std", "u_rstd", "o_rstd", "u_normed", "o_normed",
            "silu_done", "y_hi", "y_lo"]))
        u_in, o_in = [s.u0_in, s.u1_in], [s.o0_in, s.o1_in]
        block = ctx.enter_context(nc.Block())

        @block.sync
        def _(sp):
            sp.dma_start(gains[:, 0:AT], column(ln_g), allow_slow_non_contiguous=True).then_inc(s.small_in.sem, 16)
            sp.dma_start(gains[:, AT:2 * AT], column(ln_b), allow_slow_non_contiguous=True)\
              .then_inc(s.small_in.sem, 16)
            sp.dma_start(gains[:, 2 * AT:], column(subln)).then_inc(s.small_in.sem, 16)
            for c, (a, n) in enumerate(chunks):
                if c >= 2:
                    sp.wait_ge(s.y_lo.sem, 8 * (c - 1))
                sp.dma_start(u[:, c % 2, :, 0:n], conv_out.rearrange("(k p) n -> p k n", p=P)[:, :, a:a + n])\
                  .then_inc(u_in[c % 2].sem, 16)
                sp.dma_start(o[:, c % 2, :, 0:n], o_heads.rearrange("(k p) n -> p k n", p=P)[:, :, a:a + n])\
                  .then_inc(o_in[c % 2].sem, 16)

        @block.tensor
        def _(pe):
            pe.wait_ge(s.set.sem, 1)
            for c, (a, n) in enumerate(chunks):
                b = c % 2
                pe.wait_ge(u_in[b].sem, 16 * (c // 2 + 1))
                if c:
                    pe.wait_ge(s.centred.sem, AT * c)
                for k in range(AT):
                    mm = pe.matmul(ps[:, 0, 0:n], ones[:, :], u[:, b, k, 0:n], start=k == 0, stop=k == AT - 1)
                mm.then_inc(s.sum_full.sem, 1)
                for k in range(B_HEADS):
                    pe.wait_ge(s.o_squared.sem, B_HEADS * c + k + 1)
                    if c:
                        pe.wait_ge(s.o_std.sem, B_HEADS * (c - 1) + k + 1)
                    pe.matmul(ps[:, 2 + k, 0:n], ones[:, :], o_sq[:, b, k, 0:n], start=True, stop=True)\
                      .then_inc(s.ms_full.sem, 1)
                if c:
                    pe.wait_ge(s.u_std.sem, c)
                for k in range(AT):
                    pe.wait_ge(s.u_squared.sem, AT * c + k + 1)
                    mm = pe.matmul(ps[:, 1, 0:n], ones[:, :], u_sq[:, b, k, 0:n], start=k == 0, stop=k == AT - 1)
                mm.then_inc(s.var_full.sem, 1)

        @block.scalar
        def _(act):
            act.wait_ge(s.small_in.sem, 48)
            act.wait_ge(s.set.sem, 3)
            for c, (a, n) in enumerate(chunks):
                b = c % 2
                act.wait_ge(o_in[b].sem, 16 * (c // 2 + 1))
                if c >= 2:
                    act.wait_ge(s.y_lo.sem, 8 * (c - 1))
                for k in range(B_HEADS):
                    act.activation(o_sq[:, b, k, 0:n], o[:, b, k, 0:n], ACT.Square).then_inc(s.o_squared.sem, 1)
                for k in range(AT):
                    act.wait_ge(s.centred.sem, AT * c + k + 1)
                    act.activation(u_sq[:, b, k, 0:n], u[:, b, k, 0:n], ACT.Square).then_inc(s.u_squared.sem, 1)
                for k in range(B_HEADS):
                    act.wait_ge(s.ms_full.sem, B_HEADS * c + k + 1)
                    if c:
                        act.wait_ge(s.o_normed.sem, B_HEADS * (c - 1) + k + 1)
                    act.activation(std[:, 1 + k, 0:n], ps[:, 2 + k, 0:n], ACT.Sqrt, scale=1.0 / P,
                                   bias=eps[:, 1:2]).then_inc(s.o_std.sem, 1)
                act.wait_ge(s.var_full.sem, c + 1)
                if c:
                    act.wait_ge(s.u_normed.sem, AT * c)
                act.activation(std[:, 0, 0:n], ps[:, 1, 0:n], ACT.Sqrt, scale=1.0 / A_WIDTH, bias=eps[:, 0:1])\
                   .then_inc(s.u_std.sem, 1)
                for k in range(B_HEADS):
                    act.wait_ge(s.o_normed.sem, B_HEADS * c + k + 1)
                    act.activation(y_hi[:, AT + k, a:a + n], o[:, b, k, 0:n], ACT.Copy).then_inc(s.y_hi.sem, 1)
                for k in range(AT):
                    act.wait_ge(s.u_normed.sem, AT * c + k + 1)
                    act.activation(u_sq[:, b, k, 0:n], u[:, b, k, 0:n], ACT.Silu, scale=gains[:, k:k + 1],
                                   bias=gains[:, AT + k:AT + k + 1]).then_inc(s.silu_done.sem, 1)
                for k in range(AT):
                    act.wait_ge(s.silu_done.sem, AT * c + k + 1)
                    act.activation(y_hi[:, k, a:a + n], u_sq[:, b, k, 0:n], ACT.Copy).then_inc(s.y_hi.sem, 1)

        @block.vector
        def _(dve):
            dve.memset(ones[:, :], 1.0).then_inc(s.set.sem, 1)
            dve.memset(eps[:, 0:1], LN_EPS).then_inc(s.set.sem, 1)
            dve.memset(eps[:, 1:2], RMS_EPS).then_inc(s.set.sem, 1)
            dve.wait_ge(s.small_in.sem, 48)
            dve.tensor_scalar(gains[:, 2 * AT:], gains[:, 2 * AT:], 1.0 - LAMBDA_INIT, None, ALU.mult)\
               .then_inc(s.subln_scaled.sem, 1)
            dve.wait_ge(s.subln_scaled.sem, 1)
            for c, (a, n) in enumerate(chunks):
                b = c % 2
                dve.wait_ge(s.sum_full.sem, c + 1)
                for k in range(AT):
                    part = u[:, b, k, 0:n]
                    dve.scalar_tensor_tensor(out=part, in0=ps[:, 0, 0:n], scalar=-1.0 / A_WIDTH, in1=part,
                                             op0=ALU.mult, op1=ALU.add).then_inc(s.centred.sem, 1)
                for k in range(B_HEADS):
                    dve.wait_ge(s.o_std.sem, B_HEADS * c + k + 1)
                    dve.reciprocal(std[:, 1 + k, 0:n], std[:, 1 + k, 0:n]).then_inc(s.o_rstd.sem, 1)
                for k in range(B_HEADS):
                    dve.wait_ge(s.o_rstd.sem, B_HEADS * c + k + 1)
                    part = o[:, b, k, 0:n]
                    dve.scalar_tensor_tensor(out=part, in0=part, scalar=gains[:, 2 * AT:], in1=std[:, 1 + k, 0:n],
                                             op0=ALU.mult, op1=ALU.mult).then_inc(s.o_normed.sem, 1)
                dve.wait_ge(s.u_std.sem, c + 1)
                dve.reciprocal(std[:, 0, 0:n], std[:, 0, 0:n]).then_inc(s.u_rstd.sem, 1)
                dve.wait_ge(s.u_rstd.sem, c + 1)
                for k in range(AT):
                    part = u[:, b, k, 0:n]
                    dve.tensor_tensor(part, part, std[:, 0, 0:n], ALU.mult).then_inc(s.u_normed.sem, 1)
                for m in range(8):
                    dve.wait_ge(s.y_hi.sem, 8 * c + m + 1)
                    k, src = (AT + m, o) if m < B_HEADS else (m - B_HEADS, u_sq)
                    dve.tensor_tensor(y_lo[:, k, a:a + n], src[:, b, k % AT, 0:n],
                                      y_hi[:, k, a:a + n].bitcast(F32), ALU.subtract).then_inc(s.y_lo.sem, 1)


def project_out(nc, name, y_hi, y_lo, tokens, w_out, post, pre, x_old, x_new, ident):
    N = tokens // P
    with ExitStack() as ctx:
        def sb(label, shape, dt=F32):
            return ctx.enter_context(nc.sbuf_tensor(f"{name}_{label}", shape, dt))

        w_hi = sb("w_hi", [P, KD, D], F32R)
        w_lo = sb("w_lo", [P, KD, D], F32R)
        y = sb("y", [P, 2, D])
        ps = ctx.enter_context(nc.psum_tensor(f"{name}_ps", [P, 2, D], F32))
        s = ctx.enter_context(stage(nc, name, TokenTail.SIGNALS + [
            "w0_in", "w1_in", "w_hi_done", "w_ready", "y_full", "y_copied"]))
        w_in = [s.w0_in, s.w1_in]
        tail = TokenTail(nc, ctx, name, s, post, pre, 2 if tokens > SEQ else 1, N, ident)
        block = ctx.enter_context(nc.Block())

        @block.sync
        def _(sp):
            tail.load_rows(sp)
            for k in range(KD):
                if k >= 2:
                    sp.wait_ge(s.w_ready.sem, k - 1)
                sp.dma_start(y[:, k % 2, :], w_out[k * P:(k + 1) * P, :]).then_inc(w_in[k % 2].sem, 16)
            for t in range(2):
                tail.load_x(sp, t, x_old(t))
            for t in range(N):
                tail.store_x(sp, t, x_new(t))
                if t + 2 < N:
                    tail.load_x(sp, t + 2, x_old(t + 2))
            tail.stores_over(sp)

        @block.tensor
        def _(pe):
            for t in range(N + 2):
                if t < N:
                    if t >= 2:
                        pe.wait_ge(s.y_copied.sem, t - 1)
                    for half in range(2):
                        cols = slice(half * BANK, (half + 1) * BANK)
                        for k in range(KD):
                            if t == 0 and half == 0:
                                pe.wait_ge(s.w_ready.sem, k + 1)
                            rows = slice(t * P, (t + 1) * P)
                            mm = exact_product(pe, ps[:, t % 2, cols], y_hi[:, k, rows], y_lo[:, k, rows],
                                               w_hi[:, k, cols], w_lo[:, k, cols], k == 0, k == KD - 1)
                    mm.then_inc(s.y_full.sem, 1)
                if t >= 2:
                    tail.turn_tensor(pe, t - 2)

        @block.scalar
        def _(act):
            act.wait_ge(s.gs_done.sem, tail.kinds * 2)
            for k in range(KD):
                act.wait_ge(w_in[k % 2].sem, 16 * (k // 2 + 1))
                act.activation(w_hi[:, k, :], y[:, k % 2, :], ACT.Copy).then_inc(s.w_hi_done.sem, 1)
            act.wait_ge(s.w_ready.sem, KD)
            for t in range(N + 2):
                if t < N:
                    act.wait_ge(s.y_full.sem, t + 1)
                    if t >= 2:
                        act.wait_ge(s.x_new.sem, t - 1)
                    act.activation(y[:, t % 2, :], ps[:, t % 2, :], ACT.Copy).then_inc(s.y_copied.sem, 1)
                    act.wait_ge(s.y_copied.sem, t + 1)
                    tail.post_scalar(act, t, y[:, t % 2, :])
                if 1 <= t < N + 1:
                    tail.pre_scalar(act, t - 1)
                if t >= 2:
                    tail.split_scalar(act, t - 2, y_hi[:, :, (t - 2) * P:(t - 1) * P])

        @block.vector
        def _(dve):
            tail.prepare_rows(dve)
            for k in range(KD):
                dve.wait_ge(s.w_hi_done.sem, k + 1)
                dve.tensor_tensor(w_lo[:, k, :], y[:, k % 2, :], w_hi[:, k, :].bitcast(F32), ALU.subtract)\
                   .then_inc(s.w_ready.sem, 1)
            for t in range(N + 2):
                if t < N:
                    tail.post_vector(dve, t, t, y[:, t % 2, :])
                if 1 <= t < N + 1:
                    tail.pre_vector(dve, t - 1, t - 1)
                if t >= 2:
                    rows = slice((t - 2) * P, (t - 1) * P)
                    tail.split_vector(dve, t - 2, y_hi[:, :, rows], y_lo[:, :, rows])

        @block.gpsimd
        def _(pool):
            tail.prepare_gpsimd(pool)
            for t in range(N + 1):
                if t < N:
                    tail.post_gpsimd(pool, t)
                if t >= 1:
                    tail.pre_gpsimd(pool, t - 1)


def last_residual(nc, y_sum, post, x_old, out):
    with ExitStack() as ctx:
        s = ctx.enter_context(stage(nc, "last", TokenTail.SIGNALS))
        tail = TokenTail(nc, ctx, "last", s, post, None, 1, XT, None)
        block = ctx.enter_context(nc.Block())

        @block.sync
        def _(sp):
            tail.load_rows(sp)
            for t in range(2):
                tail.load_x(sp, t, x_old(t))
            for t in range(XT):
                tail.store_x(sp, t, out[t * P:(t + 1) * P, :])
                if t + 2 < XT:
                    tail.load_x(sp, t + 2, x_old(t + 2))
            tail.stores_over(sp)

        @block.scalar
        def _(act):
            for t in range(XT):
                tail.post_scalar(act, t, y_sum[:, t, :])

        @block.vector
        def _(dve):
            tail.prepare_rows(dve)
            for t in range(XT):
                tail.post_vector(dve, t, t, y_sum[:, t, :])

        @block.gpsimd
        def _(pool):
            tail.prepare_gpsimd(pool)
            for t in range(XT):
                tail.post_gpsimd(pool, t)


def project_latents(nc, y_sum, post, pre, x_old, x_new, w_in, q_gain, kv_gain, cq, ckv, k_pe, ident):
    N = TT
    splits = ((0, BANK), (BANK, C_Q_RANK - BANK), (C_Q_RANK, C_IN - C_Q_RANK))
    LATENTS = C_Q_RANK + C_KV_RANK
    LT = LATENTS // P
    QT = C_Q_RANK // P
    groups = ((0, 4), (4, LT), (LT, LT + 1))
    with ExitStack() as ctx:
        def sb(label, shape, dt=F32):
            return ctx.enter_context(nc.sbuf_tensor(f"lat_{label}", shape, dt))

        w_hi = sb("w_hi", [P, KD, C_IN], F32R)
        w_lo = sb("w_lo", [P, KD, C_IN], F32R)
        h_hi = sb("h_hi", [P, 2, KD, P], F32R)
        h_lo = sb("h_lo", [P, 2, KD, P], F32R)
        p_t = sb("p", [P, 2, C_IN])
        out_t = sb("out", [P, 2, LT + 1, P])
        squares = sb("squares", [P, LATENTS])
        gains = sb("gains", [P, LATENTS])
        small = sb("latent_norms", [P, 6, N])
        ps = ctx.enter_context(nc.psum_tensor("lat_ps", [P, 3, BANK], F32))
        out_ps = ctx.enter_context(nc.psum_tensor("lat_out_ps", [P, 3, BANK], F32))
        s = ctx.enter_context(stage(nc, "lat", TokenTail.SIGNALS + [
            "w0_in", "w1_in", "gains_in", "w_hi_done", "w_ready", "p_full", "p_copied", "p_squared", "ms_done", "p_rstd",
            "p_normed", "p_turned", "out_copied", "out0_stored", "out1_stored"]))
        w_in_sems = [s.w0_in, s.w1_in]
        out_stored = [s.out0_stored, s.out1_stored]
        tail = TokenTail(nc, ctx, "lat", s, post, pre, 2, N, ident)
        block = ctx.enter_context(nc.Block())

        def stores(t):
            return 16 * sum(3 if v < XT else 2 for v in range(t % 2, t + 1, 2))

        STEPS = N + 4

        @block.sync
        def _(sp):
            sp.dma_start(gains[:, 0:C_Q_RANK], row(q_gain)).then_inc(s.gains_in.sem, 16)
            sp.dma_start(gains[:, C_Q_RANK:], row(kv_gain)).then_inc(s.gains_in.sem, 16)
            tail.load_rows(sp)
            for t in range(2):
                tail.load_x(sp, t, x_old(t))
            for k in range(KD):
                if k >= 2:
                    sp.wait_ge(s.w_ready.sem, k - 1)
                sp.dma_start(p_t[:, k % 2, :], w_in[k * P:(k + 1) * P, :]).then_inc(w_in_sems[k % 2].sem, 16)
            for step in range(STEPS):
                if step < N:
                    tail.store_x(sp, step, x_new(step))
                if step + 2 < N:
                    tail.load_x(sp, step + 2, x_old(step + 2))
                if step >= 4:
                    t = step - 4
                    sp.wait_ge(s.out_copied.sem, 3 * t + 3)
                    cols = slice(t * P, (t + 1) * P)
                    if t < XT:
                        sp.dma_start(cq.rearrange("(k p) n -> p k n", p=P)[:, :, cols], out_t[:, t % 2, 0:QT, :])\
                          .then_inc(out_stored[t % 2].sem, 16)
                    sp.dma_start(ckv.rearrange("(k p) n -> p k n", p=P)[:, :, cols], out_t[:, t % 2, QT:LT, :])\
                      .then_inc(out_stored[t % 2].sem, 16)
                    sp.dma_start(k_pe[:, cols], out_t[0:C_ROPE, t % 2, LT, :]).then_inc(out_stored[t % 2].sem, 16)
            tail.stores_over(sp)
            for t in (N - 2, N - 1):
                sp.wait_ge(out_stored[t % 2].sem, stores(t))

        @block.tensor
        def _(pe):
            for step in range(STEPS):
                if 2 <= step < N + 2:
                    tail.turn_tensor(pe, step - 2)
                if 3 <= step < N + 3:
                    t = step - 3
                    pe.wait_ge(s.h_lo.sem, 2 * t + 2)
                    if t:
                        pe.wait_ge(s.p_copied.sem, t)
                    for b, (a, n) in enumerate(splits):
                        for k in range(KD):
                            if t == 0 and b == 0:
                                pe.wait_ge(s.w_ready.sem, k + 1)
                            mm = exact_product(pe, ps[:, b, 0:n], h_hi[:, t % 2, k, :], h_lo[:, t % 2, k, :],
                                               w_hi[:, k, a:a + n], w_lo[:, k, a:a + n], k == 0, k == KD - 1)
                    mm.then_inc(s.p_full.sem, 1)
                if step >= 4:
                    t = step - 4
                    pe.wait_ge(s.p_normed.sem, 2 * t + 2)
                    for b, (first, last) in enumerate(groups):
                        if t:
                            pe.wait_ge(s.out_copied.sem, 3 * (t - 1) + b + 1)
                        for k in range(first, last):
                            n = P if k < LT else C_ROPE
                            mm = pe.transpose(out_ps[0:n, b, (k - first) * P:(k - first + 1) * P],
                                              p_t[:, t % 2, k * P:k * P + n], ident[:, :])
                        mm.then_inc(s.p_turned.sem, 1)

        @block.scalar
        def _(act):
            act.wait_ge(s.gs_done.sem, 4)
            for k in range(KD):
                act.wait_ge(w_in_sems[k % 2].sem, 16 * (k // 2 + 1))
                act.activation(w_hi[:, k, :], p_t[:, k % 2, :], ACT.Copy).then_inc(s.w_hi_done.sem, 1)
            act.wait_ge(s.w_ready.sem, KD)
            for step in range(STEPS):
                if step < N:
                    tail.post_scalar(act, step, y_sum[:, step, :])
                if 1 <= step < N + 1:
                    tail.pre_scalar(act, step - 1)
                if 2 <= step < N + 2:
                    t = step - 2
                    if t >= 2:
                        act.wait_ge(s.p_full.sem, t - 1)
                    tail.split_scalar(act, t, h_hi[:, t % 2, :, :])
                if 3 <= step < N + 3:
                    t = step - 3
                    act.wait_ge(s.p_full.sem, t + 1)
                    if t >= 2:
                        act.wait_ge(s.p_turned.sem, 3 * (t - 1))
                    for b, (a, n) in enumerate(splits):
                        ins = act.activation(p_t[:, t % 2, a:a + n], ps[:, b, 0:n], ACT.Copy)
                    ins.then_inc(s.p_copied.sem, 1)
                    act.wait_ge(s.p_copied.sem, t + 1)
                    if t:
                        act.wait_ge(s.p_squared.sem, 2 * t)
                    for j, (a, b) in enumerate(((0, C_Q_RANK), (C_Q_RANK, LATENTS))):
                        act.activation(squares[:, a:b], p_t[:, t % 2, a:b], ACT.Square,
                                       accum_out=small[:, j, t:t + 1]).then_inc(s.p_squared.sem, 1)
                if step >= 4:
                    t = step - 4
                    if t >= 2:
                        act.wait_ge(out_stored[t % 2].sem, stores(t - 2))
                    for b, (first, last) in enumerate(groups):
                        act.wait_ge(s.p_turned.sem, 3 * t + b + 1)
                        n = C_ROPE if b == 2 else P
                        act.activation(out_t[0:n, t % 2, first:last, :],
                                       out_ps[0:n, b, 0:(last - first) * P].rearrange("p (k n) -> p k n", n=P),
                                       ACT.Copy).then_inc(s.out_copied.sem, 1)

        @block.vector
        def _(dve):
            tail.prepare_rows(dve)
            dve.wait_ge(s.gains_in.sem, 32)
            for k in range(KD):
                dve.wait_ge(s.w_hi_done.sem, k + 1)
                dve.tensor_tensor(w_lo[:, k, :], p_t[:, k % 2, :], w_hi[:, k, :].bitcast(F32), ALU.subtract)\
                   .then_inc(s.w_ready.sem, 1)
            for step in range(STEPS - 1):
                if step < N:
                    tail.post_vector(dve, step, step, y_sum[:, step, :])
                if 1 <= step < N + 1:
                    tail.pre_vector(dve, step - 1, step - 1)
                if 2 <= step < N + 2:
                    t = step - 2
                    tail.split_vector(dve, t, h_hi[:, t % 2, :, :], h_lo[:, t % 2, :, :])
                if 3 <= step < N + 3:
                    t = step - 3
                    for j, (a, b) in enumerate(((0, C_Q_RANK), (C_Q_RANK, LATENTS))):
                        dve.wait_ge(s.p_rstd.sem, 2 * t + j + 1)
                        part = p_t[:, t % 2, a:b]
                        dve.scalar_tensor_tensor(out=part, in0=part, scalar=small[:, 4 + j, t:t + 1],
                                                 in1=gains[:, a:b], op0=ALU.mult, op1=ALU.mult)\
                           .then_inc(s.p_normed.sem, 1)

        @block.gpsimd
        def _(pool):
            tail.prepare_gpsimd(pool)
            for step in range(STEPS - 1):
                if step < N:
                    tail.post_gpsimd(pool, step)
                if 1 <= step < N + 1:
                    tail.pre_gpsimd(pool, step - 1)
                if step >= 3:
                    t = step - 3
                    for j, rank in enumerate((C_Q_RANK, C_KV_RANK)):
                        ss, ms, rstd = (small[:, 2 * m + j, t:t + 1] for m in range(3))
                        pool.wait_ge(s.p_squared.sem, 2 * t + j + 1)
                        pool.tensor_scalar(ms, ss, 1.0 / rank, RMS_EPS, ALU.mult, ALU.add).then_inc(s.ms_done.sem, 1)
                        pool.wait_ge(s.ms_done.sem, 2 * t + j + 1)
                        pool.tensor_tensor(rstd, ms, tail.minus_half[:, :], ALU.pow).then_inc(s.p_rstd.sem, 1)


def mla(nc, o_parts, inv_sums, cq, ckv, k_pe, w_uq, w_ukv, cos, sin, turn, ident):
    KT = T // P
    CK = C_Q_RANK // P
    KK = C_KV_RANK // P
    HD = C_NOPE + C_ROPE
    NU = 2 * XT
    SCALE = HD ** -0.5
    k_chunks, q_chunks = token_chunks(T), token_chunks(SEQ)
    groups = [list(range(a, min(a + 4, KT))) for a in range(0, KT, 4)]
    G = len(groups)
    fills_before = [G * u + u // QP for u in range(NU + 1)]
    FILLS = fills_before[NU]
    TURNS = G * NU
    PAIRS = NU // QP

    def product_fill(i, pair):
        return i * FILLS + (pair // PAIRS * FILLS + fills_before[(pair % PAIRS + 1) * QP] - 1)

    def last_turned(i, u):
        return i * FILLS + (u // NU * FILLS + fills_before[u % NU] + G - 1)

    with ExitStack() as ctx:
        def sb(label, shape, dt=F32):
            return ctx.enter_context(nc.sbuf_tensor(f"mla_{label}", shape, dt))

        cq_hi, cq_lo = (sb(f"cq_{n}", [P, CK, SEQ], F32R) for n in ("hi", "lo"))
        ckv_hi, ckv_lo = (sb(f"ckv_{n}", [P, KK, T], F32R) for n in ("hi", "lo"))
        cos_t = sb("cos", [HD, SEQ])
        sin_t = sb("sin", [HD, SEQ])
        wq = sb("wq", [P, CK, 2 * HD])
        wkv = sb("wkv", [P, KK, 4 * C_V])
        wq_hi, wq_lo = (sb(f"wq_{n}", [P, CK, 2 * HD], F32R) for n in ("hi", "lo"))
        wkv_hi, wkv_lo = (sb(f"wkv_{n}", [P, KK, 4 * C_V], F32R) for n in ("hi", "lo"))
        q_t = sb("q", [HD, SEQ])
        sin_part = sb("sin_part", [HD, SEQ])
        q_hi, q_lo = (sb(f"q_{n}", [HD, 2, SEQ], F32R) for n in ("hi", "lo"))
        k_hi, k_lo = (sb(f"k_{n}", [HD, 2, T], F32R) for n in ("hi", "lo"))
        v_st = sb("v_stacked", [P, 2, KT, 2 * C_V], F32R)
        e = sb("e", [P, 2, T])
        pt_hi, pt_lo = (sb(f"pt_{n}", [P, 2, KT, QP * P], F32R) for n in ("hi", "lo"))
        o_t = sb("o", [P, 2, QP * P])
        neg_max = sb("neg_max", [P, 2])
        sums = sb("sums", [P, C_HEADS * XT])
        s_ps = ctx.enter_context(nc.psum_tensor("mla_scores", [P, 2, 3 * BANK], F32))
        t_ps = ctx.enter_context(nc.psum_tensor("mla_turned", [P, 2, BANK], F32))
        s = ctx.enter_context(stage(nc, "mla", [
            "tables_in", "raw0_in", "raw1_in", "raw_hi", "raw_split", "zeroed", "pe_turned", "pe_step", "pe_hi", "pe_lo",
            "asked", "w_in", "w_hi_done", "w_split", "q_full", "q_copied", "q_turned", "q_step", "q_sum", "q_hi",
            "q_lo", "k_full", "k_hi", "k_lo", "v_full", "v_hi", "v_lo", "s_full", "max", "exp", "t_full", "t_hi",
            "t_lo", "o0_stored", "o1_stored", "o_free", "inverted", "inv_turned", "inv_copied", "inv_stored"],
            {"w_split": 1, "v_full": 1, "q_step": 3, "q_lo": 1, "q_hi": 1, "v_lo": 1, "exp": 2, "s_full": 0,
             "t_full": 8, "t_lo": 2, "o_free": 2, "k_lo": 1}))
        s.w_in.step = 32
        raw_in, o_stored = [s.raw0_in, s.raw1_in], [s.o0_stored, s.o1_stored]
        block = ctx.enter_context(nc.Block())
        PIECES = CK + KK + 1

        @block.sync
        def _(sp):
            sp.dma_start(cos_t[:, :], cos[0:HD, :]).then_inc(s.tables_in.sem, 16)
            sp.dma_start(sin_t[:, :], sin[0:HD, :]).then_inc(s.tables_in.sem, 16)
            for n in range(PIECES):
                if n >= 2:
                    sp.wait_ge(s.raw_split.sem, n - 1)
                if n < CK:
                    src, dst = cq[n * P:(n + 1) * P, :], e[:, n % 2, 0:SEQ]
                elif n < CK + KK:
                    src, dst = ckv[(n - CK) * P:(n - CK + 1) * P, :], e[:, n % 2, :]
                else:
                    src, dst = k_pe, e[C_NOPE:HD, n % 2, :]
                sp.dma_start(dst, src).then_inc(raw_in[n % 2].sem, 16)
            with sp.Fori(0, C_HEADS // 2) as i:
                sp.wait_ge(s.w_split.sem, s.w_split.nth(i - 1))
                sp.sem_inc(s.asked.sem, 1)
                sp.dma_start(wq[:, :, :], w_uq.rearrange("(k p) n -> p k n", p=P)[:, :, bass.ds(i * (2 * HD), 2 * HD)])\
                  .then_inc(s.w_in.sem, 16)
                sp.dma_start(wkv[:, :, :],
                             w_ukv.rearrange("(k p) n -> p k n", p=P)[:, :, bass.ds(i * (4 * C_V), 4 * C_V)])\
                  .then_inc(s.w_in.sem, 16)
            sp.wait_ge(s.inv_copied.sem, 1)
            sp.dma_start(inv_sums, e[:, 0, 0:P]).then_inc(s.inv_stored.sem, 16)
            sp.wait_ge(s.inv_stored.sem, 16)

        def projections(pe, i):
            def q_product(j):
                for c, (a, n) in enumerate(q_chunks):
                    for k in range(CK):
                        cols = slice(j * HD, (j + 1) * HD)
                        mm = exact_product(pe, s_ps[0:HD, j, a:a + n], wq_hi[:, k, cols], wq_lo[:, k, cols],
                                           cq_hi[:, k, a:a + n], cq_lo[:, k, a:a + n], k == 0, k == CK - 1)
                mm.then_inc(s.q_full.sem, 1)

            def k_product(j):
                for c, (a, n) in enumerate(k_chunks):
                    for k in range(KK):
                        cols = slice(j * 2 * C_V, j * 2 * C_V + C_NOPE)
                        mm = exact_product(pe, s_ps[0:C_NOPE, 1 - j, a:a + n], wkv_hi[:, k, cols],
                                           wkv_lo[:, k, cols], ckv_hi[:, k, a:a + n], ckv_lo[:, k, a:a + n],
                                           k == 0, k == KK - 1)
                mm.then_inc(s.k_full.sem, 1)

            def q_turn(j):
                pe.wait_ge(s.q_copied.sem, s.q_copied.nth(i * 2 + j))
                for c, (a, n) in enumerate(q_chunks):
                    mm = pe.matmul(s_ps[0:HD, j, a:a + n], turn[0:HD, 0:HD], q_t[:, a:a + n], start=True, stop=True)
                mm.then_inc(s.q_turned.sem, 1)

            pe.wait_ge(s.w_split.sem, s.w_split.nth(i))
            pe.wait_ge(s.exp.sem, s.exp.nth(i * NU - 2))
            q_product(0)
            pe.wait_ge(s.exp.sem, s.exp.nth(i * NU - 1))
            k_product(0)
            q_turn(0)
            pe.wait_ge(s.k_lo.sem, s.k_lo.nth(i * 2))
            q_product(1)
            pe.wait_ge(s.q_step.sem, s.q_step.nth(i * 4))
            k_product(1)
            q_turn(1)
            pe.wait_ge(s.k_lo.sem, s.k_lo.nth(i * 2 + 1))
            for kt in range(KT):
                rows = slice(kt * P, (kt + 1) * P)
                for k in range(KK):
                    v_cols = [w[:, k, :].rearrange("p (h two d) -> p h two d", two=2, d=C_V)[:, :, 1, :]
                              for w in (wkv_hi, wkv_lo)]
                    mm = exact_product(pe, s_ps[:, 0, rows].rearrange("p (h d) -> p h d", d=C_V),
                                       ckv_hi[:, k, rows], ckv_lo[:, k, rows],
                                       v_cols[0], v_cols[1], k == 0, k == KK - 1)
            mm.then_inc(s.v_full.sem, 1)

        def scores(pe, i, u):
            j, qt = u // XT, u % XT
            if u == 0:
                pe.wait_ge(s.v_lo.sem, s.v_lo.nth(i))
            elif u == 1:
                pe.wait_ge(s.q_step.sem, s.q_step.nth(i * 4 + 2))
            else:
                pe.wait_ge(s.exp.sem, s.exp.nth(i * NU + (u - 2)))
            if qt == 0:
                pe.wait_ge(s.q_lo.sem, s.q_lo.nth(i * 2 + j))
            q = slice(qt * P, (qt + 1) * P)
            for a, n in k_chunks:
                mm = exact_product(pe, s_ps[:, u % 2, a:a + n], q_hi[:, j, q], q_lo[:, j, q],
                                   k_hi[:, j, a:a + n], k_lo[:, j, a:a + n], True, True)
            mm.then_inc(s.s_full.sem, 1)

        def turned(pe, i, u):
            pe.wait_ge(s.exp.sem, s.exp.nth(i * NU + u))
            for f, group in enumerate(groups):
                n = fills_before[u] + f
                pe.wait_ge(s.t_lo.sem, s.t_lo.nth(i * FILLS + (n - 2)))
                for g, kt in enumerate(group):
                    mm = pe.transpose(t_ps[:, n % 2, g * P:(g + 1) * P], e[:, u % 2, kt * P:(kt + 1) * P],
                                      ident[:, :])
                mm.then_inc(s.t_full.sem, 1)
            if u % QP == QP - 1:
                n = fills_before[u + 1] - 1
                slot = u // QP % 2
                pe.wait_ge(s.t_lo.sem, s.t_lo.nth(i * FILLS + (n - 1)))
                for kt in range(KT):
                    for pt in (pt_hi, pt_lo):
                        mm = pe.matmul(t_ps[:, n % 2, 0:QP * P], v_st[:, u // XT, kt, :], pt[:, slot, kt, :],
                                       start=kt == 0 and pt is pt_hi, stop=kt == KT - 1 and pt is pt_lo)
                mm.then_inc(s.t_full.sem, 1)

        @block.tensor
        def _(pe):
            start_ahead(pe, s.v_full, s.t_full)
            pe.wait_ge(s.zeroed.sem, 1)
            pe.wait_ge(raw_in[0].sem, 16 * (PIECES // 2 + 1))
            for c, (a, n) in enumerate(q_chunks):
                mm = pe.matmul(s_ps[0:HD, 0, a:a + n], turn[0:HD, 0:HD], e[0:HD, 0, a:a + n], start=True, stop=True)
            mm.then_inc(s.pe_turned.sem, 1)
            pe.wait_ge(s.pe_lo.sem, 2)
            with pe.Fori(0, C_HEADS // 2) as i:
                projections(pe, i)
                for u in range(NU + 1):
                    if u < NU:
                        scores(pe, i, u)
                    if u >= 1:
                        turned(pe, i, u - 1)
            pe.wait_ge(s.inverted.sem, 1)
            pe.wait_ge(s.t_lo.sem, s.t_lo.nth(FILLS * (C_HEADS // 2) - 1))
            pe.transpose(t_ps[:, 0, 0:P], sums[:, :], ident[:, :]).then_inc(s.inv_turned.sem, 1)

        def turn_copies(act, i, u):
            for f, group in enumerate(groups):
                n = fills_before[u] + f
                act.wait_ge(s.t_full.sem, s.t_full.nth(i * FILLS + n))
                if f == 0 and u % QP == 0:
                    act.wait_ge(s.t_full.sem, s.t_full.nth(product_fill(i, u // QP - 2)))
                act.activation(pt_hi[:, u // QP % 2, group[0]:group[-1] + 1, u % QP * P:(u % QP + 1) * P],
                               t_ps[:, n % 2, 0:len(group) * P].rearrange("p (k n) -> p k n", n=P), ACT.Copy)\
                   .then_inc(s.t_hi.sem, 1)

        @block.scalar
        def _(act):
            start_ahead(act, s.exp, s.q_hi)
            for n in range(CK + KK):
                act.wait_ge(raw_in[n % 2].sem, 16 * (n // 2 + 1))
                dst, src = (cq_hi[:, n, :], e[:, n % 2, 0:SEQ]) if n < CK else (ckv_hi[:, n - CK, :], e[:, n % 2, :])
                act.activation(dst, src, ACT.Copy).then_inc(s.raw_hi.sem, 1)
            act.wait_ge(s.pe_step.sem, 3)
            for j in range(2):
                act.activation(k_hi[C_NOPE:HD, j, :], e[C_NOPE:HD, 0, :], ACT.Copy).then_inc(s.pe_hi.sem, 1)
            act.wait_ge(s.pe_lo.sem, 2)

            def q_copy(i, j):
                act.wait_ge(s.q_full.sem, s.q_full.nth(i * 2 + j))
                act.wait_ge(s.q_lo.sem, s.q_lo.nth(i * 2 + j - 1))
                act.activation(q_t[:, :], s_ps[0:HD, j, 0:SEQ], ACT.Copy, scale=SCALE).then_inc(s.q_copied.sem, 1)

            def k_half(i, j):
                act.wait_ge(s.k_full.sem, s.k_full.nth(i * 2 + j))
                act.activation(k_hi[0:C_NOPE, j, :], s_ps[0:C_NOPE, 1 - j, 0:T], ACT.Copy).then_inc(s.k_hi.sem, 1)

            def q_half(i, j):
                act.wait_ge(s.q_sum.sem, s.q_sum.nth(i * 2 + j))
                act.activation(q_hi[:, j, :], q_t[:, :], ACT.Copy).then_inc(s.q_hi.sem, 1)

            with act.Fori(0, C_HEADS // 2) as i:
                act.wait_ge(s.w_in.sem, s.w_in.nth(i))
                act.wait_ge(s.v_full.sem, s.v_full.nth(i - 1))
                act.activation(wq_hi[:, :, :], wq[:, :, :], ACT.Copy)
                act.activation(wkv_hi[:, :, :], wkv[:, :, :], ACT.Copy).then_inc(s.w_hi_done.sem, 1)
                act.wait_ge(s.t_full.sem, s.t_full.nth(i * FILLS - 1))
                q_copy(i, 0)
                k_half(i, 0)
                q_half(i, 0)
                k_half(i, 1)
                q_copy(i, 1)
                q_half(i, 1)
                act.wait_ge(s.v_full.sem, s.v_full.nth(i))
                for j in range(2):
                    act.activation(v_st[:, j, :, 0:C_V],
                                   s_ps[:, 0, 0:T].rearrange("p (k h d) -> p k h d", h=2, d=C_V)[:, :, j, :],
                                   ACT.Copy).then_inc(s.v_hi.sem, 1)
                for u in range(NU + 1):
                    if u < NU:
                        act.wait_ge(s.max.sem, s.max.nth(i * NU + u))
                        act.wait_ge(s.t_full.sem, s.t_full.nth(last_turned(i, u - 2)))
                        act.activation(e[:, u % 2, :], s_ps[:, u % 2, 0:T], ACT.Exp, bias=neg_max[:, u % 2:u % 2 + 1],
                                       accum_out=sums[:, bass.ds(i * NU + u, 1)]).then_inc(s.exp.sem, 1)
                    if u >= 1:
                        turn_copies(act, i, u - 1)
            act.wait_ge(s.inv_turned.sem, 1)
            act.activation(e[:, 0, 0:P], t_ps[:, 0, 0:P], ACT.Copy).then_inc(s.inv_copied.sem, 1)

        def turn_halves(dve, i, u):
            slot = u // QP % 2
            cols = slice(u % QP * P, (u % QP + 1) * P)
            for f, group in enumerate(groups):
                n = fills_before[u] + f
                dve.wait_ge(s.t_hi.sem, s.t_hi.nth(i * TURNS + (u * G + f)))
                dve.tensor_tensor(pt_lo[:, slot, group[0]:group[-1] + 1, cols],
                                  t_ps[:, n % 2, 0:len(group) * P].rearrange("p (k n) -> p k n", n=P),
                                  pt_hi[:, slot, group[0]:group[-1] + 1, cols].bitcast(F32), ALU.subtract)\
                   .then_inc(s.t_lo.sem, 1)
            if u % QP == QP - 1:
                n = fills_before[u + 1] - 1
                dve.wait_ge(s.t_full.sem, s.t_full.nth(i * FILLS + n))
                dve.wait_ge(s.o_free.sem, s.o_free.nth(i * PAIRS + (u // QP - 2)))
                dve.tensor_copy(o_t[:, slot, :], t_ps[:, n % 2, 0:QP * P]).then_inc(s.t_lo.sem, 1)

        @block.vector
        def _(dve):
            start_ahead(dve, s.w_split, s.q_step, s.q_lo, s.v_lo, s.t_lo, s.k_lo)
            for n in range(CK + KK):
                dve.wait_ge(s.raw_hi.sem, n + 1)
                if n < CK:
                    dst, src, hi = cq_lo[:, n, :], e[:, n % 2, 0:SEQ], cq_hi[:, n, :]
                else:
                    dst, src, hi = ckv_lo[:, n - CK, :], e[:, n % 2, :], ckv_hi[:, n - CK, :]
                dve.tensor_tensor(dst, src, hi.bitcast(F32), ALU.subtract).then_inc(s.raw_split.sem, 1)
            dve.wait_ge(s.raw_split.sem, CK + KK)
            dve.memset(e[0:C_NOPE, 0, 0:SEQ], 0.0).then_inc(s.zeroed.sem, 1)
            dve.wait_ge(s.tables_in.sem, 32)
            dve.wait_ge(s.pe_turned.sem, 1)
            pe_rows = slice(C_NOPE, HD)
            dve.tensor_tensor(sin_part[pe_rows, :], s_ps[pe_rows, 0, 0:SEQ], sin_t[pe_rows, :], ALU.mult)\
               .then_inc(s.pe_step.sem, 1)
            dve.tensor_tensor(e[pe_rows, 0, 0:SEQ], e[pe_rows, 0, 0:SEQ], cos_t[pe_rows, :], ALU.mult)\
               .then_inc(s.pe_step.sem, 1)
            dve.wait_ge(s.pe_step.sem, 2)
            dve.tensor_tensor(e[pe_rows, 0, 0:SEQ], e[pe_rows, 0, 0:SEQ], sin_part[pe_rows, :], ALU.add)\
               .then_inc(s.pe_step.sem, 1)
            for j in range(2):
                dve.wait_ge(s.pe_hi.sem, j + 1)
                dve.tensor_tensor(k_lo[pe_rows, j, :], e[pe_rows, 0, :], k_hi[pe_rows, j, :].bitcast(F32),
                                  ALU.subtract).then_inc(s.pe_lo.sem, 1)

            def k_half(i, j):
                dve.wait_ge(s.k_hi.sem, s.k_hi.nth(i * 2 + j))
                dve.tensor_tensor(k_lo[0:C_NOPE, j, :], s_ps[0:C_NOPE, 1 - j, 0:T],
                                  k_hi[0:C_NOPE, j, :].bitcast(F32), ALU.subtract).then_inc(s.k_lo.sem, 1)

            def q_rotation(i, j):
                dve.wait_ge(s.q_turned.sem, s.q_turned.nth(i * 2 + j))
                if j == 0:
                    dve.wait_ge(s.q_hi.sem, s.q_hi.nth(i * 2 - 1))
                dve.tensor_tensor(sin_part[:, :], s_ps[0:HD, j, 0:SEQ], sin_t[:, :], ALU.mult)\
                   .then_inc(s.q_step.sem, 1)
                dve.tensor_tensor(q_t[:, :], q_t[:, :], cos_t[:, :], ALU.mult).then_inc(s.q_step.sem, 1)
                dve.wait_ge(s.q_step.sem, s.q_step.nth(i * 4 + (2 * j + 1)))
                dve.tensor_tensor(q_t[:, :], q_t[:, :], sin_part[:, :], ALU.add).then_inc(s.q_sum.sem, 1)

            def q_half(i, j):
                dve.wait_ge(s.q_hi.sem, s.q_hi.nth(i * 2 + j))
                dve.tensor_tensor(q_lo[:, j, :], q_t[:, :], q_hi[:, j, :].bitcast(F32), ALU.subtract)\
                   .then_inc(s.q_lo.sem, 1)

            with dve.Fori(0, C_HEADS // 2) as i:
                dve.wait_ge(s.w_hi_done.sem, s.w_hi_done.nth(i))
                dve.tensor_tensor(wq_lo[:, :, :], wq[:, :, :], wq_hi[:, :, :].bitcast(F32), ALU.subtract)
                dve.tensor_tensor(wkv_lo[:, :, :], wkv[:, :, :], wkv_hi[:, :, :].bitcast(F32), ALU.subtract)\
                   .then_inc(s.w_split.sem, 1)
                k_half(i, 0)
                q_rotation(i, 0)
                q_half(i, 0)
                k_half(i, 1)
                q_rotation(i, 1)
                q_half(i, 1)
                dve.wait_ge(s.v_hi.sem, s.v_hi.nth(i * 2 + 1))
                for j in range(2):
                    ins = dve.tensor_tensor(v_st[:, j, :, C_V:2 * C_V],
                                            s_ps[:, 0, 0:T].rearrange("p (k h d) -> p k h d", h=2, d=C_V)[:, :, j, :],
                                            v_st[:, j, :, 0:C_V].bitcast(F32), ALU.subtract)
                ins.then_inc(s.v_lo.sem, 1)
                for u in range(NU + 1):
                    if u < NU:
                        dve.wait_ge(s.s_full.sem, s.s_full.nth(i * NU + u))
                        dve.wait_ge(s.exp.sem, s.exp.nth(i * NU + (u - 2)))
                        dve.tensor_reduce(neg_max[:, u % 2:u % 2 + 1], s_ps[:, u % 2, 0:T], AX.X, ALU.max,
                                          negate=True).then_inc(s.max.sem, 1)
                    if u >= 1:
                        turn_halves(dve, i, u - 1)
            dve.wait_ge(s.exp.sem, s.exp.nth(C_HEADS * XT - 1))
            dve.reciprocal(sums[:, :], sums[:, :]).then_inc(s.inverted.sem, 1)

        @block.gpsimd
        def _(pool):
            start_ahead(pool, s.o_free)
            with pool.Fori(0, C_HEADS // 2) as i:
                def stored(pair):
                    pool.wait_ge(o_stored[pair % 2].sem, o_stored[pair % 2].nth(i * (PAIRS // 2) + pair // 2))
                    pool.sem_inc(s.o_free.sem, 1)

                for pair in range(PAIRS):
                    j, first = pair // (PAIRS // 2), pair % (PAIRS // 2) * QP * P
                    pool.wait_ge(s.t_lo.sem, s.t_lo.nth(product_fill(i, pair)))
                    pool.sem_inc(s.asked.sem, 1)
                    pool.dma_start(o_parts[bass.ds(i * (2 * P) + j * P, P), first:first + QP * P],
                                   o_t[:, pair % 2, :]).then_inc(o_stored[pair % 2].sem, 16)
                    if pair >= 1:
                        stored(pair - 1)
                stored(PAIRS - 1)


def join_heads(nc, y_hi, y_lo, o_parts, inv_sums):
    with ExitStack() as ctx:
        def sb(label, shape, dt=F32):
            return ctx.enter_context(nc.sbuf_tensor(f"heads_{label}", shape, dt))

        a = sb("a", [P, 2, SEQ])
        b = sb("b", [P, 2, SEQ])
        r = sb("r", [P, 2, SEQ])
        s = ctx.enter_context(stage(nc, "heads", ["p0_in", "p1_in", "added", "scaled", "y_hi", "y_lo"]))
        p_in = [s.p0_in, s.p1_in]
        block = ctx.enter_context(nc.Block())
        LOADS = 6

        @block.sync
        def _(sp):
            for k in range(KD):
                if k >= 2:
                    sp.wait_ge(s.y_lo.sem, k - 1)
                for j in range(2):
                    h, rows = 2 * k + j, slice(j * C_V, (j + 1) * C_V)
                    for part, dst in enumerate((a, b)):
                        first = h * P + part * C_V
                        sp.dma_start(dst[rows, k % 2, :], o_parts[first:first + C_V, :]).then_inc(p_in[k % 2].sem, 16)
                    sp.dma_start(r[rows, k % 2, :], row(inv_sums[h * XT:(h + 1) * XT, :]
                                                        .rearrange("t q -> (t q)"), C_V)).then_inc(p_in[k % 2].sem, 16)

        @block.scalar
        def _(act):
            for k in range(KD):
                act.wait_ge(s.scaled.sem, k + 1)
                act.activation(y_hi[:, k, :], a[:, k % 2, :], ACT.Copy).then_inc(s.y_hi.sem, 1)

        @block.vector
        def _(dve):
            for k in range(KD):
                m = k % 2
                dve.wait_ge(p_in[m].sem, 16 * LOADS * (k // 2 + 1))
                dve.tensor_tensor(a[:, m, :], a[:, m, :], b[:, m, :], ALU.add).then_inc(s.added.sem, 1)
                dve.wait_ge(s.added.sem, k + 1)
                dve.tensor_tensor(a[:, m, :], a[:, m, :], r[:, m, :], ALU.mult).then_inc(s.scaled.sem, 1)
                dve.wait_ge(s.y_hi.sem, k + 1)
                dve.tensor_tensor(y_lo[:, k, :], a[:, m, :], y_hi[:, k, :].bitcast(F32), ALU.subtract)\
                   .then_inc(s.y_lo.sem, 1)


INPUTS = ["x", "c", "ctx", "c_ctx", "ada_w", "ada_b", "norm_mix_pre", "norm_mix_post", "norm_ffn_pre",
          "norm_ffn_post", "ffn_w_up", "ffn_conv_w", "ffn_conv_b", "ffn_w_down", "ab_w_in", "a_conv_w",
          "a_conv_b", "a_ln_g", "a_ln_b", "b_lambda", "b_subln", "ab_w_out", "c_w_in", "c_q_norm",
          "c_kv_norm", "c_w_uq", "c_w_ukv", "c_w_out"]


def trunk(nc, i, consts, ropes, out, upto=99):
    def scratch(label, *shape):
        return nc.dram_tensor(f"scratch_{label}", list(shape), F32, kind="Internal").ap()

    mod = scratch("mod", 2, 2 * 6 * D)
    conv_out = scratch("conv", A_WIDTH, T)
    qk = scratch("qk", 4 * B_HEADS * B_DIM, T)
    v_rows = scratch("v", T, A_WIDTH)

    def mods(layer, part, kinds=2):
        first = (layer * 6 + part) * D
        return [mod[r, first:first + D] for r in range(kinds)]

    x = i.x[0]
    ctx_rows = i.ctx[0]
    with ExitStack() as ctx:
        def sb(label, shape, dt=F32):
            return ctx.enter_context(nc.sbuf_tensor(label, shape, dt))

        ident, turn_a, turn_c = (sb(n, [P, P]) for n in ("ident", "turn_a", "turn_c"))
        load_constants(nc, consts, ident, turn_a, turn_c)
        modulation(nc, mod, i.c[0], i.c_ctx, i.ada_w, i.ada_b)
        if upto < 2: return
        with ExitStack() as layer0:
            h_hi = layer0.enter_context(nc.sbuf_tensor("h_hi0", [P, KD, T], F32R))
            h_lo = layer0.enter_context(nc.sbuf_tensor("h_lo0", [P, KD, T], F32R))
            first_norm(nc, h_hi, h_lo, x, ctx_rows,
                       (mods(0, MIX_SCALE), mods(0, MIX_SHIFT), i.norm_mix_pre[0]), ident)
            if upto < 3: return
            project_conv_diff(nc, h_hi, h_lo, conv_out, qk, v_rows, i.ab_w_in[0], i.a_conv_w[0], i.a_conv_b[0],
                              ropes[0], ropes[1], turn_a)
            if upto < 4: return
        o_heads = scratch("o_heads", A_WIDTH, T)
        diff_attention(nc, o_heads, qk, v_rows, i.b_lambda[0], ident)
        if upto < 5: return

        def old_rows(t):
            return x[t * P:(t + 1) * P, :] if t < XT else ctx_rows[(t - XT) * P:(t - XT + 1) * P, :]

        x1, x2, x3 = (scratch(n, T, D) for n in ("x1", "x2", "x3"))

        def tile_of(rows):
            return lambda t: rows[t * P:(t + 1) * P, :]

        with ExitStack() as layer0:
            y_hi = layer0.enter_context(nc.sbuf_tensor("y_hi0", [P, KD, T], F32R))
            y_lo = layer0.enter_context(nc.sbuf_tensor("y_lo0", [P, KD, T], F32R))
            join_conv_diff(nc, y_hi, y_lo, conv_out, o_heads, i.a_ln_g[0], i.a_ln_b[0], i.b_subln[0])
            project_out(nc, "out0", y_hi, y_lo, T, i.ab_w_out[0], (mods(0, MIX_GATE), i.norm_mix_post[0]),
                        (mods(0, FFN_SCALE), mods(0, FFN_SHIFT), i.norm_ffn_pre[0]), old_rows, tile_of(x1), ident)
            if upto < 6: return
            with nc.sbuf_tensor("y_sum0", [P, TT, D], F32, side="right") as y_sum:
                ffn(nc, "ffn0", T, y_hi, y_lo, y_sum, i.ffn_w_up[0], i.ffn_conv_w[0], i.ffn_conv_b[0],
                    i.ffn_w_down[0])
                layer0.close()
                if upto < 7: return
                cq, ckv, k_pe = scratch("cq", C_Q_RANK, SEQ), scratch("ckv", C_KV_RANK, T), scratch("k_pe", C_ROPE, T)
                project_latents(nc, y_sum, (mods(0, FFN_GATE), i.norm_ffn_post[0]),
                                (mods(1, MIX_SCALE), mods(1, MIX_SHIFT), i.norm_mix_pre[1]), tile_of(x1),
                                tile_of(x2), i.c_w_in[0], i.c_q_norm[0], i.c_kv_norm[0], cq, ckv, k_pe, ident)
        if upto < 8: return
        o_parts, inv_sums = scratch("o_parts", C_HEADS * P, SEQ), scratch("inv_sums", C_HEADS * XT, P)
        mla(nc, o_parts, inv_sums, cq, ckv, k_pe, i.c_w_uq[0], i.c_w_ukv[0], ropes[2], ropes[3], turn_c, ident)
        if upto < 9: return
        with ExitStack() as layer1:
            y_hi = layer1.enter_context(nc.sbuf_tensor("y_hi1", [P, KD, SEQ], F32R))
            y_lo = layer1.enter_context(nc.sbuf_tensor("y_lo1", [P, KD, SEQ], F32R))
            join_heads(nc, y_hi, y_lo, o_parts, inv_sums)
            project_out(nc, "out1", y_hi, y_lo, SEQ, i.c_w_out[0], (mods(1, MIX_GATE, 1), i.norm_mix_post[1]),
                        (mods(1, FFN_SCALE, 1), mods(1, FFN_SHIFT, 1), i.norm_ffn_pre[1]), tile_of(x2), tile_of(x3),
                        ident)
            with nc.sbuf_tensor("y_sum1", [P, XT, D], F32, side="right") as y_sum:
                ffn(nc, "ffn1", SEQ, y_hi, y_lo, y_sum, i.ffn_w_up[1], i.ffn_conv_w[1], i.ffn_conv_b[1],
                    i.ffn_w_down[1])
                last_residual(nc, y_sum, (mods(1, FFN_GATE, 1), i.norm_ffn_post[1]), tile_of(x3), out)


def rope_constants():
    squares, tables = [np.eye(P, dtype=np.float32)], []
    token = np.arange(SEQ)
    for dims, still in ((B_DIM, 0), (C_ROPE, C_NOPE)):
        half = dims // 4
        m = np.zeros((P, P), np.float32)
        for d in range(still, P):
            if d % (2 * half) < half:
                m[d + half, d] = -1.0
            else:
                m[d - half, d] = 1.0
        squares.append(m)
        freq = np.float32(ROPE_BASE) ** (-np.arange(half, dtype=np.float32) / np.float32(half))
        d = np.arange(P) % dims
        pos = np.where((d < dims // 2)[:, None], token[None, :] // GRID_W, token[None, :] % GRID_W)
        angle = pos.astype(np.float32) * freq[d % half][:, None]
        angle[:still] = 0
        tables += [np.cos(angle), np.sin(angle)]
    return np.concatenate(squares, axis=1), np.stack(tables).astype(np.float32)


def kernel(**inputs):
    import concourse.bacc as bacc
    from concourse.bass_utils import run_bass_kernel_spmd

    nc = bacc.Bacc("TRN2", target_bir_lowering=False, num_devices=1)
    arrays, aps = {}, {}
    squares, tables = rope_constants()
    for name, a in [*((n, inputs[n]) for n in INPUTS), ("squares", squares), ("tables", tables)]:
        arrays[f"in_{name}"] = a = np.ascontiguousarray(a)
        aps[name] = nc.dram_tensor(f"in_{name}", a.shape, mybir.dt.from_np(a.dtype), kind="ExternalInput").ap()
    out = nc.dram_tensor("out", (1, SEQ, D), F32, kind="ExternalOutput").ap()
    trunk(nc, namedtuple("Inputs", INPUTS)(*(aps[n] for n in INPUTS)), aps["squares"], aps["tables"], out[0])
    r = run_bass_kernel_spmd(nc, [arrays], core_ids=[0])
    return r.results[0]["out"]
```

```python
import math
from collections import namedtuple
from contextlib import ExitStack, contextmanager

import numpy as np

import concourse.bass as bass
from concourse import mybir

F32 = mybir.dt.float32
F32R = mybir.dt.float32r
ALU = mybir.AluOpType
ACT = mybir.ActivationFunctionType
AX = mybir.AxisListType

P = 128
BANK = 512
D = 1024
KD = D // P
SEQ = 1024
CTX = 256
T = SEQ + CTX
XT = SEQ // P
TT = T // P
GRID_W = 64
ROPE_BASE = 10000.0
RMS_EPS = 1e-6
LN_EPS = 1e-5

A_WIDTH = 512
A_KERNEL = 31
B_HEADS = 4
B_DIM = 64
LAMBDA_INIT = 0.8 - 0.6 * math.exp(-0.3 * 0)
C_HEADS = 16
C_NOPE = 64
C_ROPE = 32
C_V = 64
C_Q_RANK = 768
C_KV_RANK = 256
C_IN = C_Q_RANK + C_KV_RANK + C_ROPE
FFN = 2816
FT = FFN // P

MIX_SHIFT, MIX_SCALE, MIX_GATE, FFN_SHIFT, FFN_SCALE, FFN_GATE = range(6)


def token_chunks(tokens):
    return [(a, min(BANK, tokens - a)) for a in range(0, tokens, BANK)]


class Signal:

    def __init__(self, sem, ahead=0, step=1):
        self.sem, self.ahead, self.step = sem, ahead, step

    def nth(self, n):
        return n * self.step + (1 + self.ahead) * self.step


@contextmanager
def stage(nc, name, signals, ahead=()):
    ahead = dict(ahead)
    handles = [nc.alloc_semaphore(name=f"{name}_{n}") for n in signals]
    yield namedtuple("Signals", signals)(*(
        Signal(h, ahead.get(n, 0), 16 if n.endswith("_in") or n.endswith("_stored") else 1)
        for n, h in zip(signals, handles)))
    nc.clear_and_free_semaphores(handles)
    nc.all_engine_barrier()


def start_ahead(eng, *signals):
    for signal in signals:
        eng.sem_inc(signal.sem, signal.ahead * signal.step)


def exact_product(pe, out, a_hi, a_lo, b_hi, b_lo, first, last):
    pe.matmul(out, a_hi, b_hi, start=first, stop=False)
    pe.matmul(out, a_hi, b_lo, start=False, stop=False)
    return pe.matmul(out, a_lo, b_hi, start=False, stop=last)


def row(ap_1d, n=P):
    return ap_1d.rearrange("(a n) -> a n", a=1).broadcast_to([n, ap_1d.shape[0]])


def column(ap_1d):
    return ap_1d.rearrange("(k p) -> p k", p=P)


class Modulation:

    SIGNALS = ["ada0_in", "ada1_in", "ada2_in", "ada_product", "row_done", "row0_stored", "row1_stored"]
    CHUNKS = 2 * 6 * D // BANK

    def __init__(self, nc, ctx, name, s, silu, mod, ada_w, ada_b, first, count):
        def sb(label, shape):
            return ctx.enter_context(nc.sbuf_tensor(f"{name}_{label}", shape, F32))

        self.s, self.silu, self.mod, self.ada_w, self.ada_b = s, silu, mod, ada_w, ada_b
        self.first, self.count = first, count
        self.w = sb("ada_w", [P, 3, KD, BANK])
        self.bias = sb("ada_b", [2, 3, BANK])
        self.rows = sb("mod_rows", [2, 2, BANK])
        self.ps = ctx.enter_context(nc.psum_tensor(f"{name}_mod_ps", [P, 2, BANK], F32))
        self.ada_in, self.stored = (s.ada0_in, s.ada1_in, s.ada2_in), (s.row0_stored, s.row1_stored)

    def load(self, sp, n):
        s = self.s
        if n >= self.count:
            return
        if n >= 3:
            sp.wait_ge(s.row_done.sem, n - 2)
        layer, a = divmod((self.first + n) * BANK, 6 * D)
        sem = self.ada_in[n % 3].sem
        sp.dma_start(self.w[:, n % 3, :, :], self.ada_w[layer].rearrange("(k p) n -> p k n", p=P)[:, :, a:a + BANK])\
          .then_inc(sem, 16)
        sp.dma_start(self.bias[:, n % 3, :], row(self.ada_b[layer, a:a + BANK], 2)).then_inc(sem, 16)

    def store(self, sp, n):
        sp.wait_ge(self.s.row_done.sem, n + 1)
        a = (self.first + n) * BANK
        sp.dma_start(self.mod[:, a:a + BANK], self.rows[:, n % 2, :]).then_inc(self.stored[n % 2].sem, 16)

    def stores_over(self, sp):
        for j in range(2):
            sp.wait_ge(self.stored[j].sem, 16 * (self.count // 2))

    def product(self, pe, n):
        s = self.s
        pe.wait_ge(self.ada_in[n % 3].sem, 32 * (n // 3 + 1))
        if n >= 2:
            pe.wait_ge(s.row_done.sem, n - 1)
        for k in range(KD):
            mm = pe.matmul(self.ps[0:2, n % 2, :], self.silu[:, k, :], self.w[:, n % 3, k, :],
                           start=k == 0, stop=k == KD - 1)
        mm.then_inc(s.ada_product.sem, 1)

    def add(self, dve, n):
        dve.wait_ge(self.s.ada_product.sem, n + 1)
        if n >= 2:
            dve.wait_ge(self.stored[n % 2].sem, 16 * (n // 2))
        dve.tensor_tensor(self.rows[:, n % 2, :], self.ps[0:2, n % 2, :], self.bias[:, n % 3, :], ALU.add)\
           .then_inc(self.s.row_done.sem, 1)


def first_modulation(nc, silu, mod, c, c_ctx, ada_w, ada_b, count):
    with ExitStack() as ctx:
        cond = ctx.enter_context(nc.sbuf_tensor("mod_cond", [P, 2, KD], F32))
        s = ctx.enter_context(stage(nc, "mod", Modulation.SIGNALS + ["cond_in", "silu_done"]))
        m = Modulation(nc, ctx, "mod", s, silu, mod, ada_w, ada_b, 0, count)
        block = ctx.enter_context(nc.Block())

        @block.sync
        def _(sp):
            for r, vec in enumerate((c, c_ctx)):
                sp.dma_start(cond[:, r, :], column(vec), allow_slow_non_contiguous=True).then_inc(s.cond_in.sem, 16)
            for n in range(3):
                m.load(sp, n)
            for n in range(count):
                m.store(sp, n)
                m.load(sp, n + 3)
            m.stores_over(sp)

        @block.scalar
        def _(act):
            act.wait_ge(s.cond_in.sem, 32)
            act.activation(silu[:, :, :], cond[:, :, :].rearrange("p r k -> p k r"), ACT.Silu)\
               .then_inc(s.silu_done.sem, 1)

        @block.tensor
        def _(pe):
            pe.wait_ge(s.silu_done.sem, 1)
            for n in range(count):
                m.product(pe, n)

        @block.vector
        def _(dve):
            for n in range(count):
                m.add(dve, n)


def load_constants(nc, consts, ident, turn_a, turn_c):
    with ExitStack() as ctx:
        s = ctx.enter_context(stage(nc, "const", ["const_in"]))
        block = ctx.enter_context(nc.Block())

        @block.sync
        def _(sp):
            for j, m in enumerate((ident, turn_a, turn_c)):
                sp.dma_start(m[:, :], consts[:, j * P:(j + 1) * P]).then_inc(s.const_in.sem, 16)
            sp.wait_ge(s.const_in.sem, 48)


class TokenTail:

    SIGNALS = ["half_set", "rows_in", "gs_done", "x0_in", "x1_in", "x2_in", "square", "rstd_step", "rstd", "post_step", "x_new",
               "x0_stored", "x1_stored", "x2_stored", "pre_step", "h_done", "h_turned", "h_hi", "h_lo"]

    def __init__(self, nc, ctx, name, s, post, pre, kinds, turns, ident):
        def sb(label, shape, dt=F32):
            return ctx.enter_context(nc.sbuf_tensor(f"{name}_{label}", shape, dt))

        self.s, self.post, self.pre, self.kinds, self.ident = s, post, pre, kinds, ident
        self.turns = turns
        self.x_in = [s.x0_in, s.x1_in, s.x2_in]
        self.x_stored = [s.x0_stored, s.x1_stored, s.x2_stored]
        self.x = sb("x", [P, 3, D])
        self.junk = sb("junk", [P, D])
        self.small = sb("small", [P, 8, TT])
        self.minus_half = sb("minus_half", [P, 1])
        self.rows = sb("rows", [P, kinds * (3 if post and pre else 1 if post else 2), D])
        if pre:
            self.h = sb("h", [P, 2, D])
            self.turned = ctx.enter_context(nc.psum_tensor(f"{name}_turned", [P, 2, BANK], F32))
        n = 0
        self.gate_row = self.scale_row = self.shift_row = None
        if post:
            self.gate_row, n = n, kinds
        if pre:
            self.scale_row, self.shift_row = n, n + kinds
        self.squares_per_tile = (1 if post else 0) + (1 if pre else 0)
        self.row_loads = kinds * ((1 if post else 0) + (2 if pre else 0)) + (1 if post else 0) + (1 if pre else 0)

    def kind(self, tile):
        return 0 if tile < XT else 1

    def load_rows(self, sp):
        s = self.s
        if self.post:
            gates, gain = self.post
            for r in range(self.kinds):
                sp.dma_start(self.rows[:, self.gate_row + r, :], row(gates[r])).then_inc(s.rows_in.sem, 16)
            sp.dma_start(self.x[:, 0, :], row(gain)).then_inc(s.rows_in.sem, 16)
        if self.pre:
            scales, shifts, gain = self.pre
            for r in range(self.kinds):
                sp.dma_start(self.rows[:, self.scale_row + r, :], row(scales[r])).then_inc(s.rows_in.sem, 16)
                sp.dma_start(self.rows[:, self.shift_row + r, :], row(shifts[r])).then_inc(s.rows_in.sem, 16)
            sp.dma_start(self.x[:, 1, :], row(gain)).then_inc(s.rows_in.sem, 16)
        sp.wait_ge(s.gs_done.sem, s.gs_done.nth((1 if self.post else 0) * self.kinds
                                                + (1 if self.pre else 0) * self.kinds - 1))

    def load_x(self, sp, turn, src):
        s = self.s
        if turn >= 3:
            if self.post:
                sp.wait_ge(self.x_stored[turn % 3].sem, 16 * (turn // 3))
            if self.pre:
                sp.wait_ge(s.h_done.sem, turn - 2)
        sp.dma_start(self.x[:, turn % 3, :], src).then_inc(self.x_in[turn % 3].sem, 16)

    def store_x(self, sp, turn, dst):
        s = self.s
        sp.wait_ge(s.x_new.sem, turn + 1)
        sp.dma_start(dst, self.x[:, turn % 3, :]).then_inc(self.x_stored[turn % 3].sem, 16)

    def stores_over(self, sp):
        for j, stored in enumerate(self.x_stored):
            sp.wait_ge(stored.sem, 16 * len(range(j, self.turns, 3)))

    def prepare_rows(self, dve):
        s = self.s
        dve.wait_ge(s.rows_in.sem, 16 * self.row_loads)
        if self.post:
            for r in range(self.kinds):
                g = self.rows[:, self.gate_row + r, :]
                dve.tensor_tensor(g, g, self.x[:, 0, :], ALU.mult).then_inc(s.gs_done.sem, 1)
        if self.pre:
            for r in range(self.kinds):
                g = self.rows[:, self.scale_row + r, :]
                dve.scalar_tensor_tensor(out=g, in0=g, scalar=1.0, in1=self.x[:, 1, :],
                                         op0=ALU.add, op1=ALU.mult).then_inc(s.gs_done.sem, 1)
        dve.wait_ge(s.gs_done.sem, self.kinds * self.squares_per_tile)

    def post_vector(self, dve, turn, tile, y):
        s = self.s
        x = self.x[:, turn % 3, :]
        dve.wait_ge(s.rstd.sem, self.square_of_post(turn) + 1)
        dve.scalar_tensor_tensor(out=y, in0=y, scalar=self.small[:, 2, turn:turn + 1],
                                 in1=self.rows[:, self.gate_row + self.kind(tile), :],
                                 op0=ALU.mult, op1=ALU.mult).then_inc(s.post_step.sem, 1)
        dve.wait_ge(s.post_step.sem, turn + 1)
        dve.wait_ge(self.x_in[turn % 3].sem, 16 * (turn // 3 + 1))
        dve.tensor_tensor(x, x, y, ALU.add).then_inc(s.x_new.sem, 1)

    def pre_vector(self, dve, turn, tile):
        s = self.s
        x, h = self.x[:, turn % 3, :], self.h[:, turn % 2, :]
        dve.wait_ge(s.rstd.sem, self.square_of_pre(turn) + 1)
        if turn >= 2:
            dve.wait_ge(s.h_turned.sem, 2 * (turn - 1))
        dve.scalar_tensor_tensor(out=h, in0=x, scalar=self.small[:, 5, turn:turn + 1],
                                 in1=self.rows[:, self.scale_row + self.kind(tile), :],
                                 op0=ALU.mult, op1=ALU.mult).then_inc(s.pre_step.sem, 1)
        dve.wait_ge(s.pre_step.sem, turn + 1)
        dve.tensor_tensor(h, h, self.rows[:, self.shift_row + self.kind(tile), :], ALU.add)\
           .then_inc(s.h_done.sem, 1)

    def split_vector(self, dve, turn, hi, lo):
        s = self.s
        for b in range(2):
            dve.wait_ge(s.h_hi.sem, 2 * turn + b + 1)
            dve.tensor_tensor(lo[:, 4 * b:4 * b + 4, :],
                              self.turned[:, b, :].rearrange("p (k n) -> p k n", n=P),
                              hi[:, 4 * b:4 * b + 4, :].bitcast(F32), ALU.subtract).then_inc(s.h_lo.sem, 1)

    def square_of_post(self, turn):
        return turn if not self.pre else (0 if turn == 0 else 2 * turn - 1)

    def square_of_pre(self, turn):
        if not self.post:
            return turn
        return 2 * turn + 2 if turn < self.turns - 1 else 2 * turn + 1

    def square(self, act, n, src, out):
        s = self.s
        if n:
            act.wait_ge(s.square.sem, n)
        act.activation(self.junk[:, :], src, ACT.Square, accum_out=out).then_inc(s.square.sem, 1)

    def post_scalar(self, act, turn, y):
        self.square(act, self.square_of_post(turn), y, self.small[:, 0, turn:turn + 1])

    def pre_scalar(self, act, turn):
        s = self.s
        if self.post:
            act.wait_ge(s.x_new.sem, turn + 1)
        else:
            act.wait_ge(self.x_in[turn % 3].sem, 16 * (turn // 3 + 1))
        self.square(act, self.square_of_pre(turn), self.x[:, turn % 3, :], self.small[:, 3, turn:turn + 1])

    def split_scalar(self, act, turn, hi):
        s = self.s
        for b in range(2):
            act.wait_ge(s.h_turned.sem, 2 * turn + b + 1)
            act.activation(hi[:, 4 * b:4 * b + 4, :], self.turned[:, b, :].rearrange("p (k n) -> p k n", n=P),
                           ACT.Copy).then_inc(s.h_hi.sem, 1)

    def prepare_gpsimd(self, pool):
        pool.memset(self.minus_half[:, :], -0.5).then_inc(self.s.half_set.sem, 1)
        pool.wait_ge(self.s.half_set.sem, 1)

    def rstd_gpsimd(self, pool, n, turn, at):
        s = self.s
        ss, ms, rstd = (self.small[:, at + j, turn:turn + 1] for j in range(3))
        pool.wait_ge(s.square.sem, n + 1)
        pool.tensor_scalar(ms, ss, 1.0 / D, RMS_EPS, ALU.mult, ALU.add).then_inc(s.rstd_step.sem, 1)
        pool.wait_ge(s.rstd_step.sem, n + 1)
        pool.tensor_tensor(rstd, ms, self.minus_half[:, :], ALU.pow).then_inc(s.rstd.sem, 1)

    def post_gpsimd(self, pool, turn):
        self.rstd_gpsimd(pool, self.square_of_post(turn), turn, 0)

    def pre_gpsimd(self, pool, turn):
        self.rstd_gpsimd(pool, self.square_of_pre(turn), turn, 3)

    def turn_tensor(self, pe, turn):
        s = self.s
        pe.wait_ge(s.h_done.sem, turn + 1)
        for b in range(2):
            if turn:
                pe.wait_ge(s.h_lo.sem, 2 * (turn - 1) + b + 1)
            for k in range(4):
                mm = pe.transpose(self.turned[:, b, k * P:(k + 1) * P],
                                  self.h[:, turn % 2, (4 * b + k) * P:(4 * b + k + 1) * P], self.ident[:, :])
            mm.then_inc(s.h_turned.sem, 1)


def first_norm(nc, h_hi, h_lo, x, ctx_rows, pre, ident, silu, mod, ada_w, ada_b, first_chunk):
    REST = Modulation.CHUNKS - first_chunk
    share = REST // TT
    with ExitStack() as ctx:
        s = ctx.enter_context(stage(nc, "norm", TokenTail.SIGNALS + Modulation.SIGNALS))
        tail = TokenTail(nc, ctx, "norm", s, None, pre, 2, TT, ident)
        m = Modulation(nc, ctx, "norm", s, silu, mod, ada_w, ada_b, first_chunk, REST)
        block = ctx.enter_context(nc.Block())

        @block.sync
        def _(sp):
            def load_x(t):
                if t < TT:
                    tail.load_x(sp, t, x[t * P:(t + 1) * P, :] if t < XT
                                else ctx_rows[(t - XT) * P:(t - XT + 1) * P, :])

            m.load(sp, 0)
            tail.load_rows(sp)
            load_x(0)
            m.load(sp, 1)
            load_x(1)
            m.load(sp, 2)
            load_x(2)
            for t in range(TT):
                for n in range(share * t, share * (t + 1)):
                    m.store(sp, n)
                    m.load(sp, n + 3)
                load_x(t + 3)
            m.stores_over(sp)

        @block.scalar
        def _(act):
            act.wait_ge(s.gs_done.sem, 2)
            for t in range(TT + 1):
                if t < TT:
                    tail.pre_scalar(act, t)
                if t >= 1:
                    tail.split_scalar(act, t - 1, h_hi[:, :, (t - 1) * P:t * P])

        @block.vector
        def _(dve):
            tail.prepare_rows(dve)
            for t in range(TT + 1):
                if t < TT:
                    tail.pre_vector(dve, t, t)
                if t >= 1:
                    tail.split_vector(dve, t - 1, h_hi[:, :, (t - 1) * P:t * P], h_lo[:, :, (t - 1) * P:t * P])
                if t < TT:
                    for n in range(share * t, share * (t + 1)):
                        m.add(dve, n)

        @block.gpsimd
        def _(pool):
            tail.prepare_gpsimd(pool)
            for t in range(TT):
                tail.pre_gpsimd(pool, t)

        @block.tensor
        def _(pe):
            for t in range(TT):
                for n in range(share * t, share * (t + 1)):
                    m.product(pe, n)
                tail.turn_tensor(pe, t)


def project_conv_diff(nc, h_hi, h_lo, conv_out, qk, v_rows, w_in, conv_w, conv_b, cos, sin, turn):
    chunks = token_chunks(T)
    NC = len(chunks)
    HALO = A_KERNEL // 2
    PAD = T + 3 * HALO
    SPAN = T + HALO
    AT = A_WIDTH // P
    QT = 2 * B_HEADS
    PIECES = 2 * AT + QT + A_WIDTH // P
    PARTS = ((0, 1), (1, 7), (7, 13), (13, 22), (22, A_KERNEL))

    def padded(a):
        return a + HALO + (HALO if a >= SEQ else 0)

    with ExitStack() as ctx:
        def sb(label, shape, dt=F32):
            return ctx.enter_context(nc.sbuf_tensor(f"ab_{label}", shape, dt))

        raw = sb("raw", [P, 2, KD, P])
        w_hi = sb("w_hi", [P, 2, KD, P], F32R)
        w_lo = sb("w_lo", [P, 2, KD, P], F32R)
        v_hi = sb("v_hi", [P, KD, A_WIDTH], F32R)
        v_lo = sb("v_lo", [P, KD, A_WIDTH], F32R)
        u = sb("u", [P, 2, PAD])
        conv = sb("conv", [P, 2, SPAN])
        sig = sb("sig", [P, T])
        taps = sb("taps", [P, AT, A_KERNEL + 1])
        cos_t = sb("cos", [P, SEQ])
        sin_t = sb("sin", [P, SEQ])
        qk_t = sb("qk", [P, 2, T])
        part = sb("part", [P, 2, SEQ])
        v_t = sig
        main_ps = ctx.enter_context(nc.psum_tensor("ab_main", [P, 2, NC, BANK], F32))
        turn_ps = ctx.enter_context(nc.psum_tensor("ab_turn", [P, 2, BANK], F32))
        s = ctx.enter_context(stage(nc, "ab", [
            "small_in", "raw0_in", "raw1_in", "asked", "hi_done", "w_ready", "zeroed", "full0", "full1",
            "sig_done", "u_done", "conv_step", "conv_done", "conv_stored", "conv_free", "qk_free", "copied", "turned", "cos_part",
            "sin_part", "sum_done", "qk0_stored", "qk1_stored", "v_full", "v_copied", "v0_stored",
            "v1_stored"],
            {"sig_done": 3, "u_done": 3, "conv_done": 2, "conv_free": 2, "copied": 2, "cos_part": 2,
             "sin_part": 4, "sum_done": 2, "qk_free": 2, "w_ready": 2, "full0": 1, "full1": 1}))
        s.conv_stored.step = 32
        qk_stored, v_stored = [s.qk0_stored, s.qk1_stored], [s.v0_stored, s.v1_stored]
        raw_in, full = [s.raw0_in, s.raw1_in], [s.full0, s.full1]
        block = ctx.enter_context(nc.Block())
        w_tiles = w_in.rearrange("(k p) n -> p k n", p=P)

        def turns(eng, one_turn, piece_v):
            for i in range(AT):
                one_turn(i)
            for j in range(AT):
                piece_v(j)

        @block.sync
        def _(sp):
            for j in range(AT):
                sp.dma_start(taps[:, j, 0:A_KERNEL], conv_w[:, j * P:(j + 1) * P].rearrange("t p -> p t"),
                             allow_slow_non_contiguous=True).then_inc(s.small_in.sem, 16)
                sp.dma_start(taps[:, j, A_KERNEL:], conv_b[j * P:(j + 1) * P].rearrange("(p a) -> p a", a=1))\
                  .then_inc(s.small_in.sem, 16)
            sp.dma_start(cos_t[:, :], cos).then_inc(s.small_in.sem, 16)
            sp.dma_start(sin_t[:, :], sin).then_inc(s.small_in.sem, 16)

            def load(piece, slot, cols):
                sp.wait_ge(s.w_ready.sem, s.w_ready.nth(piece - 2))
                sp.sem_inc(s.asked.sem, 1)
                sp.dma_start(raw[:, slot, :, :], w_tiles[:, :, cols]).then_inc(raw_in[slot].sem, 16)

            def one_turn(i):
                load(i * 4, 0, slice(i * P + A_WIDTH, (i + 1) * P + A_WIDTH))
                load(i * 4 + 1, 1, slice(i * P, (i + 1) * P))
                for j in range(2):
                    first = 2 * A_WIDTH + (2 * i + j) * P
                    load(i * 4 + (2 + j), j, slice(first, first + P))

            def piece_v(j):
                first = 2 * A_WIDTH + QT * P + j * P
                load(2 * AT + QT + j, j % 2, slice(first, first + P))

            turns(sp, one_turn, piece_v)

        @block.scalar
        def _(act):
            start_ahead(act, s.sig_done, s.copied)

            def hi(piece, slot, n, dst):
                act.wait_ge(raw_in[slot].sem, raw_in[slot].nth(n))
                act.activation(dst, raw[:, slot, :, :], ACT.Copy).then_inc(s.hi_done.sem, 1)

            def weights(piece):
                j, n = piece % 2, piece // 2
                act.wait_ge(full[j].sem, full[j].nth(n * NC - 1))
                hi(piece, j, n, w_hi[:, j, :, :])

            def copy(i, j):
                act.wait_ge(s.qk_free.sem, s.qk_free.nth(i * 2 + (j - 2)))
                for c, (a, n) in enumerate(chunks):
                    act.wait_ge(full[j].sem, full[j].nth(i * (2 * NC) + (NC + c)))
                    ins = act.activation(qk_t[:, j, a:a + n], main_ps[:, j, c, 0:n], ACT.Copy)
                ins.then_inc(s.copied.sem, 1)

            def one_turn(i):
                if i == 0:
                    weights(0)
                    weights(1)
                weights(4 * i + 2)
                act.wait_ge(s.u_done.sem, s.u_done.nth(i * NC - 1))
                for c, (a, n) in enumerate(chunks):
                    act.wait_ge(s.full0.sem, s.full0.nth(i * (2 * NC) + c))
                    act.activation(sig[:, a:a + n], main_ps[:, 0, c, 0:n], ACT.Sigmoid).then_inc(s.sig_done.sem, 1)
                weights(4 * i + 3)
                for j in range(2):
                    if i + 1 < AT:
                        weights(4 * i + 4 + j)
                    copy(i, j)

            def piece_v(j):
                hi(2 * AT + QT + j, j % 2, AT + QT // 2 + j // 2, v_hi[:, :, j * P:(j + 1) * P])

            turns(act, one_turn, piece_v)
            act.wait_ge(s.u_done.sem, s.u_done.nth(AT * NC - 1))
            for t in range(TT):
                act.wait_ge(s.v_full.sem, t + 1)
                if t >= 2:
                    act.wait_ge(v_stored[t % 2].sem, 16 * (t // 2))
                act.activation(v_t[:, (t % 2) * BANK:(t % 2 + 1) * BANK], turn_ps[:, t % 2, :], ACT.Copy)\
                   .then_inc(s.v_copied.sem, 1)

        @block.vector
        def _(dve):
            start_ahead(dve, s.w_ready, s.u_done, s.conv_done, s.sin_part, s.sum_done)
            dve.memset(u[:, :, :], 0.0).then_inc(s.zeroed.sem, 1)
            dve.wait_ge(s.zeroed.sem, 1)
            dve.wait_ge(s.small_in.sem, s.small_in.nth(2 * AT + 1))

            def lo(piece, slot, hi_part, dst):
                dve.wait_ge(s.hi_done.sem, s.hi_done.nth(piece))
                dve.tensor_tensor(dst, raw[:, slot, :, :], hi_part.bitcast(F32), ALU.subtract)\
                   .then_inc(s.w_ready.sem, 1)

            def weights(piece):
                lo(piece, piece % 2, w_hi[:, piece % 2, :, :], w_lo[:, piece % 2, :, :])

            def convolve(i, part):
                steps = A_KERNEL - 1
                out, src = conv[:, i % 2, :], u[:, i % 2, :]
                for j in range(*PARTS[part]):
                    if j == 0:
                        dve.wait_ge(s.u_done.sem, s.u_done.nth(i * NC + (NC - 1)))
                        dve.wait_ge(s.conv_free.sem, s.conv_free.nth(i - 2))
                        dve.tensor_scalar(out, src[:, 0:SPAN], taps[:, i, 0:1], taps[:, i, A_KERNEL:],
                                          ALU.mult, ALU.add).then_inc(s.conv_step.sem, 1)
                        continue
                    dve.wait_ge(s.conv_step.sem, s.conv_step.nth(i * steps + (j - 1)))
                    dve.scalar_tensor_tensor(out=out, in0=src[:, j:j + SPAN], scalar=taps[:, i, j:j + 1],
                                             in1=out, op0=ALU.mult, op1=ALU.add)\
                       .then_inc((s.conv_step if j < A_KERNEL - 1 else s.conv_done).sem, 1)

            def gated(i):
                dve.wait_ge(s.conv_done.sem, s.conv_done.nth(i - 2))
                for c, (a, n) in enumerate(chunks):
                    dve.wait_ge(s.sig_done.sem, s.sig_done.nth(i * NC + c))
                    dve.wait_ge(s.full1.sem, s.full1.nth(i * (2 * NC) + c))
                    dve.tensor_tensor(u[:, i % 2, padded(a):padded(a) + n], main_ps[:, 1, c, 0:n], sig[:, a:a + n],
                                      ALU.mult).then_inc(s.u_done.sem, 1)

            def rotated(i, j):
                n = i * 2 + j
                for c in range(2):
                    dve.wait_ge(s.turned.sem, s.turned.nth(n * 2 + c))
                    dve.tensor_tensor(part[:, j, c * BANK:(c + 1) * BANK], turn_ps[:, c, :],
                                      sin_t[:, c * BANK:(c + 1) * BANK], ALU.mult).then_inc(s.sin_part.sem, 1)
                dve.wait_ge(s.sin_part.sem, s.sin_part.nth(n * 2 + 1))
                dve.wait_ge(s.cos_part.sem, s.cos_part.nth(n))
                dve.tensor_tensor(qk_t[:, j, 0:SEQ], qk_t[:, j, 0:SEQ], part[:, j, :], ALU.add)\
                   .then_inc(s.sum_done.sem, 1)

            def one_turn(i):
                if i == 0:
                    weights(0)
                    weights(1)
                else:
                    convolve(i - 1, 3)
                weights(4 * i + 2)
                if i:
                    convolve(i - 1, 4)
                gated(i)
                convolve(i, 0)
                weights(4 * i + 3)
                convolve(i, 1)
                if i + 1 < AT:
                    weights(4 * i + 4)
                convolve(i, 2)
                if i + 1 < AT:
                    weights(4 * i + 5)
                rotated(i, 0)
                rotated(i, 1)

            def piece_v(j):
                lo(2 * AT + QT + j, j % 2, v_hi[:, :, j * P:(j + 1) * P], v_lo[:, :, j * P:(j + 1) * P])

            turns(dve, one_turn, piece_v)
            convolve(AT - 1, 3)
            convolve(AT - 1, 4)

        @block.gpsimd
        def _(pool):
            start_ahead(pool, s.conv_free, s.cos_part, s.qk_free)
            pool.wait_ge(s.small_in.sem, s.small_in.nth(2 * AT + 1))

            def store_conv(i):
                pool.wait_ge(s.conv_done.sem, s.conv_done.nth(i))
                rows, src = conv_out[i * P:(i + 1) * P, :], conv[:, i % 2, :]
                pool.dma_start(rows[:, 0:SEQ], src[:, 0:SEQ]).then_inc(s.conv_stored.sem, 16)
                pool.dma_start(rows[:, SEQ:T], src[:, SEQ + HALO:T + HALO]).then_inc(s.conv_stored.sem, 16)
                pool.wait_ge(s.conv_stored.sem, s.conv_stored.nth(i))
                pool.sem_inc(s.conv_free.sem, 1)

            def one_turn(i):
                if i:
                    store_conv(i - 1)
                for j in range(2):
                    n = i * 2 + j
                    pool.wait_ge(s.turned.sem, s.turned.nth(n * 2 + 1))
                    pool.tensor_tensor(qk_t[:, j, 0:SEQ], qk_t[:, j, 0:SEQ], cos_t[:, :], ALU.mult)\
                        .then_inc(s.cos_part.sem, 1)
                for j in range(2):
                    n = i * 2 + j
                    pool.wait_ge(s.sum_done.sem, s.sum_done.nth(n))
                    pool.dma_start(qk[n * P:(n + 1) * P, :], qk_t[:, j, :]).then_inc(qk_stored[j].sem, 16)
                for j in range(2):
                    pool.wait_ge(qk_stored[j].sem, qk_stored[j].nth(i))
                    pool.sem_inc(s.qk_free.sem, 1)

            turns(pool, one_turn, lambda j: None)
            for t in range(TT):
                pool.wait_ge(s.v_copied.sem, t + 1)
                pool.dma_start(v_rows[t * P:(t + 1) * P, :], v_t[:, (t % 2) * BANK:(t % 2 + 1) * BANK])\
                    .then_inc(v_stored[t % 2].sem, 16)
            store_conv(AT - 1)
            for j in range(2):
                pool.wait_ge(v_stored[j].sem, 16 * TT // 2)

        @block.tensor
        def _(pe):
            start_ahead(pe, s.full0, s.full1)

            def product(piece, j, bank_read):
                pe.wait_ge(s.w_ready.sem, s.w_ready.nth(piece))
                for c, (a, n) in enumerate(chunks):
                    bank_read(c)
                    for k in range(KD):
                        mm = exact_product(pe, main_ps[:, j, c, 0:n], w_hi[:, j, k, :], w_lo[:, j, k, :],
                                           h_hi[:, k, a:a + n], h_lo[:, k, a:a + n], k == 0, k == KD - 1)
                    mm.then_inc(full[j].sem, 1)

            def one_turn(i):
                for j in range(2):
                    pe.wait_ge(s.copied.sem, s.copied.nth(i * 2 + (j - 2)))
                    product(i * 4 + j, j, lambda c: None)
                for j in range(2):
                    used = (s.sig_done, s.u_done)[j]
                    product(i * 4 + (2 + j), j, lambda c: pe.wait_ge(used.sem, used.nth(i * NC + c)))
                for j in range(2):
                    n = i * 2 + j
                    pe.wait_ge(s.copied.sem, s.copied.nth(n))
                    for c in range(2):
                        pe.wait_ge(s.sin_part.sem, s.sin_part.nth(n * 2 + (c - 2)))
                        pe.matmul(turn_ps[:, c, :], turn[:, :], qk_t[:, j, c * BANK:(c + 1) * BANK],
                                  start=True, stop=True).then_inc(s.turned.sem, 1)

            turns(pe, one_turn, lambda j: None)
            pe.wait_ge(s.w_ready.sem, s.w_ready.nth(PIECES - 1))
            for t in range(TT):
                if t < 2:
                    pe.wait_ge(s.sin_part.sem, s.sin_part.nth((QT - 1) * 2 + t))
                else:
                    pe.wait_ge(s.v_copied.sem, t - 1)
                for k in range(KD):
                    mm = exact_product(pe, turn_ps[:, t % 2, :], h_hi[:, k, t * P:(t + 1) * P],
                                       h_lo[:, k, t * P:(t + 1) * P], v_hi[:, k, :], v_lo[:, k, :],
                                       k == 0, k == KD - 1)
                mm.then_inc(s.v_full.sem, 1)


@contextmanager
def bare_stage(nc, name, signals):
    handles = {n: nc.alloc_semaphore(name=f"{name}_{n}") for n in signals}
    yield namedtuple("Semaphores", signals)(*handles.values())
    nc.clear_and_free_semaphores(list(handles.values()))
    nc.all_engine_barrier()


def ffn(nc, name, tokens, h_hi, h_lo, y_sum, w_up, conv_w, conv_b, w_down):
    chunks = token_chunks(tokens)
    NC = len(chunks)
    TT = tokens // P
    SUMS = 2 * TT
    segments = [(0, SEQ)] + ([(SEQ, CTX)] if tokens > SEQ else [])
    NS = len(segments)
    PAD = tokens + 1 + NS
    GROUPS = FT // 2

    def padded(a):
        return a + 1 + (a >= SEQ)

    with ExitStack() as ctx:
        def sb(label, shape, dt=F32):
            return ctx.enter_context(nc.sbuf_tensor(f"{name}_{label}", shape, dt))

        def ps(label, shape):
            return ctx.enter_context(nc.psum_tensor(f"{name}_{label}", shape, F32))

        raw = sb("raw", [P, 4, D])
        w_hi = sb("w_hi", [P, 4, D], F32R)
        w_lo = sb("w_lo", [P, 4, D], F32R)
        act_hi = sb("act_hi", [P, 2, tokens], F32R)
        act_lo = sb("act_lo", [P, 2, tokens], F32R)
        gate = sb("gate", [P, PAD])
        conv = sb("conv", [P, PAD])
        taps = sb("taps", [P, 4, FT])
        gate_ps = ps("gate_ps", [P, NC, BANK])
        val_ps = ps("val_ps", [P, NC, BANK])
        down_ps = ps("down_ps", [P, 2, BANK])

        s = ctx.enter_context(bare_stage(nc, name, [
            "taps_in", "value_in", "gate_w_in", "down0_in", "down1_in", "asked", "w_hi_done", "w_ready", "gate_full", "gate_in",
            "zeroed", "val_full", "val_used", "conv_step", "conv_done", "silu_done",
            "act_hi_done", "act_ready", "sum_full", "sum_done"]))
        raw_in = [s.value_in, s.gate_w_in, s.down0_in, s.down1_in]
        block = ctx.enter_context(nc.Block())

        VALUE, GATE, DOWN0, DOWN1 = range(4)
        w_up_tiles = w_up.rearrange("(k p) (two f) -> p k two f", p=P, two=2)

        def schedule(eng, split, gate_product, gate_work, value_product, value_work, down):
            split(GATE, 0, 0, 2)
            split(VALUE, 0, 1, 2)
            for tile in range(2):
                gate_product(tile, 2 * tile)
                gate_work(tile)
                split(GATE, tile + 1, 2 * tile + 2, 2)
                value_product(tile, 2 * tile + 1)
                split(VALUE, tile + 1, 2 * tile + 3, 2)
                value_work(tile, tile)

            def group(g, more):
                gate_product(2 * g, 6 * g - 2)
                gate_work(2 * g)
                split(DOWN0, 2 * g - 2, 6 * g, 6)
                split(DOWN1, 2 * g - 1, 6 * g + 1, 6)
                split(GATE, 2 * g + 1, 6 * g + 2, 4)
                value_product(2 * g, 6 * g - 1)
                split(VALUE, 2 * g + 1, 6 * g + 3, 4)
                down(g - 1, 6 * g + 1)
                value_work(2 * g, 0)
                gate_product(2 * g + 1, 6 * g + 2)
                gate_work(2 * g + 1)
                split(GATE if more else DOWN0, 2 * g + 2 if more else 2 * g, 6 * g + 4, 2 if more else 4)
                value_product(2 * g + 1, 6 * g + 3)
                split(VALUE if more else DOWN1, 2 * g + 2 if more else 2 * g + 1, 6 * g + 5, 2 if more else 4)
                value_work(2 * g + 1, 1)

            with eng.Fori(1, GROUPS - 1) as g:
                group(g, True)
            group(GROUPS - 1, False)
            down(GROUPS - 1, 6 * GROUPS - 1)

        def idle(*_):
            pass

        @block.sync
        def _(sp):
            for j in range(3):
                sp.dma_start(taps[:, j, :], conv_w[j].rearrange("(t p) -> p t", p=P),
                             allow_slow_non_contiguous=True).then_inc(s.taps_in, 16)
            sp.dma_start(taps[:, 3, :], conv_b.rearrange("(t p) -> p t", p=P),
                         allow_slow_non_contiguous=True).then_inc(s.taps_in, 16)

            def split(kind, tile, piece, back):
                if kind in (GATE, VALUE):
                    src = w_up_tiles[:, :, kind, :][:, :, bass.ds(tile * P, P)]
                else:
                    src = w_down[bass.ds(tile * P, P), :].rearrange("(k p) n -> p k n", k=1)
                if not (isinstance(piece, int) and piece < 2):
                    sp.wait_ge(s.w_ready, piece - (back - 1))
                    sp.sem_inc(s.asked, 1)
                sp.dma_start(raw[:, kind, :].rearrange("p (k n) -> p k n", n=src.shape[-1]), src)\
                  .then_inc(raw_in[kind], 16)

            schedule(sp, split, idle, idle, idle, idle, idle)

        @block.scalar
        def _(act):
            def split(kind, tile, piece, back):
                if kind in (GATE, VALUE):
                    act.wait_ge(raw_in[kind], tile * 16 + 16)
                else:
                    act.wait_ge(raw_in[kind], (tile - (kind - DOWN0)) * 8 + 16)
                if kind in (GATE, VALUE):
                    if not (isinstance(tile, int) and tile == 0):
                        act.wait_ge(s.gate_full if kind == GATE else s.val_full, tile * NC)
                else:
                    act.wait_ge(s.sum_full, (tile - (kind - DOWN0)) * TT + 1)
                act.activation(w_hi[:, kind, :], raw[:, kind, :], ACT.Copy).then_inc(s.w_hi_done, 1)

            def gate_work(tile):
                if isinstance(tile, int) and tile == 0:
                    act.wait_ge(s.zeroed, 2)
                else:
                    act.wait_ge(s.conv_done, tile)
                for c, (a, n) in enumerate(chunks):
                    act.wait_ge(s.gate_full, tile * NC + (c + 1))
                    act.activation(gate[:, padded(a):padded(a) + n], gate_ps[:, c, 0:n], ACT.Copy)\
                       .then_inc(s.gate_in, 1)
                act.wait_ge(s.conv_done, tile + 1)
                act.activation(conv[:, 1:PAD - 1], conv[:, 1:PAD - 1], ACT.Silu).then_inc(s.silu_done, 1)

            def value_work(tile, slot):
                act.wait_ge(s.val_used, tile * NC + NC)
                if not (isinstance(tile, int) and tile < 2):
                    act.wait_ge(s.sum_full, (tile - slot) * TT + 1)
                for b, m in segments:
                    act.activation(act_hi[:, slot, b:b + m], conv[:, padded(b):padded(b) + m], ACT.Copy)\
                       .then_inc(s.act_hi_done, 1)

            schedule(act, split, idle, gate_work, idle, value_work, idle)

        @block.vector
        def _(dve):
            dve.memset(gate[:, :], 0.0).then_inc(s.zeroed, 1)
            dve.memset(y_sum[:, 0:TT, :], 0.0).then_inc(s.zeroed, 1)
            dve.wait_ge(s.zeroed, 2)
            dve.sem_inc(s.sum_done, SUMS)
            dve.wait_ge(s.taps_in, 64)

            def split(kind, tile, piece, back):
                dve.wait_ge(s.w_hi_done, piece + 1)
                dve.tensor_tensor(w_lo[:, kind, :], raw[:, kind, :], w_hi[:, kind, :].bitcast(F32),
                                  ALU.subtract).then_inc(s.w_ready, 1)

            def gate_work(tile):
                dve.wait_ge(s.gate_in, tile * NC + NC)
                if not (isinstance(tile, int) and tile == 0):
                    dve.wait_ge(s.act_ready, tile * NS)
                before, here, after, bias = (taps[:, j, bass.ds(tile, 1)] for j in range(4))
                inner = conv[:, 1:PAD - 1]
                dve.tensor_scalar(inner, gate[:, 1:PAD - 1], here, bias, ALU.mult, ALU.add)\
                   .then_inc(s.conv_step, 1)
                dve.wait_ge(s.conv_step, tile * 2 + 1)
                dve.scalar_tensor_tensor(out=inner, in0=gate[:, 0:PAD - 2], scalar=before, in1=inner,
                                         op0=ALU.mult, op1=ALU.add).then_inc(s.conv_step, 1)
                dve.wait_ge(s.conv_step, tile * 2 + 2)
                dve.scalar_tensor_tensor(out=inner, in0=gate[:, 2:PAD], scalar=after, in1=inner,
                                         op0=ALU.mult, op1=ALU.add).then_inc(s.conv_done, 1)

            def value_work(tile, slot):
                dve.wait_ge(s.silu_done, tile + 1)
                for c, (a, n) in enumerate(chunks):
                    dve.wait_ge(s.val_full, tile * NC + (c + 1))
                    part = conv[:, padded(a):padded(a) + n]
                    dve.tensor_tensor(part, val_ps[:, c, 0:n], part, ALU.mult).then_inc(s.val_used, 1)
                for i, (b, m) in enumerate(segments):
                    dve.wait_ge(s.act_hi_done, tile * NS + (i + 1))
                    dve.tensor_tensor(act_lo[:, slot, b:b + m], conv[:, padded(b):padded(b) + m],
                                      act_hi[:, slot, b:b + m].bitcast(F32), ALU.subtract)\
                       .then_inc(s.act_ready, 1)

            def down(group, piece):
                for t in range(TT):
                    for half in range(2):
                        n = t * 2 + half
                        dve.wait_ge(s.sum_full, group * SUMS + (n + 2))
                        dve.wait_ge(s.sum_done, group * SUMS + (n + 1))
                        part = y_sum[:, t, half * BANK:(half + 1) * BANK]
                        dve.tensor_tensor(part, down_ps[:, half, :], part, ALU.add).then_inc(s.sum_done, 1)

            schedule(dve, split, idle, gate_work, idle, value_work, down)

        @block.tensor
        def _(pe):
            pe.sem_inc(s.sum_full, 1)

            def product(kind, bank, full, used, tile, piece):
                pe.wait_ge(s.w_ready, piece + 1)
                for c, (a, n) in enumerate(chunks):
                    if not (isinstance(tile, int) and tile == 0):
                        pe.wait_ge(used, (tile - 1) * NC + (c + 1))
                    for k in range(KD):
                        w = slice(k * P, (k + 1) * P)
                        mm = exact_product(pe, bank[:, c, 0:n], w_hi[:, kind, w], w_lo[:, kind, w],
                                           h_hi[:, k, a:a + n], h_lo[:, k, a:a + n],
                                           k == 0, k == KD - 1)
                    mm.then_inc(full, 1)

            def gate_product(tile, piece):
                product(GATE, gate_ps, s.gate_full, s.gate_in, tile, piece)

            def value_product(tile, piece):
                product(VALUE, val_ps, s.val_full, s.val_used, tile, piece)

            def down(group, piece):
                pe.wait_ge(s.w_ready, piece + 1)
                pe.wait_ge(s.act_ready, (group * 2 + 2) * NS)
                for t in range(TT):
                    for half in range(2):
                        n = t * 2 + half
                        pe.wait_ge(s.sum_done, (group + 1) * SUMS + (n - 1))
                        for j in range(2):
                            mm = exact_product(pe, down_ps[:, half, :],
                                               act_hi[:, j, t * P:(t + 1) * P],
                                               act_lo[:, j, t * P:(t + 1) * P],
                                               w_hi[:, DOWN0 + j, half * BANK:(half + 1) * BANK],
                                               w_lo[:, DOWN0 + j, half * BANK:(half + 1) * BANK],
                                               j == 0, j == 1)
                        mm.then_inc(s.sum_full, 1)

            schedule(pe, idle, gate_product, idle, value_product, idle, down)


QP = 2


class Fills:

    def __init__(self, groups):
        self.turned, self.product = [], []
        units, n = len(groups), 0
        for u in range(units + 1):
            if u < units:
                self.turned.append(list(range(n, n + len(groups[u]))))
                n += len(groups[u])
            if u and u % QP == 0:
                self.product.append(n)
                n += 1
        self.count = n
        self.turns_before = [sum(len(g) for g in groups[:u]) for u in range(units)]
        self.turns = n - len(self.product)


def diff_attention(nc, o_heads, qk, v_rows, lam_vecs, ident):
    KT = T // P
    chunks = token_chunks(T)
    units = [(u, 0) for u in range(XT)] + [(u, XT) for u in range(XT, TT)]
    NU = len(units)
    groups = [[list(range(a, min(a + 4, KT))) for a in range(k0, KT, 4)] for _, k0 in units]
    fills = Fills(groups)
    FILLS, TURNS, PAIRS = fills.count, fills.turns, NU // QP

    def product_fill(h, pair):
        return h * FILLS + (pair // PAIRS * FILLS + fills.product[pair % PAIRS])

    with ExitStack() as ctx:
        def sb(label, shape, dt=F32):
            return ctx.enter_context(nc.sbuf_tensor(f"da_{label}", shape, dt))

        raw = sb("raw", [P, 2, T])
        q_top = sb("q_top", [P, T], F32R)
        q_st = sb("q_stacked", [P, 2, 2, T], F32R)
        k_hi = sb("k_hi", [P, 2, 2, T], F32R)
        k_lo = sb("k_lo", [P, 2, 2, T], F32R)
        v_hi = sb("v_hi", [P, 2, KT, P], F32R)
        v_lo = sb("v_lo", [P, 2, KT, P], F32R)
        e1 = sb("e1", [P, 2, T])
        e2 = sb("e2", [P, 2, T])
        pt_hi = sb("pt_hi", [P, 2, KT, QP * P], F32R)
        pt_lo = sb("pt_lo", [P, 2, KT, QP * P], F32R)
        o_t = sb("o", [P, 2, QP * P])
        lam_t = sb("lam", [P, 4, B_DIM])
        lam_prod = sb("lam_prod", [P, 2, B_DIM])
        lam_small = sb("lam_small", [P, 8])
        stats = sb("stats", [P, 2, 8])
        s_ps = ctx.enter_context(nc.psum_tensor("da_scores", [P, 2, 3 * BANK], F32))
        t_ps = ctx.enter_context(nc.psum_tensor("da_turned", [P, 2, BANK], F32))
        s = ctx.enter_context(stage(nc, "da", [
            "lam_in", "raw0_in", "raw1_in", "asked", "lam_step", "lam_exp", "lam_done", "raw_hi", "raw_split",
            "s1_full", "s2_full", "max1", "max2", "exp1", "exp2", "scale_step", "scale_done", "p_step", "p_done",
            "t_full", "t_hi", "t_lo", "o0_stored", "o1_stored", "o_free"],
            {"raw_split": 2, "exp1": 1, "exp2": 1, "max1": 2, "max2": 2, "p_done": 2, "t_full": FILLS + 1,
             "t_hi": 2, "t_lo": 2, "o_free": 2, "scale_done": 2, "p_step": 2,
             "s1_full": 1, "s2_full": 1}))
        raw_in = [s.raw0_in, s.raw1_in]
        o_stored = [s.o0_stored, s.o1_stored]
        block = ctx.enter_context(nc.Block())
        PIECES = 5

        FIRST_SPLIT = 3

        def heads(eng, one_head):
            for h in range(B_HEADS):
                one_head(h // 2, h % 2, h)

        @block.sync
        def _(sp):
            sp.dma_start(lam_t[:, :, :].rearrange("p a d -> p (a d)"), row(lam_vecs.rearrange("a d -> (a d)")))\
              .then_inc(s.lam_in.sem, 16)

            def one_head(i, j, h):
                for n in range(PIECES):
                    piece = h * PIECES + n
                    slot = (j * PIECES + n) % 2
                    sp.wait_ge(s.raw_split.sem, s.raw_split.nth(piece - 2))
                    sp.sem_inc(s.asked.sem, 1)
                    if n < 4:
                        first = i * (4 * B_DIM) + (j * 2 * B_DIM + (n // 2) * B_HEADS * 2 * B_DIM + n % 2 * B_DIM)
                        for half in range(2):
                            sp.dma_start(raw[half * B_DIM:(half + 1) * B_DIM, slot, :],
                                         qk[bass.ds(first, B_DIM), :]).then_inc(raw_in[slot].sem, 16)
                    else:
                        first = i * (2 * P) + j * P
                        sp.dma_start(raw[:, slot, :].rearrange("p (t n) -> p t n", n=P),
                                     v_rows.rearrange("(t p) n -> p t n", p=P)[:, :, bass.ds(first, P)])\
                          .then_inc(raw_in[slot].sem, 16)

            heads(sp, one_head)

        def loads_done(i, j, n):
            def dmas(k):
                slot = (j * PIECES + n) % 2
                return sum((1 if m % PIECES == 4 else 2) for m in range(k) if m % 2 == slot)
            return i * (16 * dmas(2 * PIECES)) + 16 * dmas(j * PIECES + n + 1)

        @block.scalar
        def _(act):
            start_ahead(act, s.exp1, s.exp2, s.t_hi)
            act.wait_ge(s.lam_step.sem, 2)
            act.activation(lam_small[:, 2:4], lam_small[:, 0:2], ACT.Exp).then_inc(s.lam_exp.sem, 1)

            def first_half(h, n):
                i, j = h // 2, h % 2
                slot = (j * PIECES + n) % 2
                act.wait_ge(raw_in[slot].sem, loads_done(i, j, n))
                act.wait_ge(s.t_full.sem, s.t_full.nth(product_fill(h, -PAIRS - 1)))
                half = n % 2
                if n < 2:
                    act.activation(q_st[0:B_DIM, j, half, :], raw[0:B_DIM, slot, :], ACT.Copy)
                    act.wait_ge(s.raw_split.sem, s.raw_split.nth(h * PIECES + n - 1))
                    act.activation(q_top[B_DIM:P, :], raw[B_DIM:P, slot, :], ACT.Copy).then_inc(s.raw_hi.sem, 1)
                else:
                    dst = k_hi[:, j, half, :] if n < 4 else v_hi[:, j, :, :].rearrange("p t n -> p (t n)")
                    act.activation(dst, raw[:, slot, :], ACT.Copy).then_inc(s.raw_hi.sem, 1)

            def one_head(i, j, h):
                for u in range(NU + 1):
                    if u >= 1:
                        turn_copy(j, h, u - 1, 0)
                    if u < NU:
                        exponentials(h, u, e1, 2, s.max1, s.exp1, 0)
                    if u >= 1 and len(groups[u - 1]) > 1:
                        turn_copy(j, h, u - 1, 1)
                    if u < NU:
                        exponentials(h, u, e2, 3, s.max2, s.exp2, 1)
                    if u >= 1 and len(groups[u - 1]) > 2:
                        turn_copy(j, h, u - 1, 2)
                    if 0 <= u - FIRST_SPLIT < PIECES and h + 1 < B_HEADS:
                        first_half(h + 1, u - FIRST_SPLIT)

            def exponentials(h, u, e, sums, mx, done, half):
                n = h * NU + u
                first = units[u][1] * P
                act.wait_ge(s.p_done.sem, s.p_done.nth(n - 2))
                if u >= 2:
                    act.wait_ge(s.t_full.sem, s.t_full.nth(h * FILLS + fills.turned[u - 2][-1]))
                else:
                    act.wait_ge(s.t_full.sem, s.t_full.nth(h * FILLS - 1))
                act.wait_ge(mx.sem, mx.nth(n))
                act.activation(e[:, u % 2, first:T], s_ps[:, half, first:T], ACT.Exp, scale=B_DIM ** -0.5,
                               bias=stats[:, u % 2, half:half + 1],
                               accum_out=stats[:, u % 2, sums:sums + 1]).then_inc(done.sem, 1)

            def turn_copy(j, h, u, f):
                pair = u // QP
                slot = (j * PAIRS + pair) % 2
                group, n = groups[u][f], fills.turned[u][f]
                act.wait_ge(s.t_full.sem, s.t_full.nth(h * FILLS + n))
                if f == 0 and u % QP == 0:
                    act.wait_ge(s.t_full.sem, s.t_full.nth(product_fill(h, pair - 2)))
                act.activation(pt_hi[:, slot, group[0]:group[-1] + 1, u % QP * P:(u % QP + 1) * P],
                               t_ps[:, (j * FILLS + n) % 2, 0:len(group) * P]
                               .rearrange("p (k n) -> p k n", n=P), ACT.Copy).then_inc(s.t_hi.sem, 1)

            for n in range(PIECES):
                first_half(0, n)
            heads(act, one_head)

        @block.vector
        def _(dve):
            start_ahead(dve, s.raw_split, s.max1, s.max2, s.scale_done, s.p_step, s.p_done, s.t_lo)
            dve.wait_ge(s.lam_in.sem, 16)
            for a in range(2):
                dve.tensor_tensor_reduce(lam_prod[:, a, :], lam_t[:, 2 * a, :], lam_t[:, 2 * a + 1, :], 1.0, 0.0,
                                         ALU.mult, ALU.add, lam_small[:, a:a + 1]).then_inc(s.lam_step.sem, 1)
            dve.wait_ge(s.lam_exp.sem, 1)
            dve.tensor_tensor(lam_small[:, 4:5], lam_small[:, 3:4], lam_small[:, 2:3], ALU.subtract)\
               .then_inc(s.lam_step.sem, 1)
            dve.wait_ge(s.lam_step.sem, 3)
            dve.tensor_scalar(lam_small[:, 5:6], lam_small[:, 4:5], -LAMBDA_INIT, None, ALU.add)\
               .then_inc(s.lam_done.sem, 1)
            dve.wait_ge(s.lam_done.sem, 1)

            def second_half(h, n):
                j = h % 2
                slot = (j * PIECES + n) % 2
                half = n % 2
                dve.wait_ge(s.raw_hi.sem, s.raw_hi.nth(h * PIECES + n))
                if n < 2:
                    ins = dve.tensor_tensor(q_st[B_DIM:P, j, half, :], raw[B_DIM:P, slot, :],
                                            q_top[B_DIM:P, :].bitcast(F32), ALU.subtract)
                elif n < 4:
                    ins = dve.tensor_tensor(k_lo[:, j, half, :], raw[:, slot, :],
                                            k_hi[:, j, half, :].bitcast(F32), ALU.subtract)
                else:
                    ins = dve.tensor_tensor(v_lo[:, j, :, :].rearrange("p t n -> p (t n)"), raw[:, slot, :],
                                            v_hi[:, j, :, :].rearrange("p t n -> p (t n)").bitcast(F32),
                                            ALU.subtract)
                ins.then_inc(s.raw_split.sem, 1)

            def one_head(i, j, h):
                for u in range(NU + 1):
                    if u < NU:
                        maxima(h, u)
                    if u >= 1:
                        turn_halves(j, h, u - 1)
                    if u < NU:
                        combine(h, u)
                    if u >= 3 and (u - 1) % QP == 0:
                        output(j, h, (u - 1) // QP - 1)
                    if 0 <= u - FIRST_SPLIT < PIECES and h + 1 < B_HEADS:
                        second_half(h + 1, u - FIRST_SPLIT)
                output(j, h, PAIRS - 1)

            def turn_halves(j, h, u):
                slot = (j * PAIRS + u // QP) % 2
                cols = slice(u % QP * P, (u % QP + 1) * P)
                for f, (group, n) in enumerate(zip(groups[u], fills.turned[u])):
                    dve.wait_ge(s.t_hi.sem, s.t_hi.nth(h * TURNS + (fills.turns_before[u] + f)))
                    dve.tensor_tensor(pt_lo[:, slot, group[0]:group[-1] + 1, cols],
                                      t_ps[:, (j * FILLS + n) % 2, 0:len(group) * P]
                                      .rearrange("p (k n) -> p k n", n=P),
                                      pt_hi[:, slot, group[0]:group[-1] + 1, cols].bitcast(F32),
                                      ALU.subtract).then_inc(s.t_lo.sem, 1)

            def output(j, h, pair):
                n, slot = fills.product[pair], (j * PAIRS + pair) % 2
                dve.wait_ge(s.t_full.sem, s.t_full.nth(h * FILLS + n))
                dve.wait_ge(s.o_free.sem, s.o_free.nth(h * PAIRS + (pair - 2)))
                dve.tensor_copy(o_t[:, slot, :], t_ps[:, (j * FILLS + n) % 2, 0:QP * P])\
                   .then_inc(s.t_lo.sem, 1)

            def maxima(h, u):
                n = h * NU + u
                first = units[u][1] * P
                st = stats[:, u % 2, :]
                dve.wait_ge(s.p_done.sem, s.p_done.nth(n - 2))
                for half, full, mx in ((0, s.s1_full, s.max1), (1, s.s2_full, s.max2)):
                    dve.wait_ge(full.sem, full.nth(n))
                    dve.tensor_reduce(st[:, 4 + half:5 + half], s_ps[:, half, first:T], AX.X, ALU.max)\
                       .then_inc(s.scale_step.sem, 1)
                    dve.wait_ge(s.scale_step.sem, s.scale_step.nth(n * 4 + half))
                    dve.tensor_scalar(st[:, half:half + 1], st[:, 4 + half:5 + half], -(B_DIM ** -0.5), None,
                                      ALU.mult).then_inc(mx.sem, 1)

            def combine(h, u):
                n = h * NU + u
                first = units[u][1] * P
                st = stats[:, u % 2, :]
                dve.wait_ge(s.exp1.sem, s.exp1.nth(n))
                dve.wait_ge(s.exp2.sem, s.exp2.nth(n))
                dve.reciprocal(st[:, 6:8], st[:, 2:4]).then_inc(s.scale_step.sem, 1)
                dve.wait_ge(s.scale_step.sem, s.scale_step.nth(n * 4 + 2))
                dve.tensor_scalar(st[:, 7:8], st[:, 7:8], lam_small[:, 5:6], None, ALU.mult)\
                   .then_inc(s.scale_step.sem, 1)
                dve.wait_ge(s.scale_step.sem, s.scale_step.nth(n * 4 + 3))
                a, b = e1[:, u % 2, first:T], e2[:, u % 2, first:T]
                dve.tensor_scalar(b, b, st[:, 7:8], None, ALU.mult).then_inc(s.p_step.sem, 1)
                dve.wait_ge(s.p_step.sem, s.p_step.nth(n))
                dve.scalar_tensor_tensor(out=a, in0=a, scalar=st[:, 6:7], in1=b, op0=ALU.mult, op1=ALU.add)\
                   .then_inc(s.p_done.sem, 1)

            for n in range(PIECES):
                second_half(0, n)
            heads(dve, one_head)

        @block.gpsimd
        def _(pool):
            start_ahead(pool, s.o_free)

            def one_head(i, j, h):
                for pair in range(PAIRS):
                    slot = (j * PAIRS + pair) % 2
                    pool.wait_ge(s.t_lo.sem, s.t_lo.nth(product_fill(h, pair)))
                    pool.sem_inc(s.asked.sem, 1)
                    pool.dma_start(o_heads[bass.ds(i * (2 * P) + j * P, P), pair * QP * P:(pair + 1) * QP * P],
                                   o_t[:, slot, :]).then_inc(o_stored[slot].sem, 16)
                    if pair >= 1:
                        stored(i, j, pair - 1)
                stored(i, j, PAIRS - 1)

            def stored(i, j, pair):
                n = j * PAIRS + pair
                pool.wait_ge(o_stored[n % 2].sem, o_stored[n % 2].nth(i * PAIRS + n // 2))
                pool.sem_inc(s.o_free.sem, 1)

            heads(pool, one_head)

        @block.tensor
        def _(pe):
            start_ahead(pe, s.s1_full, s.s2_full, s.t_full)

            def one_head(i, j, h):
                pe.wait_ge(s.raw_split.sem, s.raw_split.nth(h * PIECES + PIECES - 1))
                for u in range(NU + 1):
                    if u < NU:
                        scores(j, h, u)
                    if u >= 1:
                        turned(j, h, u - 1)
                    if u >= 3 and (u - 1) % QP == 0:
                        product(j, h, (u - 1) // QP - 1)
                product(j, h, PAIRS - 1)

            def scores(j, h, u):
                n = h * NU + u
                for half, full, exp in ((0, s.s1_full, s.exp1), (1, s.s2_full, s.exp2)):
                    pe.wait_ge(exp.sem, exp.nth(n - 1))
                    q = q_st[:, j, half, u * P:(u + 1) * P]
                    for a, m in chunks:
                        if a + m <= units[u][1] * P:
                            continue
                        pe.matmul(s_ps[:, half, a:a + m], q, k_hi[:, j, half, a:a + m], start=True, stop=False)
                        mm = pe.matmul(s_ps[:, half, a:a + m], q, k_lo[:, j, half, a:a + m],
                                       start=False, stop=True)
                    mm.then_inc(full.sem, 1)

            def turned(j, h, u):
                pe.wait_ge(s.p_done.sem, s.p_done.nth(h * NU + u))
                for group, n in zip(groups[u], fills.turned[u]):
                    pe.wait_ge(s.t_lo.sem, s.t_lo.nth(h * FILLS + (n - 2)))
                    for g, kt in enumerate(group):
                        mm = pe.transpose(t_ps[:, (j * FILLS + n) % 2, g * P:(g + 1) * P],
                                          e1[:, u % 2, kt * P:(kt + 1) * P], ident[:, :])
                    mm.then_inc(s.t_full.sem, 1)

            def product(j, h, pair):
                n, slot = fills.product[pair], (j * PAIRS + pair) % 2
                last = fills.turned[pair * QP + QP - 1][-1]
                pe.wait_ge(s.t_lo.sem, s.t_lo.nth(h * FILLS + max(n - 2, last)))
                keys = list(range(units[pair * QP][1], KT))
                for kt in keys:
                    mm = exact_product(pe, t_ps[:, (j * FILLS + n) % 2, 0:QP * P], v_hi[:, j, kt, :],
                                       v_lo[:, j, kt, :], pt_hi[:, slot, kt, :], pt_lo[:, slot, kt, :],
                                       kt == keys[0], kt == keys[-1])
                mm.then_inc(s.t_full.sem, 1)

            heads(pe, one_head)


class OutWeights:

    SIGNALS = ["w0_in", "w1_in", "w_hi_done", "w_ready"]

    def __init__(self, nc, ctx, name, w_out):
        self.w_out = w_out
        self.hi = ctx.enter_context(nc.sbuf_tensor(f"{name}_w_hi", [P, KD, D], F32R))
        self.lo = ctx.enter_context(nc.sbuf_tensor(f"{name}_w_lo", [P, KD, D], F32R))
        self.raw = ctx.enter_context(nc.sbuf_tensor(f"{name}_raw", [P, 2, D], F32))

    def load(self, sp, s, k):
        if k >= 2:
            sp.wait_ge(s.w_ready.sem, k - 1)
        sp.dma_start(self.raw[:, k % 2, :], self.w_out[k * P:(k + 1) * P, :])\
          .then_inc((s.w0_in, s.w1_in)[k % 2].sem, 16)

    def split_scalar(self, act, s, k):
        act.wait_ge((s.w0_in, s.w1_in)[k % 2].sem, 16 * (k // 2 + 1))
        act.activation(self.hi[:, k, :], self.raw[:, k % 2, :], ACT.Copy).then_inc(s.w_hi_done.sem, 1)

    def split_vector(self, dve, s, k):
        dve.wait_ge(s.w_hi_done.sem, k + 1)
        dve.tensor_tensor(self.lo[:, k, :], self.raw[:, k % 2, :], self.hi[:, k, :].bitcast(F32), ALU.subtract)\
           .then_inc(s.w_ready.sem, 1)


def join_conv_diff(nc, y_hi, y_lo, conv_out, o_heads, ln_g, ln_b, subln, weights):
    CHUNK = 256
    chunks = [(a, CHUNK) for a in range(0, T, CHUNK)]
    shares = [range(2 * c, min(2 * c + 2, KD)) for c in range(len(chunks))]
    AT = A_WIDTH // P
    with ExitStack() as ctx:
        def sb(label, shape, dt=F32):
            return ctx.enter_context(nc.sbuf_tensor(f"join_{label}", shape, dt))

        u = sb("u", [P, 2, AT, CHUNK])
        o = sb("o", [P, 2, B_HEADS, CHUNK])
        u_sq = sb("u_sq", [P, 2, AT, CHUNK])
        o_sq = sb("o_sq", [P, 2, B_HEADS, CHUNK])
        std = sb("std", [P, 1 + B_HEADS, CHUNK])
        ones = sb("ones", [P, P])
        eps = sb("eps", [P, 2])
        gains = sb("gains", [P, 2 * AT + 1])
        ps = ctx.enter_context(nc.psum_tensor("join_ps", [P, 2 + B_HEADS, BANK], F32))
        s = ctx.enter_context(stage(nc, "join", [
            "small_in", "set", "subln_scaled", "u0_in", "u1_in", "o0_in", "o1_in", "sum_full", "centred", "u_squared",
            "o_squared", "var_full", "ms_full", "u_std", "o_std", "u_rstd", "o_rstd", "u_normed", "o_normed",
            "silu_done", "y_hi", "y_lo"] + OutWeights.SIGNALS))
        u_in, o_in = [s.u0_in, s.u1_in], [s.o0_in, s.o1_in]
        block = ctx.enter_context(nc.Block())

        @block.sync
        def _(sp):
            sp.dma_start(gains[:, 0:AT], column(ln_g), allow_slow_non_contiguous=True).then_inc(s.small_in.sem, 16)
            sp.dma_start(gains[:, AT:2 * AT], column(ln_b), allow_slow_non_contiguous=True)\
              .then_inc(s.small_in.sem, 16)
            sp.dma_start(gains[:, 2 * AT:], column(subln)).then_inc(s.small_in.sem, 16)
            for c, (a, n) in enumerate(chunks):
                if c >= 2:
                    sp.wait_ge(s.y_lo.sem, 8 * (c - 1))
                sp.dma_start(u[:, c % 2, :, 0:n], conv_out.rearrange("(k p) n -> p k n", p=P)[:, :, a:a + n])\
                  .then_inc(u_in[c % 2].sem, 16)
                sp.dma_start(o[:, c % 2, :, 0:n], o_heads.rearrange("(k p) n -> p k n", p=P)[:, :, a:a + n])\
                  .then_inc(o_in[c % 2].sem, 16)
                for k in shares[c]:
                    weights.load(sp, s, k)

        @block.tensor
        def _(pe):
            pe.wait_ge(s.set.sem, 1)
            for c, (a, n) in enumerate(chunks):
                b = c % 2
                pe.wait_ge(u_in[b].sem, 16 * (c // 2 + 1))
                if c:
                    pe.wait_ge(s.centred.sem, AT * c)
                for k in range(AT):
                    mm = pe.matmul(ps[:, 0, 0:n], ones[:, :], u[:, b, k, 0:n], start=k == 0, stop=k == AT - 1)
                mm.then_inc(s.sum_full.sem, 1)
                for k in range(B_HEADS):
                    pe.wait_ge(s.o_squared.sem, B_HEADS * c + k + 1)
                    if c:
                        pe.wait_ge(s.o_std.sem, B_HEADS * (c - 1) + k + 1)
                    pe.matmul(ps[:, 2 + k, 0:n], ones[:, :], o_sq[:, b, k, 0:n], start=True, stop=True)\
                      .then_inc(s.ms_full.sem, 1)
                if c:
                    pe.wait_ge(s.u_std.sem, c)
                for k in range(AT):
                    pe.wait_ge(s.u_squared.sem, AT * c + k + 1)
                    mm = pe.matmul(ps[:, 1, 0:n], ones[:, :], u_sq[:, b, k, 0:n], start=k == 0, stop=k == AT - 1)
                mm.then_inc(s.var_full.sem, 1)

        @block.scalar
        def _(act):
            act.wait_ge(s.small_in.sem, 48)
            act.wait_ge(s.set.sem, 3)
            for c, (a, n) in enumerate(chunks):
                b = c % 2
                act.wait_ge(o_in[b].sem, 16 * (c // 2 + 1))
                if c >= 2:
                    act.wait_ge(s.y_lo.sem, 8 * (c - 1))
                for k in range(B_HEADS):
                    act.activation(o_sq[:, b, k, 0:n], o[:, b, k, 0:n], ACT.Square).then_inc(s.o_squared.sem, 1)
                for k in range(AT):
                    act.wait_ge(s.centred.sem, AT * c + k + 1)
                    act.activation(u_sq[:, b, k, 0:n], u[:, b, k, 0:n], ACT.Square).then_inc(s.u_squared.sem, 1)
                for k in range(B_HEADS):
                    act.wait_ge(s.ms_full.sem, B_HEADS * c + k + 1)
                    if c:
                        act.wait_ge(s.o_normed.sem, B_HEADS * (c - 1) + k + 1)
                    act.activation(std[:, 1 + k, 0:n], ps[:, 2 + k, 0:n], ACT.Sqrt, scale=1.0 / P,
                                   bias=eps[:, 1:2]).then_inc(s.o_std.sem, 1)
                act.wait_ge(s.var_full.sem, c + 1)
                if c:
                    act.wait_ge(s.u_normed.sem, AT * c)
                act.activation(std[:, 0, 0:n], ps[:, 1, 0:n], ACT.Sqrt, scale=1.0 / A_WIDTH, bias=eps[:, 0:1])\
                   .then_inc(s.u_std.sem, 1)
                for k in range(B_HEADS):
                    act.wait_ge(s.o_normed.sem, B_HEADS * c + k + 1)
                    act.activation(y_hi[:, AT + k, a:a + n], o[:, b, k, 0:n], ACT.Copy).then_inc(s.y_hi.sem, 1)
                for k in range(AT):
                    act.wait_ge(s.u_normed.sem, AT * c + k + 1)
                    act.activation(u_sq[:, b, k, 0:n], u[:, b, k, 0:n], ACT.Silu, scale=gains[:, k:k + 1],
                                   bias=gains[:, AT + k:AT + k + 1]).then_inc(s.silu_done.sem, 1)
                for k in range(AT):
                    act.wait_ge(s.silu_done.sem, AT * c + k + 1)
                    act.activation(y_hi[:, k, a:a + n], u_sq[:, b, k, 0:n], ACT.Copy).then_inc(s.y_hi.sem, 1)
                for k in shares[c]:
                    weights.split_scalar(act, s, k)

        @block.vector
        def _(dve):
            dve.memset(ones[:, :], 1.0).then_inc(s.set.sem, 1)
            dve.memset(eps[:, 0:1], LN_EPS).then_inc(s.set.sem, 1)
            dve.memset(eps[:, 1:2], RMS_EPS).then_inc(s.set.sem, 1)
            dve.wait_ge(s.small_in.sem, 48)
            dve.tensor_scalar(gains[:, 2 * AT:], gains[:, 2 * AT:], 1.0 - LAMBDA_INIT, None, ALU.mult)\
               .then_inc(s.subln_scaled.sem, 1)
            dve.wait_ge(s.subln_scaled.sem, 1)
            for c, (a, n) in enumerate(chunks):
                b = c % 2
                dve.wait_ge(s.sum_full.sem, c + 1)
                for k in range(AT):
                    part = u[:, b, k, 0:n]
                    dve.scalar_tensor_tensor(out=part, in0=ps[:, 0, 0:n], scalar=-1.0 / A_WIDTH, in1=part,
                                             op0=ALU.mult, op1=ALU.add).then_inc(s.centred.sem, 1)
                for k in range(B_HEADS):
                    dve.wait_ge(s.o_std.sem, B_HEADS * c + k + 1)
                    dve.reciprocal(std[:, 1 + k, 0:n], std[:, 1 + k, 0:n]).then_inc(s.o_rstd.sem, 1)
                for k in range(B_HEADS):
                    dve.wait_ge(s.o_rstd.sem, B_HEADS * c + k + 1)
                    part = o[:, b, k, 0:n]
                    dve.scalar_tensor_tensor(out=part, in0=part, scalar=gains[:, 2 * AT:], in1=std[:, 1 + k, 0:n],
                                             op0=ALU.mult, op1=ALU.mult).then_inc(s.o_normed.sem, 1)
                dve.wait_ge(s.u_std.sem, c + 1)
                dve.reciprocal(std[:, 0, 0:n], std[:, 0, 0:n]).then_inc(s.u_rstd.sem, 1)
                dve.wait_ge(s.u_rstd.sem, c + 1)
                for k in range(AT):
                    part = u[:, b, k, 0:n]
                    dve.tensor_tensor(part, part, std[:, 0, 0:n], ALU.mult).then_inc(s.u_normed.sem, 1)
                for m in range(8):
                    dve.wait_ge(s.y_hi.sem, 8 * c + m + 1)
                    k, src = (AT + m, o) if m < B_HEADS else (m - B_HEADS, u_sq)
                    dve.tensor_tensor(y_lo[:, k, a:a + n], src[:, b, k % AT, 0:n],
                                      y_hi[:, k, a:a + n].bitcast(F32), ALU.subtract).then_inc(s.y_lo.sem, 1)
                for k in shares[c]:
                    weights.split_vector(dve, s, k)


def project_out(nc, name, y_hi, y_lo, tokens, weights, post, pre, x_old, x_new, ident):
    N = tokens // P
    with ExitStack() as ctx:
        w_hi, w_lo = weights.hi, weights.lo
        y = weights.raw
        ps = ctx.enter_context(nc.psum_tensor(f"{name}_ps", [P, 2, D], F32))
        s = ctx.enter_context(stage(nc, name, TokenTail.SIGNALS + ["y_full", "y_copied"]))
        tail = TokenTail(nc, ctx, name, s, post, pre, 2 if tokens > SEQ else 1, N, ident)
        block = ctx.enter_context(nc.Block())

        @block.sync
        def _(sp):
            tail.load_rows(sp)
            for t in range(2):
                tail.load_x(sp, t, x_old(t))
            for t in range(N):
                tail.store_x(sp, t, x_new(t))
                if t + 2 < N:
                    tail.load_x(sp, t + 2, x_old(t + 2))
            tail.stores_over(sp)

        @block.tensor
        def _(pe):
            for t in range(N + 2):
                if t < N:
                    if t >= 2:
                        pe.wait_ge(s.y_copied.sem, t - 1)
                    for half in range(2):
                        cols = slice(half * BANK, (half + 1) * BANK)
                        for k in range(KD):
                            rows = slice(t * P, (t + 1) * P)
                            mm = exact_product(pe, ps[:, t % 2, cols], y_hi[:, k, rows], y_lo[:, k, rows],
                                               w_hi[:, k, cols], w_lo[:, k, cols], k == 0, k == KD - 1)
                    mm.then_inc(s.y_full.sem, 1)
                if t >= 2:
                    tail.turn_tensor(pe, t - 2)

        @block.scalar
        def _(act):
            act.wait_ge(s.gs_done.sem, tail.kinds * 2)
            for t in range(N + 2):
                if t < N:
                    act.wait_ge(s.y_full.sem, t + 1)
                    if t >= 2:
                        act.wait_ge(s.x_new.sem, t - 1)
                    act.activation(y[:, t % 2, :], ps[:, t % 2, :], ACT.Copy).then_inc(s.y_copied.sem, 1)
                    act.wait_ge(s.y_copied.sem, t + 1)
                    tail.post_scalar(act, t, y[:, t % 2, :])
                if 1 <= t < N + 1:
                    tail.pre_scalar(act, t - 1)
                if t >= 2:
                    tail.split_scalar(act, t - 2, y_hi[:, :, (t - 2) * P:(t - 1) * P])

        @block.vector
        def _(dve):
            tail.prepare_rows(dve)
            for t in range(N + 2):
                if t < N:
                    tail.post_vector(dve, t, t, y[:, t % 2, :])
                if 1 <= t < N + 1:
                    tail.pre_vector(dve, t - 1, t - 1)
                if t >= 2:
                    rows = slice((t - 2) * P, (t - 1) * P)
                    tail.split_vector(dve, t - 2, y_hi[:, :, rows], y_lo[:, :, rows])

        @block.gpsimd
        def _(pool):
            tail.prepare_gpsimd(pool)
            for t in range(N + 1):
                if t < N:
                    tail.post_gpsimd(pool, t)
                if t >= 1:
                    tail.pre_gpsimd(pool, t - 1)


def last_residual(nc, y_sum, post, x_old, out):
    with ExitStack() as ctx:
        s = ctx.enter_context(stage(nc, "last", TokenTail.SIGNALS))
        tail = TokenTail(nc, ctx, "last", s, post, None, 1, XT, None)
        block = ctx.enter_context(nc.Block())

        @block.sync
        def _(sp):
            tail.load_rows(sp)
            for t in range(2):
                tail.load_x(sp, t, x_old(t))
            for t in range(XT):
                tail.store_x(sp, t, out[t * P:(t + 1) * P, :])
                if t + 2 < XT:
                    tail.load_x(sp, t + 2, x_old(t + 2))
            tail.stores_over(sp)

        @block.scalar
        def _(act):
            for t in range(XT):
                tail.post_scalar(act, t, y_sum[:, t, :])

        @block.vector
        def _(dve):
            tail.prepare_rows(dve)
            for t in range(XT):
                tail.post_vector(dve, t, t, y_sum[:, t, :])

        @block.gpsimd
        def _(pool):
            tail.prepare_gpsimd(pool)
            for t in range(XT):
                tail.post_gpsimd(pool, t)


def project_latents(nc, y_sum, post, pre, x_old, x_new, w_in, q_gain, kv_gain, cq, ckv, k_pe, ident):
    N = TT
    splits = ((0, BANK), (BANK, C_Q_RANK - BANK), (C_Q_RANK, C_IN - C_Q_RANK))
    LATENTS = C_Q_RANK + C_KV_RANK
    LT = LATENTS // P
    QT = C_Q_RANK // P
    groups = ((0, 4), (4, LT), (LT, LT + 1))
    with ExitStack() as ctx:
        def sb(label, shape, dt=F32):
            return ctx.enter_context(nc.sbuf_tensor(f"lat_{label}", shape, dt))

        w_hi = sb("w_hi", [P, KD, C_IN], F32R)
        w_lo = sb("w_lo", [P, KD, C_IN], F32R)
        h_hi = sb("h_hi", [P, 2, KD, P], F32R)
        h_lo = sb("h_lo", [P, 2, KD, P], F32R)
        p_t = sb("p", [P, 2, C_IN])
        out_t = sb("out", [P, 2, LT + 1, P])
        squares = sb("squares", [P, LATENTS])
        gains = sb("gains", [P, LATENTS])
        small = sb("latent_norms", [P, 6, N])
        ps = ctx.enter_context(nc.psum_tensor("lat_ps", [P, 3, BANK], F32))
        out_ps = ctx.enter_context(nc.psum_tensor("lat_out_ps", [P, 3, BANK], F32))
        s = ctx.enter_context(stage(nc, "lat", TokenTail.SIGNALS + [
            "w0_in", "w1_in", "gains_in", "w_hi_done", "w_ready", "p_full", "p_copied", "p_squared", "ms_done", "p_rstd",
            "p_normed", "p_turned", "out_copied", "out0_stored", "out1_stored"]))
        w_in_sems = [s.w0_in, s.w1_in]
        out_stored = [s.out0_stored, s.out1_stored]
        tail = TokenTail(nc, ctx, "lat", s, post, pre, 2, N, ident)
        block = ctx.enter_context(nc.Block())

        def stores(t):
            return 16 * sum(3 if v < XT else 2 for v in range(t % 2, t + 1, 2))

        STEPS = N + 4
        shares = {0: range(0, 3), 1: range(3, 6), 2: range(6, KD)}

        @block.sync
        def _(sp):
            sp.dma_start(gains[:, 0:C_Q_RANK], row(q_gain)).then_inc(s.gains_in.sem, 16)
            sp.dma_start(gains[:, C_Q_RANK:], row(kv_gain)).then_inc(s.gains_in.sem, 16)
            tail.load_rows(sp)
            for t in range(2):
                tail.load_x(sp, t, x_old(t))
            for k in range(KD):
                if k >= 2:
                    sp.wait_ge(s.w_ready.sem, k - 1)
                sp.dma_start(p_t[:, k % 2, :], w_in[k * P:(k + 1) * P, :]).then_inc(w_in_sems[k % 2].sem, 16)
            for step in range(STEPS):
                if step < N:
                    tail.store_x(sp, step, x_new(step))
                if step + 2 < N:
                    tail.load_x(sp, step + 2, x_old(step + 2))
                if step >= 4:
                    t = step - 4
                    sp.wait_ge(s.out_copied.sem, 3 * t + 3)
                    cols = slice(t * P, (t + 1) * P)
                    if t < XT:
                        sp.dma_start(cq.rearrange("(k p) n -> p k n", p=P)[:, :, cols], out_t[:, t % 2, 0:QT, :])\
                          .then_inc(out_stored[t % 2].sem, 16)
                    sp.dma_start(ckv.rearrange("(k p) n -> p k n", p=P)[:, :, cols], out_t[:, t % 2, QT:LT, :])\
                      .then_inc(out_stored[t % 2].sem, 16)
                    sp.dma_start(k_pe[:, cols], out_t[0:C_ROPE, t % 2, LT, :]).then_inc(out_stored[t % 2].sem, 16)
            tail.stores_over(sp)
            for t in (N - 2, N - 1):
                sp.wait_ge(out_stored[t % 2].sem, stores(t))

        @block.tensor
        def _(pe):
            for step in range(STEPS):
                if 2 <= step < N + 2:
                    tail.turn_tensor(pe, step - 2)
                if 3 <= step < N + 3:
                    t = step - 3
                    pe.wait_ge(s.h_lo.sem, 2 * t + 2)
                    if t:
                        pe.wait_ge(s.p_copied.sem, t)
                    for b, (a, n) in enumerate(splits):
                        for k in range(KD):
                            if t == 0 and b == 0:
                                pe.wait_ge(s.w_ready.sem, k + 1)
                            mm = exact_product(pe, ps[:, b, 0:n], h_hi[:, t % 2, k, :], h_lo[:, t % 2, k, :],
                                               w_hi[:, k, a:a + n], w_lo[:, k, a:a + n], k == 0, k == KD - 1)
                    mm.then_inc(s.p_full.sem, 1)
                if step >= 4:
                    t = step - 4
                    pe.wait_ge(s.p_normed.sem, 2 * t + 2)
                    for b, (first, last) in enumerate(groups):
                        if t:
                            pe.wait_ge(s.out_copied.sem, 3 * (t - 1) + b + 1)
                        for k in range(first, last):
                            n = P if k < LT else C_ROPE
                            mm = pe.transpose(out_ps[0:n, b, (k - first) * P:(k - first + 1) * P],
                                              p_t[:, t % 2, k * P:k * P + n], ident[:, :])
                        mm.then_inc(s.p_turned.sem, 1)

        @block.scalar
        def _(act):
            act.wait_ge(s.gs_done.sem, 4)
            for step in range(STEPS):
                if step < N:
                    tail.post_scalar(act, step, y_sum[:, step, :])
                if 1 <= step < N + 1:
                    tail.pre_scalar(act, step - 1)
                if 2 <= step < N + 2:
                    t = step - 2
                    if t >= 2:
                        act.wait_ge(s.p_full.sem, t - 1)
                    tail.split_scalar(act, t, h_hi[:, t % 2, :, :])
                for k in shares.get(step, ()):
                    act.wait_ge(w_in_sems[k % 2].sem, 16 * (k // 2 + 1))
                    act.activation(w_hi[:, k, :], p_t[:, k % 2, :], ACT.Copy).then_inc(s.w_hi_done.sem, 1)
                if 3 <= step < N + 3:
                    t = step - 3
                    act.wait_ge(s.p_full.sem, t + 1)
                    if t == 0:
                        act.wait_ge(s.w_ready.sem, KD)
                    if t >= 2:
                        act.wait_ge(s.p_turned.sem, 3 * (t - 1))
                    for b, (a, n) in enumerate(splits):
                        ins = act.activation(p_t[:, t % 2, a:a + n], ps[:, b, 0:n], ACT.Copy)
                    ins.then_inc(s.p_copied.sem, 1)
                    act.wait_ge(s.p_copied.sem, t + 1)
                    if t:
                        act.wait_ge(s.p_squared.sem, 2 * t)
                    for j, (a, b) in enumerate(((0, C_Q_RANK), (C_Q_RANK, LATENTS))):
                        act.activation(squares[:, a:b], p_t[:, t % 2, a:b], ACT.Square,
                                       accum_out=small[:, j, t:t + 1]).then_inc(s.p_squared.sem, 1)
                if step >= 4:
                    t = step - 4
                    if t >= 2:
                        act.wait_ge(out_stored[t % 2].sem, stores(t - 2))
                    for b, (first, last) in enumerate(groups):
                        act.wait_ge(s.p_turned.sem, 3 * t + b + 1)
                        n = C_ROPE if b == 2 else P
                        act.activation(out_t[0:n, t % 2, first:last, :],
                                       out_ps[0:n, b, 0:(last - first) * P].rearrange("p (k n) -> p k n", n=P),
                                       ACT.Copy).then_inc(s.out_copied.sem, 1)

        @block.vector
        def _(dve):
            tail.prepare_rows(dve)
            dve.wait_ge(s.gains_in.sem, 32)
            for step in range(STEPS - 1):
                if step < N:
                    tail.post_vector(dve, step, step, y_sum[:, step, :])
                if 1 <= step < N + 1:
                    tail.pre_vector(dve, step - 1, step - 1)
                if 2 <= step < N + 2:
                    t = step - 2
                    tail.split_vector(dve, t, h_hi[:, t % 2, :, :], h_lo[:, t % 2, :, :])
                for k in shares.get(step, ()):
                    dve.wait_ge(s.w_hi_done.sem, k + 1)
                    dve.tensor_tensor(w_lo[:, k, :], p_t[:, k % 2, :], w_hi[:, k, :].bitcast(F32), ALU.subtract)\
                       .then_inc(s.w_ready.sem, 1)
                if 3 <= step < N + 3:
                    t = step - 3
                    for j, (a, b) in enumerate(((0, C_Q_RANK), (C_Q_RANK, LATENTS))):
                        dve.wait_ge(s.p_rstd.sem, 2 * t + j + 1)
                        part = p_t[:, t % 2, a:b]
                        dve.scalar_tensor_tensor(out=part, in0=part, scalar=small[:, 4 + j, t:t + 1],
                                                 in1=gains[:, a:b], op0=ALU.mult, op1=ALU.mult)\
                           .then_inc(s.p_normed.sem, 1)

        @block.gpsimd
        def _(pool):
            tail.prepare_gpsimd(pool)
            for step in range(STEPS - 1):
                if step < N:
                    tail.post_gpsimd(pool, step)
                if 1 <= step < N + 1:
                    tail.pre_gpsimd(pool, step - 1)
                if step >= 3:
                    t = step - 3
                    for j, rank in enumerate((C_Q_RANK, C_KV_RANK)):
                        ss, ms, rstd = (small[:, 2 * m + j, t:t + 1] for m in range(3))
                        pool.wait_ge(s.p_squared.sem, 2 * t + j + 1)
                        pool.tensor_scalar(ms, ss, 1.0 / rank, RMS_EPS, ALU.mult, ALU.add).then_inc(s.ms_done.sem, 1)
                        pool.wait_ge(s.ms_done.sem, 2 * t + j + 1)
                        pool.tensor_tensor(rstd, ms, tail.minus_half[:, :], ALU.pow).then_inc(s.p_rstd.sem, 1)


def mla(nc, o_rows, inv_sums, cq, ckv, k_pe, w_uq, w_ukv, cos, sin, turn, ident):
    KT = T // P
    CK = C_Q_RANK // P
    KK = C_KV_RANK // P
    HD = C_NOPE + C_ROPE
    NU = 2 * XT
    SCALE = HD ** -0.5
    k_chunks, q_chunks = token_chunks(T), token_chunks(SEQ)
    groups = [list(range(a, min(a + 4, KT))) for a in range(0, KT, 4)]
    G = len(groups)
    fills = Fills([groups] * NU)
    FILLS, TURNS, PAIRS = fills.count, fills.turns, NU // QP

    with ExitStack() as ctx:
        def sb(label, shape, dt=F32):
            return ctx.enter_context(nc.sbuf_tensor(f"mla_{label}", shape, dt))

        cq_hi, cq_lo = (sb(f"cq_{n}", [P, CK, SEQ], F32R) for n in ("hi", "lo"))
        ckv_hi, ckv_lo = (sb(f"ckv_{n}", [P, KK, T], F32R) for n in ("hi", "lo"))
        cos_t = sb("cos", [HD, SEQ])
        sin_t = sb("sin", [HD, SEQ])
        wq = sb("wq", [P, CK, 2 * HD])
        wkv = sb("wkv", [P, KK, 4 * C_V])
        wq_hi, wq_lo = (sb(f"wq_{n}", [P, CK, 2 * HD], F32R) for n in ("hi", "lo"))
        wkv_hi, wkv_lo = (sb(f"wkv_{n}", [P, KK, 2, 2 * C_V], F32R) for n in ("hi", "lo"))
        q_t = sb("q", [HD, SEQ])
        sin_part = sb("sin_part", [HD, SEQ])
        q_hi, q_lo = (sb(f"q_{n}", [HD, 2, SEQ], F32R) for n in ("hi", "lo"))
        k_hi, k_lo = (sb(f"k_{n}", [HD, 2, T], F32R) for n in ("hi", "lo"))
        v_st = sb("v_stacked", [P, 2, KT, 2 * C_V], F32R)
        e = sb("e", [P, 2, T])
        pt_hi, pt_lo = (sb(f"pt_{n}", [P, 2, KT, QP * P], F32R) for n in ("hi", "lo"))
        o_t = sb("o", [C_V, 2, QP * P])
        neg_max = sb("neg_max", [P, 2])
        sums = sb("sums", [P, C_HEADS * XT])
        s_ps = ctx.enter_context(nc.psum_tensor("mla_scores", [P, 2, 3 * BANK], F32))
        t_ps = ctx.enter_context(nc.psum_tensor("mla_turned", [P, 2, BANK], F32))
        s = ctx.enter_context(stage(nc, "mla", [
            "tables_in", "raw0_in", "raw1_in", "raw_hi", "raw_split", "zeroed", "pe_turned", "pe_step", "pe_hi", "pe_lo",
            "asked", "w_in", "w_hi_done", "w_split", "q_full", "q_copied", "q_turned", "q_step", "q_sum", "q_hi",
            "q_lo", "k_full", "k_hi", "k_lo", "v_full", "v_hi", "v_lo", "s_full", "max", "exp", "t_full", "t_hi",
            "t_lo", "o0_stored", "o1_stored", "o_hi", "o_free", "inverted", "inv_turned", "inv_copied", "inv_stored"],
            {"w_split": 1, "q_step": 3, "q_lo": 1, "q_hi": 1, "v_lo": 1, "exp": 2,
             "t_full": 1, "t_lo": 2, "o_free": 2, "k_lo": 1}))
        s.w_in.step = 32
        raw_in, o_stored = [s.raw0_in, s.raw1_in], [s.o0_stored, s.o1_stored]
        block = ctx.enter_context(nc.Block())
        def by_head(w, k, raw):
            if raw:
                return w[:, k, :].rearrange("p (h two d) -> p h two d", two=2, d=C_V)
            return w[:, k, :, :].rearrange("p two (h d) -> p h two d", d=C_V)

        PIECES = CK + KK + 1
        ROUNDS = C_HEADS // 2
        NEXT_WEIGHTS = 3

        def rounds(eng, one_round):
            with eng.Fori(0, ROUNDS - 1) as i:
                one_round(i, True)
            one_round(ROUNDS - 1, False)

        @block.sync
        def _(sp):
            sp.dma_start(cos_t[:, :], cos[0:HD, :]).then_inc(s.tables_in.sem, 16)
            sp.dma_start(sin_t[:, :], sin[0:HD, :]).then_inc(s.tables_in.sem, 16)
            for n in range(PIECES):
                if n >= 2:
                    sp.wait_ge(s.raw_split.sem, n - 1)
                if n < CK:
                    src, dst = cq[n * P:(n + 1) * P, :], e[:, n % 2, 0:SEQ]
                elif n < CK + KK:
                    src, dst = ckv[(n - CK) * P:(n - CK + 1) * P, :], e[:, n % 2, :]
                else:
                    src, dst = k_pe, e[C_NOPE:HD, n % 2, :]
                sp.dma_start(dst, src).then_inc(raw_in[n % 2].sem, 16)
            with sp.Fori(0, C_HEADS // 2) as i:
                sp.wait_ge(s.w_split.sem, s.w_split.nth(i - 1))
                sp.sem_inc(s.asked.sem, 1)
                sp.dma_start(wq[:, :, :], w_uq.rearrange("(k p) n -> p k n", p=P)[:, :, bass.ds(i * (2 * HD), 2 * HD)])\
                  .then_inc(s.w_in.sem, 16)
                sp.dma_start(wkv[:, :, :],
                             w_ukv.rearrange("(k p) n -> p k n", p=P)[:, :, bass.ds(i * (4 * C_V), 4 * C_V)])\
                  .then_inc(s.w_in.sem, 16)
            sp.wait_ge(s.inv_copied.sem, 1)
            sp.dma_start(inv_sums, e[:, 0, 0:P]).then_inc(s.inv_stored.sem, 16)
            sp.wait_ge(s.inv_stored.sem, 16)

        def projections(pe, i):
            def q_product(j):
                for c, (a, n) in enumerate(q_chunks):
                    for k in range(CK):
                        cols = slice(j * HD, (j + 1) * HD)
                        mm = exact_product(pe, s_ps[0:HD, 1, a:a + n], wq_hi[:, k, cols], wq_lo[:, k, cols],
                                           cq_hi[:, k, a:a + n], cq_lo[:, k, a:a + n], k == 0, k == CK - 1)
                mm.then_inc(s.q_full.sem, 1)

            def k_product():
                for c, (a, n) in enumerate(k_chunks):
                    for k in range(KK):
                        mm = exact_product(pe, s_ps[:, 0, a:a + n], wkv_hi[:, k, 0, :], wkv_lo[:, k, 0, :],
                                           ckv_hi[:, k, a:a + n], ckv_lo[:, k, a:a + n], k == 0, k == KK - 1)
                mm.then_inc(s.k_full.sem, 1)

            def q_turn(j):
                pe.wait_ge(s.q_copied.sem, s.q_copied.nth(i * 2 + j))
                for c, (a, n) in enumerate(q_chunks):
                    mm = pe.matmul(s_ps[0:HD, 1, a:a + n], turn[0:HD, 0:HD], q_t[:, a:a + n], start=True, stop=True)
                mm.then_inc(s.q_turned.sem, 1)

            def v_product():
                for kt in range(KT):
                    rows = slice(kt * P, (kt + 1) * P)
                    for k in range(KK):
                        mm = exact_product(pe, s_ps[:, 0, rows], ckv_hi[:, k, rows], ckv_lo[:, k, rows],
                                           wkv_hi[:, k, 1, :], wkv_lo[:, k, 1, :], k == 0, k == KK - 1)
                mm.then_inc(s.v_full.sem, 1)

            pe.wait_ge(s.w_split.sem, s.w_split.nth(i))
            pe.wait_ge(s.exp.sem, s.exp.nth(i * NU - 2))
            v_product()
            pe.wait_ge(s.exp.sem, s.exp.nth(i * NU - 1))
            q_product(0)
            pe.wait_ge(s.v_lo.sem, s.v_lo.nth(i))
            k_product()
            q_turn(0)
            pe.wait_ge(s.q_step.sem, s.q_step.nth(i * 4))
            q_product(1)
            scores(pe, i, 0)
            q_turn(1)
            scores(pe, i, 1)

        def scores(pe, i, u):
            j, qt = u // XT, u % XT
            if u == 0:
                pe.wait_ge(s.k_lo.sem, s.k_lo.nth(i * 2 + 1))
            elif u == 1:
                pe.wait_ge(s.q_step.sem, s.q_step.nth(i * 4 + 2))
            else:
                pe.wait_ge(s.exp.sem, s.exp.nth(i * NU + (u - 2)))
            if qt == 0:
                pe.wait_ge(s.q_lo.sem, s.q_lo.nth(i * 2 + j))
            q = slice(qt * P, (qt + 1) * P)
            for a, n in k_chunks:
                mm = exact_product(pe, s_ps[:, u % 2, a:a + n], q_hi[:, j, q], q_lo[:, j, q],
                                   k_hi[:, j, a:a + n], k_lo[:, j, a:a + n], True, True)
            mm.then_inc(s.s_full.sem, 1)

        def turned(pe, i, u, f):
            n = fills.turned[u][f]
            if f == 0:
                pe.wait_ge(s.exp.sem, s.exp.nth(i * NU + u))
            pe.wait_ge(s.t_lo.sem, s.t_lo.nth(i * FILLS + (n - 2)))
            for g, kt in enumerate(groups[f]):
                mm = pe.transpose(t_ps[:, n % 2, g * P:(g + 1) * P], e[:, u % 2, kt * P:(kt + 1) * P], ident[:, :])
            mm.then_inc(s.t_full.sem, 1)

        def product(pe, i, pair):
            n = fills.product[pair]
            pe.wait_ge(s.t_lo.sem, s.t_lo.nth(i * FILLS + max(n - 2, fills.turned[pair * QP + QP - 1][-1])))
            for kt in range(KT):
                for pt in (pt_hi, pt_lo):
                    mm = pe.matmul(t_ps[:, n % 2, 0:QP * P], v_st[:, pair * QP // XT, kt, :], pt[:, pair % 2, kt, :],
                                   start=kt == 0 and pt is pt_hi, stop=kt == KT - 1 and pt is pt_lo)
            mm.then_inc(s.t_full.sem, 1)

        @block.tensor
        def _(pe):
            start_ahead(pe, s.t_full)
            pe.wait_ge(s.zeroed.sem, 1)
            pe.wait_ge(raw_in[0].sem, 16 * (PIECES // 2 + 1))
            for c, (a, n) in enumerate(q_chunks):
                mm = pe.matmul(s_ps[0:HD, 0, a:a + n], turn[0:HD, 0:HD], e[0:HD, 0, a:a + n], start=True, stop=True)
            mm.then_inc(s.pe_turned.sem, 1)
            pe.wait_ge(s.pe_lo.sem, 2)

            def one_round(i, more):
                projections(pe, i)
                for u in range(NU):
                    turned(pe, i, u, 0)
                    turned(pe, i, u, 1)
                    if u + 2 < NU:
                        scores(pe, i, u + 2)
                    turned(pe, i, u, 2)
                    if u and u % QP == 0:
                        product(pe, i, u // QP - 1)
                product(pe, i, PAIRS - 1)

            rounds(pe, one_round)
            pe.wait_ge(s.inverted.sem, 1)
            pe.wait_ge(s.t_lo.sem, s.t_lo.nth(FILLS * (C_HEADS // 2) - 1))
            pe.transpose(t_ps[:, 0, 0:P], sums[:, :], ident[:, :]).then_inc(s.inv_turned.sem, 1)

        def exponentials(act, i, u):
            act.wait_ge(s.max.sem, s.max.nth(i * NU + u))
            if u >= 2:
                act.wait_ge(s.t_full.sem, s.t_full.nth(i * FILLS + fills.turned[u - 2][-1]))
            act.activation(e[:, u % 2, :], s_ps[:, u % 2, 0:T], ACT.Exp, bias=neg_max[:, u % 2:u % 2 + 1],
                           accum_out=sums[:, bass.ds(i * NU + u, 1)]).then_inc(s.exp.sem, 1)

        def turn_copy(act, i, u, f):
            n, group, pair = fills.turned[u][f], groups[f], u // QP
            act.wait_ge(s.t_full.sem, s.t_full.nth(i * FILLS + n))
            if f == 0 and u % QP == 0 and pair >= 2:
                act.wait_ge(s.t_full.sem, s.t_full.nth(i * FILLS + fills.product[pair - 2]))
            act.activation(pt_hi[:, pair % 2, group[0]:group[-1] + 1, u % QP * P:(u % QP + 1) * P],
                           t_ps[:, n % 2, 0:len(group) * P].rearrange("p (k n) -> p k n", n=P), ACT.Copy)\
               .then_inc(s.t_hi.sem, 1)

        def output_hi(act, i, pair):
            n = fills.product[pair]
            act.wait_ge(s.t_full.sem, s.t_full.nth(i * FILLS + n))
            act.wait_ge(s.o_free.sem, s.o_free.nth(i * PAIRS + (pair - 2)))
            act.activation(o_t[:, pair % 2, :], t_ps[0:C_V, n % 2, 0:QP * P], ACT.Copy).then_inc(s.o_hi.sem, 1)

        @block.scalar
        def _(act):
            start_ahead(act, s.exp, s.q_hi)
            for n in range(CK + KK):
                act.wait_ge(raw_in[n % 2].sem, 16 * (n // 2 + 1))
                dst, src = (cq_hi[:, n, :], e[:, n % 2, 0:SEQ]) if n < CK else (ckv_hi[:, n - CK, :], e[:, n % 2, :])
                act.activation(dst, src, ACT.Copy).then_inc(s.raw_hi.sem, 1)
            act.wait_ge(s.pe_step.sem, 3)
            for j in range(2):
                act.activation(k_hi[C_NOPE:HD, j, :], e[C_NOPE:HD, 0, :], ACT.Copy).then_inc(s.pe_hi.sem, 1)
            act.wait_ge(s.pe_lo.sem, 2)

            def q_copy(i, j):
                act.wait_ge(s.q_full.sem, s.q_full.nth(i * 2 + j))
                act.wait_ge(s.q_lo.sem, s.q_lo.nth(i * 2 + j - 1))
                act.activation(q_t[:, :], s_ps[0:HD, 1, 0:SEQ], ACT.Copy, scale=SCALE).then_inc(s.q_copied.sem, 1)

            def k_half(i, j):
                act.wait_ge(s.k_full.sem, s.k_full.nth(i))
                act.activation(k_hi[0:C_NOPE, j, :], s_ps[j * C_NOPE:(j + 1) * C_NOPE, 0, 0:T], ACT.Copy)\
                   .then_inc(s.k_hi.sem, 1)

            def q_half(i, j):
                act.wait_ge(s.q_sum.sem, s.q_sum.nth(i * 2 + j))
                act.activation(q_hi[:, j, :], q_t[:, :], ACT.Copy).then_inc(s.q_hi.sem, 1)

            def w_half(i):
                act.wait_ge(s.w_in.sem, s.w_in.nth(i))
                act.activation(wq_hi[:, :, :], wq[:, :, :], ACT.Copy)
                for k in range(KK):
                    ins = act.activation(*(by_head(w, k, n) for n, w in enumerate((wkv_hi, wkv))), ACT.Copy)
                ins.then_inc(s.w_hi_done.sem, 1)

            def one_round(i, more):
                act.wait_ge(s.t_full.sem, s.t_full.nth(i * FILLS - 1))
                act.wait_ge(s.v_full.sem, s.v_full.nth(i))
                for j in range(2):
                    act.activation(v_st[:, j, :, 0:C_V],
                                   s_ps[:, 0, 0:T].rearrange("p (k h d) -> p k h d", h=2, d=C_V)[:, :, j, :],
                                   ACT.Copy).then_inc(s.v_hi.sem, 1)
                q_copy(i, 0)
                k_half(i, 0)
                q_half(i, 0)
                k_half(i, 1)
                q_copy(i, 1)
                exponentials(act, i, 0)
                q_half(i, 1)
                for u in range(NU):
                    turn_copy(act, i, u, 0)
                    turn_copy(act, i, u, 1)
                    if u + 1 < NU:
                        exponentials(act, i, u + 1)
                    turn_copy(act, i, u, 2)
                    if u and u % QP == 0:
                        output_hi(act, i, u // QP - 1)
                    if u == NEXT_WEIGHTS and more:
                        act.wait_ge(s.q_full.sem, s.q_full.nth(i * 2 + 1))
                        w_half(i + 1)
                output_hi(act, i, PAIRS - 1)

            w_half(0)
            rounds(act, one_round)
            act.wait_ge(s.inv_turned.sem, 1)
            act.activation(e[:, 0, 0:P], t_ps[:, 0, 0:P], ACT.Copy).then_inc(s.inv_copied.sem, 1)

        def maximum(dve, i, u):
            dve.wait_ge(s.s_full.sem, s.s_full.nth(i * NU + u))
            dve.wait_ge(s.exp.sem, s.exp.nth(i * NU + (u - 2)))
            dve.tensor_reduce(neg_max[:, u % 2:u % 2 + 1], s_ps[:, u % 2, 0:T], AX.X, ALU.max,
                              negate=True).then_inc(s.max.sem, 1)

        def turn_halves(dve, i, u):
            slot = u // QP % 2
            cols = slice(u % QP * P, (u % QP + 1) * P)
            for f, group in enumerate(groups):
                n = fills.turned[u][f]
                dve.wait_ge(s.t_hi.sem, s.t_hi.nth(i * TURNS + (u * G + f)))
                dve.tensor_tensor(pt_lo[:, slot, group[0]:group[-1] + 1, cols],
                                  t_ps[:, n % 2, 0:len(group) * P].rearrange("p (k n) -> p k n", n=P),
                                  pt_hi[:, slot, group[0]:group[-1] + 1, cols].bitcast(F32), ALU.subtract)\
                   .then_inc(s.t_lo.sem, 1)

        def output(dve, i, pair):
            n = fills.product[pair]
            dve.wait_ge(s.o_hi.sem, s.o_hi.nth(i * PAIRS + pair))
            part = o_t[:, pair % 2, :]
            dve.tensor_tensor(part, t_ps[C_V:P, n % 2, 0:QP * P], part, ALU.add).then_inc(s.t_lo.sem, 1)

        @block.vector
        def _(dve):
            start_ahead(dve, s.w_split, s.q_step, s.q_lo, s.v_lo, s.t_lo, s.k_lo)
            for n in range(CK + KK):
                dve.wait_ge(s.raw_hi.sem, n + 1)
                if n < CK:
                    dst, src, hi = cq_lo[:, n, :], e[:, n % 2, 0:SEQ], cq_hi[:, n, :]
                else:
                    dst, src, hi = ckv_lo[:, n - CK, :], e[:, n % 2, :], ckv_hi[:, n - CK, :]
                dve.tensor_tensor(dst, src, hi.bitcast(F32), ALU.subtract).then_inc(s.raw_split.sem, 1)
            dve.wait_ge(s.raw_split.sem, CK + KK)
            dve.memset(e[0:C_NOPE, 0, 0:SEQ], 0.0).then_inc(s.zeroed.sem, 1)
            dve.wait_ge(s.tables_in.sem, 32)
            dve.wait_ge(s.pe_turned.sem, 1)
            pe_rows = slice(C_NOPE, HD)
            dve.tensor_tensor(sin_part[pe_rows, :], s_ps[pe_rows, 0, 0:SEQ], sin_t[pe_rows, :], ALU.mult)\
               .then_inc(s.pe_step.sem, 1)
            dve.tensor_tensor(e[pe_rows, 0, 0:SEQ], e[pe_rows, 0, 0:SEQ], cos_t[pe_rows, :], ALU.mult)\
               .then_inc(s.pe_step.sem, 1)
            dve.wait_ge(s.pe_step.sem, 2)
            dve.tensor_tensor(e[pe_rows, 0, 0:SEQ], e[pe_rows, 0, 0:SEQ], sin_part[pe_rows, :], ALU.add)\
               .then_inc(s.pe_step.sem, 1)
            for j in range(2):
                dve.wait_ge(s.pe_hi.sem, j + 1)
                dve.tensor_tensor(k_lo[pe_rows, j, :], e[pe_rows, 0, :], k_hi[pe_rows, j, :].bitcast(F32),
                                  ALU.subtract).then_inc(s.pe_lo.sem, 1)

            def k_half(i, j):
                dve.wait_ge(s.k_hi.sem, s.k_hi.nth(i * 2 + j))
                dve.tensor_tensor(k_lo[0:C_NOPE, j, :], s_ps[j * C_NOPE:(j + 1) * C_NOPE, 0, 0:T],
                                  k_hi[0:C_NOPE, j, :].bitcast(F32), ALU.subtract).then_inc(s.k_lo.sem, 1)

            def q_rotation(i, j):
                dve.wait_ge(s.q_turned.sem, s.q_turned.nth(i * 2 + j))
                dve.tensor_tensor(sin_part[:, :], s_ps[0:HD, 1, 0:SEQ], sin_t[:, :], ALU.mult)\
                   .then_inc(s.q_step.sem, 1)
                dve.tensor_tensor(q_t[:, :], q_t[:, :], cos_t[:, :], ALU.mult).then_inc(s.q_step.sem, 1)
                dve.wait_ge(s.q_step.sem, s.q_step.nth(i * 4 + (2 * j + 1)))
                dve.tensor_tensor(q_t[:, :], q_t[:, :], sin_part[:, :], ALU.add).then_inc(s.q_sum.sem, 1)

            def q_half(i, j):
                dve.wait_ge(s.q_hi.sem, s.q_hi.nth(i * 2 + j))
                dve.tensor_tensor(q_lo[:, j, :], q_t[:, :], q_hi[:, j, :].bitcast(F32), ALU.subtract)\
                   .then_inc(s.q_lo.sem, 1)

            def w_half(i):
                dve.wait_ge(s.w_hi_done.sem, s.w_hi_done.nth(i))
                dve.tensor_tensor(wq_lo[:, :, :], wq[:, :, :], wq_hi[:, :, :].bitcast(F32), ALU.subtract)
                for k in range(KK):
                    ins = dve.tensor_tensor(by_head(wkv_lo, k, 0), by_head(wkv, k, 1),
                                            by_head(wkv_hi, k, 0).bitcast(F32), ALU.subtract)
                ins.then_inc(s.w_split.sem, 1)

            def one_round(i, more):
                dve.wait_ge(s.v_hi.sem, s.v_hi.nth(i * 2 + 1))
                for j in range(2):
                    ins = dve.tensor_tensor(v_st[:, j, :, C_V:2 * C_V],
                                            s_ps[:, 0, 0:T].rearrange("p (k h d) -> p k h d", h=2, d=C_V)[:, :, j, :],
                                            v_st[:, j, :, 0:C_V].bitcast(F32), ALU.subtract)
                ins.then_inc(s.v_lo.sem, 1)
                k_half(i, 0)
                q_rotation(i, 0)
                q_half(i, 0)
                k_half(i, 1)
                maximum(dve, i, 0)
                q_rotation(i, 1)
                maximum(dve, i, 1)
                q_half(i, 1)
                for u in range(NU):
                    turn_halves(dve, i, u)
                    if u + 2 < NU:
                        maximum(dve, i, u + 2)
                    if u and u % QP == 0:
                        output(dve, i, u // QP - 1)
                    if u == NEXT_WEIGHTS and more:
                        w_half(i + 1)
                output(dve, i, PAIRS - 1)

            w_half(0)
            rounds(dve, one_round)
            dve.wait_ge(s.exp.sem, s.exp.nth(C_HEADS * XT - 1))
            dve.reciprocal(sums[:, :], sums[:, :]).then_inc(s.inverted.sem, 1)

        @block.gpsimd
        def _(pool):
            start_ahead(pool, s.o_free)
            with pool.Fori(0, C_HEADS // 2) as i:
                def stored(pair):
                    pool.wait_ge(o_stored[pair % 2].sem, o_stored[pair % 2].nth(i * (PAIRS // 2) + pair // 2))
                    pool.sem_inc(s.o_free.sem, 1)

                for pair in range(PAIRS):
                    j, first = pair // (PAIRS // 2), pair % (PAIRS // 2) * QP * P
                    pool.wait_ge(s.t_lo.sem, s.t_lo.nth(i * FILLS + fills.product[pair]))
                    pool.sem_inc(s.asked.sem, 1)
                    pool.dma_start(o_rows[bass.ds(i * (2 * C_V) + j * C_V, C_V), first:first + QP * P],
                                   o_t[:, pair % 2, :]).then_inc(o_stored[pair % 2].sem, 16)
                    if pair >= 1:
                        stored(pair - 1)
                stored(PAIRS - 1)


def join_heads(nc, y_hi, y_lo, o_rows, inv_sums, weights):
    with ExitStack() as ctx:
        def sb(label, shape, dt=F32):
            return ctx.enter_context(nc.sbuf_tensor(f"heads_{label}", shape, dt))

        a = sb("a", [P, 2, SEQ])
        r = sb("r", [P, 2, SEQ])
        s = ctx.enter_context(stage(nc, "heads", ["p0_in", "p1_in", "scaled", "y_hi", "y_lo"]
                                    + OutWeights.SIGNALS))
        p_in = [s.p0_in, s.p1_in]
        block = ctx.enter_context(nc.Block())
        LOADS = 3

        @block.sync
        def _(sp):
            for k in range(KD):
                if k >= 2:
                    sp.wait_ge(s.y_lo.sem, k - 1)
                sp.dma_start(a[:, k % 2, :], o_rows[k * P:(k + 1) * P, :]).then_inc(p_in[k % 2].sem, 16)
                for j in range(2):
                    h, rows = 2 * k + j, slice(j * C_V, (j + 1) * C_V)
                    sp.dma_start(r[rows, k % 2, :], row(inv_sums[h * XT:(h + 1) * XT, :]
                                                        .rearrange("t q -> (t q)"), C_V)).then_inc(p_in[k % 2].sem, 16)
                weights.load(sp, s, k)

        @block.scalar
        def _(act):
            for k in range(KD):
                act.wait_ge(s.scaled.sem, k + 1)
                act.activation(y_hi[:, k, :], a[:, k % 2, :], ACT.Copy).then_inc(s.y_hi.sem, 1)
                weights.split_scalar(act, s, k)

        @block.vector
        def _(dve):
            for k in range(KD):
                m = k % 2
                dve.wait_ge(p_in[m].sem, 16 * LOADS * (k // 2 + 1))
                dve.tensor_tensor(a[:, m, :], a[:, m, :], r[:, m, :], ALU.mult).then_inc(s.scaled.sem, 1)
                dve.wait_ge(s.y_hi.sem, k + 1)
                dve.tensor_tensor(y_lo[:, k, :], a[:, m, :], y_hi[:, k, :].bitcast(F32), ALU.subtract)\
                   .then_inc(s.y_lo.sem, 1)
                weights.split_vector(dve, s, k)


INPUTS = ["x", "c", "ctx", "c_ctx", "ada_w", "ada_b", "norm_mix_pre", "norm_mix_post", "norm_ffn_pre",
          "norm_ffn_post", "ffn_w_up", "ffn_conv_w", "ffn_conv_b", "ffn_w_down", "ab_w_in", "a_conv_w",
          "a_conv_b", "a_ln_g", "a_ln_b", "b_lambda", "b_subln", "ab_w_out", "c_w_in", "c_q_norm",
          "c_kv_norm", "c_w_uq", "c_w_ukv", "c_w_out"]


def trunk(nc, i, consts, ropes, out):
    def scratch(label, *shape):
        return nc.dram_tensor(f"scratch_{label}", list(shape), F32, kind="Internal").ap()

    mod = scratch("mod", 2, 2 * 6 * D)
    conv_out = scratch("conv", A_WIDTH, T)
    qk = scratch("qk", 4 * B_HEADS * B_DIM, T)
    v_rows = scratch("v", T, A_WIDTH)

    def mods(layer, part, kinds=2):
        first = (layer * 6 + part) * D
        return [mod[r, first:first + D] for r in range(kinds)]

    x = i.x[0]
    ctx_rows = i.ctx[0]
    with ExitStack() as ctx:
        def sb(label, shape, dt=F32):
            return ctx.enter_context(nc.sbuf_tensor(label, shape, dt))

        ident, turn_a, turn_c = (sb(n, [P, P]) for n in ("ident", "turn_a", "turn_c"))
        load_constants(nc, consts, ident, turn_a, turn_c)
        silu = sb("silu", [P, KD, 2])
        first_chunks = 2 * D // BANK
        first_modulation(nc, silu, mod, i.c[0], i.c_ctx, i.ada_w, i.ada_b, first_chunks)
        with ExitStack() as layer0:
            h_hi = layer0.enter_context(nc.sbuf_tensor("h_hi0", [P, KD, T], F32R))
            h_lo = layer0.enter_context(nc.sbuf_tensor("h_lo0", [P, KD, T], F32R))
            first_norm(nc, h_hi, h_lo, x, ctx_rows,
                       (mods(0, MIX_SCALE), mods(0, MIX_SHIFT), i.norm_mix_pre[0]), ident,
                       silu, mod, i.ada_w, i.ada_b, first_chunks)
            project_conv_diff(nc, h_hi, h_lo, conv_out, qk, v_rows, i.ab_w_in[0], i.a_conv_w[0], i.a_conv_b[0],
                              ropes[0], ropes[1], turn_a)
        o_heads = scratch("o_heads", A_WIDTH, T)
        diff_attention(nc, o_heads, qk, v_rows, i.b_lambda[0], ident)

        def old_rows(t):
            return x[t * P:(t + 1) * P, :] if t < XT else ctx_rows[(t - XT) * P:(t - XT + 1) * P, :]

        x1, x2, x3 = (scratch(n, T, D) for n in ("x1", "x2", "x3"))

        def tile_of(rows):
            return lambda t: rows[t * P:(t + 1) * P, :]

        with ExitStack() as layer0:
            y_hi = layer0.enter_context(nc.sbuf_tensor("y_hi0", [P, KD, T], F32R))
            y_lo = layer0.enter_context(nc.sbuf_tensor("y_lo0", [P, KD, T], F32R))
            with ExitStack() as projection:
                weights = OutWeights(nc, projection, "out0", i.ab_w_out[0])
                join_conv_diff(nc, y_hi, y_lo, conv_out, o_heads, i.a_ln_g[0], i.a_ln_b[0], i.b_subln[0], weights)
                project_out(nc, "out0", y_hi, y_lo, T, weights, (mods(0, MIX_GATE), i.norm_mix_post[0]),
                            (mods(0, FFN_SCALE), mods(0, FFN_SHIFT), i.norm_ffn_pre[0]), old_rows, tile_of(x1),
                            ident)
            with nc.sbuf_tensor("y_sum0", [P, TT, D], F32, side="right") as y_sum:
                ffn(nc, "ffn0", T, y_hi, y_lo, y_sum, i.ffn_w_up[0], i.ffn_conv_w[0], i.ffn_conv_b[0],
                    i.ffn_w_down[0])
                layer0.close()
                cq, ckv, k_pe = scratch("cq", C_Q_RANK, SEQ), scratch("ckv", C_KV_RANK, T), scratch("k_pe", C_ROPE, T)
                project_latents(nc, y_sum, (mods(0, FFN_GATE), i.norm_ffn_post[0]),
                                (mods(1, MIX_SCALE), mods(1, MIX_SHIFT), i.norm_mix_pre[1]), tile_of(x1),
                                tile_of(x2), i.c_w_in[0], i.c_q_norm[0], i.c_kv_norm[0], cq, ckv, k_pe, ident)
        o_rows, inv_sums = scratch("o_rows", C_HEADS * C_V, SEQ), scratch("inv_sums", C_HEADS * XT, P)
        mla(nc, o_rows, inv_sums, cq, ckv, k_pe, i.c_w_uq[0], i.c_w_ukv[0], ropes[2], ropes[3], turn_c, ident)
        with ExitStack() as layer1:
            y_hi = layer1.enter_context(nc.sbuf_tensor("y_hi1", [P, KD, SEQ], F32R))
            y_lo = layer1.enter_context(nc.sbuf_tensor("y_lo1", [P, KD, SEQ], F32R))
            with ExitStack() as projection:
                weights = OutWeights(nc, projection, "out1", i.c_w_out[0])
                join_heads(nc, y_hi, y_lo, o_rows, inv_sums, weights)
                project_out(nc, "out1", y_hi, y_lo, SEQ, weights, (mods(1, MIX_GATE, 1), i.norm_mix_post[1]),
                            (mods(1, FFN_SCALE, 1), mods(1, FFN_SHIFT, 1), i.norm_ffn_pre[1]), tile_of(x2),
                            tile_of(x3), ident)
            with nc.sbuf_tensor("y_sum1", [P, XT, D], F32, side="right") as y_sum:
                ffn(nc, "ffn1", SEQ, y_hi, y_lo, y_sum, i.ffn_w_up[1], i.ffn_conv_w[1], i.ffn_conv_b[1],
                    i.ffn_w_down[1])
                last_residual(nc, y_sum, (mods(1, FFN_GATE, 1), i.norm_ffn_post[1]), tile_of(x3), out)


def rope_constants():
    squares, tables = [np.eye(P, dtype=np.float32)], []
    token = np.arange(SEQ)
    for dims, still in ((B_DIM, 0), (C_ROPE, C_NOPE)):
        half = dims // 4
        m = np.zeros((P, P), np.float32)
        for d in range(still, P):
            if d % (2 * half) < half:
                m[d + half, d] = -1.0
            else:
                m[d - half, d] = 1.0
        squares.append(m)
        freq = np.float32(ROPE_BASE) ** (-np.arange(half, dtype=np.float32) / np.float32(half))
        d = np.arange(P) % dims
        pos = np.where((d < dims // 2)[:, None], token[None, :] // GRID_W, token[None, :] % GRID_W)
        angle = pos.astype(np.float32) * freq[d % half][:, None]
        angle[:still] = 0
        tables += [np.cos(angle), np.sin(angle)]
    return np.concatenate(squares, axis=1), np.stack(tables).astype(np.float32)


def kernel(**inputs):
    import concourse.bacc as bacc
    from concourse.bass_utils import run_bass_kernel_spmd

    nc = bacc.Bacc("TRN2", target_bir_lowering=False, num_devices=1)
    arrays, aps = {}, {}
    squares, tables = rope_constants()
    for name, a in [*((n, inputs[n]) for n in INPUTS), ("squares", squares), ("tables", tables)]:
        arrays[f"in_{name}"] = a = np.ascontiguousarray(a)
        aps[name] = nc.dram_tensor(f"in_{name}", a.shape, mybir.dt.from_np(a.dtype), kind="ExternalInput").ap()
    out = nc.dram_tensor("out", (1, SEQ, D), F32, kind="ExternalOutput").ap()
    trunk(nc, namedtuple("Inputs", INPUTS)(*(aps[n] for n in INPUTS)), aps["squares"], aps["tables"], out[0])
    r = run_bass_kernel_spmd(nc, [arrays], core_ids=[0])
    return r.results[0]["out"]
```
